# Optimizing a Trainium2 kernel written in Bass

```python
import jax, jax.numpy as jnp
from jax import lax
import numpy as np

D_MODEL = 1024
BATCH = 1
SEQ = 128
DEPTH = 2
DEC_BATCH = 1
DEC_SEQ = 128
PAST_LEN = 128

GRID_W = 64
N_HEADS = 8
KV_HEADS = 2
GROUP = N_HEADS // KV_HEADS
HEAD_DIM = 64
ATTN_WIDTH = N_HEADS * HEAD_DIM
KV_WIDTH = KV_HEADS * HEAD_DIM
Q_BLOCK = 128
ROPE_THETA = 10000.0
GLA_HEADS = 4
GLA_DK = 64
GLA_DV = 128
GLA_KW = GLA_HEADS * GLA_DK
GLA_VW = GLA_HEADS * GLA_DV
GLA_RANK = 16
GLA_GATE_NORM = 16.0
GLA_CHUNK = 16
N_EXPERTS = 16
N_GROUPS = 4
EXPERTS_PER_GROUP = N_EXPERTS // N_GROUPS
TOP_K = 2
D_EXPERT = 512
NORM_EPS = 1e-6
IN_SPLIT_WIDTHS = (ATTN_WIDTH, KV_WIDTH, KV_WIDTH, GLA_KW, GLA_KW, GLA_VW, GLA_VW, GLA_RANK, GLA_RANK, D_MODEL, D_MODEL)
IN_WIDTH = ATTN_WIDTH + 2 * KV_WIDTH + 2 * GLA_KW + 2 * GLA_VW + 2 * GLA_RANK + 2 * D_MODEL

kernel_name = 'hybrid_diffusion_gqa_gla_groupmoe_step'

def rmsnorm(x, g):
    x32 = x.astype(jnp.float32)
    y = x32 * lax.rsqrt(jnp.mean(x32 * x32, axis=-1, keepdims=True) + NORM_EPS)
    return y.astype(x.dtype) * g

def axial_rope_angles(n_tokens):
    n_rows = n_tokens // GRID_W
    rows = jnp.repeat(jnp.arange(n_rows), GRID_W).astype(jnp.float32)
    cols = jnp.tile(jnp.arange(GRID_W), n_rows).astype(jnp.float32)
    half = HEAD_DIM // 2
    inv_freq = ROPE_THETA ** (-jnp.arange(0, half, 2, dtype=jnp.float32) / half)
    return rows[:, None] * inv_freq[None, :], cols[:, None] * inv_freq[None, :]

def _rotate_half(x, ang):
    n = ang.shape[-1]
    x1, x2 = x[..., :n], x[..., n:]
    cos, sin = jnp.cos(ang).astype(x.dtype), jnp.sin(ang).astype(x.dtype)
    return jnp.concatenate([x1 * cos - x2 * sin, x1 * sin + x2 * cos], axis=-1)

def apply_axial_rope(x, ang_r, ang_c):
    shape = (ang_r.shape[0],) + (1,) * (x.ndim - 3) + (ang_r.shape[1],)
    half = HEAD_DIM // 2
    return jnp.concatenate([_rotate_half(x[..., :half], ang_r.reshape(shape)),
                            _rotate_half(x[..., half:], ang_c.reshape(shape))], axis=-1)

def block_attention(q, k, v):
    b, t = q.shape[:2]
    nb = t // Q_BLOCK
    qb = jnp.moveaxis(q.reshape(b, nb, Q_BLOCK, KV_HEADS, GROUP, HEAD_DIM), 1, 0)

    def one_block(qi):
        s = jnp.einsum('bqhgd,bkhd->bhgqk', qi, k, preferred_element_type=jnp.float32)
        p = jax.nn.softmax(s, axis=-1)
        return jnp.einsum('bhgqk,bkhd->bqhgd', p.astype(v.dtype), v)

    o = lax.map(one_block, qb)
    return jnp.moveaxis(o, 0, 1).reshape(b, t, ATTN_WIDTH)

def gla_chunked(q, k, v, log_a, s0):
    b, t = q.shape[:2]
    n = t // GLA_CHUNK

    def chunks(z):
        return z.astype(jnp.float32).reshape(b, n, GLA_CHUNK, GLA_HEADS, z.shape[-1]).transpose(1, 0, 3, 2, 4)

    q, k, v, la = chunks(q), chunks(k), chunks(v), chunks(log_a)
    bcum = jnp.cumsum(la, axis=3)
    causal = jnp.tril(jnp.ones((GLA_CHUNK, GLA_CHUNK), dtype=bool))[:, :, None]
    diff = bcum[..., :, None, :] - bcum[..., None, :, :]
    decay = jnp.where(causal, jnp.exp(jnp.where(causal, diff, 0.0)), 0.0)
    scores = jnp.einsum('nbhtk,nbhsk,nbhtsk->nbhts', q, k, decay)
    o_intra = jnp.einsum('nbhts,nbhsv->nbhtv', scores, v)
    b_last = bcum[..., -1:, :]
    q_in = q * jnp.exp(bcum)
    k_st = k * jnp.exp(b_last - bcum)
    a_tot = jnp.exp(b_last[..., 0, :])

    def step(S, inp):
        qi, ki, vi, ai = inp
        o = jnp.einsum('bhtk,bhkv->bhtv', qi, S)
        S = ai[..., None] * S + jnp.einsum('bhsk,bhsv->bhkv', ki, vi)
        return S, o

    s_fin, o_inter = lax.scan(step, s0.astype(jnp.float32), (q_in, k_st, v, a_tot))
    o = (o_intra + o_inter).transpose(1, 0, 3, 2, 4).reshape(b, t, GLA_HEADS, GLA_DV)
    return o, s_fin

def bidirectional_gla(q, k, v, la_f, la_b, s0_f, s0_b):
    o_f, s_f = gla_chunked(q, k, v, la_f, s0_f)
    flip = lambda z: jnp.flip(z, axis=1)
    o_b, s_b = gla_chunked(flip(q), flip(k), flip(v), flip(la_b), s0_b)
    return o_f + flip(o_b), s_f, s_b

def grouped_moe(h, router_w, router_bias, w_gate, w_up, w_down):
    b, t, d = h.shape
    hf = h.reshape(b * t, d)
    scores = jax.nn.sigmoid(jnp.matmul(hf, router_w, preferred_element_type=jnp.float32))
    biased = scores + router_bias.astype(jnp.float32)
    group_score = lax.top_k(biased.reshape(-1, N_GROUPS, EXPERTS_PER_GROUP), TOP_K)[0].sum(-1)
    best_group = jnp.argmax(group_score, axis=-1)
    in_group = (jnp.arange(N_EXPERTS) // EXPERTS_PER_GROUP)[None, :] == best_group[:, None]
    _, top_idx = lax.top_k(jnp.where(in_group, biased, -jnp.inf), TOP_K)
    top_w = jnp.take_along_axis(scores, top_idx, axis=-1)
    top_w = top_w / jnp.sum(top_w, axis=-1, keepdims=True)
    gates = jnp.sum(jax.nn.one_hot(top_idx, N_EXPERTS, dtype=jnp.float32) * top_w[..., None], axis=1)
    act = jax.nn.silu(jnp.einsum('nd,edf->nef', hf, w_gate)) * jnp.einsum('nd,edf->nef', hf, w_up)
    y = jnp.einsum('nef,efd->nd', act * gates[..., None].astype(act.dtype), w_down)
    return y.reshape(b, t, d)

def _split_proj(proj):
    offsets = np.cumsum(IN_SPLIT_WIDTHS)[:-1].tolist()
    return jnp.split(proj, offsets, axis=-1)

def trunk_layer(x, cond, p, router_w, router_bias, rope=None, ctx_k=None, ctx_v=None, s0_f=None, s0_b=None):
    b, t, _ = x.shape
    mod = (jnp.matmul(jax.nn.silu(cond), p['w_ada']) + p['b_ada'])[:, None, :]
    sh1, sc1, g1, sh2, sc2, g2 = jnp.split(mod, 6, axis=-1)
    h = rmsnorm(x, p['norm1']) * (1 + sc1) + sh1
    q, k, v, gq, gk, gv, gg, lr_f, lr_b, ga, gb = _split_proj(jnp.matmul(h, p['w_in']))
    q = rmsnorm(q.reshape(b, t, KV_HEADS, GROUP, HEAD_DIM), p['q_norm'])
    k = rmsnorm(k.reshape(b, t, KV_HEADS, HEAD_DIM), p['k_norm'])
    v = v.reshape(b, t, KV_HEADS, HEAD_DIM)
    if rope is None:
        k_all, v_all = k, v
        s0_f = jnp.zeros((b, GLA_HEADS, GLA_DK, GLA_DV), jnp.float32)
        s0_b = jnp.zeros((b, GLA_HEADS, GLA_DK, GLA_DV), jnp.float32)
    else:
        ang_r, ang_c = rope
        q = apply_axial_rope(q, ang_r, ang_c)
        k_all = jnp.concatenate([apply_axial_rope(k, ang_r, ang_c), ctx_k.astype(k.dtype)], axis=1)
        v_all = jnp.concatenate([v, ctx_v.astype(v.dtype)], axis=1)
    o_attn = block_attention(q * HEAD_DIM ** -0.5, k_all, v_all)
    gq = gq.reshape(b, t, GLA_HEADS, GLA_DK) * GLA_DK ** -0.5
    gk = gk.reshape(b, t, GLA_HEADS, GLA_DK)
    gv = gv.reshape(b, t, GLA_HEADS, GLA_DV)
    la_f = jax.nn.log_sigmoid((jnp.matmul(lr_f, p['gla_w2'][0]) + p['gla_b'][0]).astype(jnp.float32)) / GLA_GATE_NORM
    la_b = jax.nn.log_sigmoid((jnp.matmul(lr_b, p['gla_w2'][1]) + p['gla_b'][1]).astype(jnp.float32)) / GLA_GATE_NORM
    la_f = la_f.reshape(b, t, GLA_HEADS, GLA_DK)
    la_b = la_b.reshape(b, t, GLA_HEADS, GLA_DK)
    o_gla, s_f, s_b = bidirectional_gla(gq, gk, gv, la_f, la_b, s0_f, s0_b)
    o_gla = rmsnorm(o_gla.astype(x.dtype), p['gla_norm']).reshape(b, t, GLA_VW) * jax.nn.silu(gg)
    merged = jax.nn.sigmoid(ga) * jnp.matmul(o_attn, p['w_pa']) + jax.nn.sigmoid(gb) * jnp.matmul(o_gla, p['w_pb'])
    x = x + g1 * jnp.matmul(merged, p['w_out'])
    h2 = rmsnorm(x, p['norm2']) * (1 + sc2) + sh2
    x = x + g2 * grouped_moe(h2, router_w, router_bias, p['w_gate'], p['w_up'], p['w_down'])
    return x, k, v, s_f, s_b

def setup_inputs(seed: int = 0) -> dict:
    key = jax.random.key(seed)
    ks = jax.random.split(key, 26)
    f32 = jnp.float32
    nrm = lambda k, shape, s=1.0: jax.random.normal(k, shape, f32) * s
    return {
        'x_prompt': nrm(ks[0], (BATCH, SEQ, D_MODEL)),
        'x_sample': nrm(ks[1], (DEC_BATCH, DEC_SEQ, D_MODEL)),
        'cache_k': nrm(ks[2], (DEC_BATCH, DEPTH, PAST_LEN, KV_HEADS, HEAD_DIM)),
        'cache_v': nrm(ks[3], (DEC_BATCH, DEPTH, PAST_LEN, KV_HEADS, HEAD_DIM)),
        'state_gla': nrm(ks[4], (DEC_BATCH, DEPTH, 2, GLA_HEADS, GLA_DK, GLA_DV)),
        'c': nrm(ks[5], (DEC_BATCH, D_MODEL)),
        'c_ctx': nrm(ks[6], (D_MODEL,)),
        'norm1': 1.0 + nrm(ks[7], (DEPTH, D_MODEL), 0.02),
        'norm2': 1.0 + nrm(ks[8], (DEPTH, D_MODEL), 0.02),
        'w_ada': nrm(ks[9], (DEPTH, D_MODEL, 6 * D_MODEL), 0.5 * D_MODEL ** -0.5),
        'b_ada': nrm(ks[10], (DEPTH, 6 * D_MODEL), 0.02),
        'w_in': nrm(ks[11], (DEPTH, D_MODEL, IN_WIDTH), D_MODEL ** -0.5),
        'q_norm': 1.0 + nrm(ks[12], (DEPTH, HEAD_DIM), 0.02),
        'k_norm': 1.0 + nrm(ks[13], (DEPTH, HEAD_DIM), 0.02),
        'gla_w2': nrm(ks[14], (DEPTH, 2, GLA_RANK, GLA_KW), GLA_RANK ** -0.5),
        'gla_b': nrm(ks[15], (DEPTH, 2, GLA_KW), 0.1),
        'gla_norm': 1.0 + nrm(ks[16], (DEPTH, GLA_DV), 0.02),
        'w_pa': nrm(ks[17], (DEPTH, ATTN_WIDTH, D_MODEL), ATTN_WIDTH ** -0.5),
        'w_pb': nrm(ks[18], (DEPTH, GLA_VW, D_MODEL), GLA_VW ** -0.5),
        'w_out': nrm(ks[19], (DEPTH, D_MODEL, D_MODEL), D_MODEL ** -0.5),
        'router_w': nrm(ks[20], (D_MODEL, N_EXPERTS), D_MODEL ** -0.5),
        'router_bias': nrm(ks[21], (N_EXPERTS,), 0.01),
        'w_gate': nrm(ks[22], (DEPTH, N_EXPERTS, D_MODEL, D_EXPERT), D_MODEL ** -0.5),
        'w_up': nrm(ks[23], (DEPTH, N_EXPERTS, D_MODEL, D_EXPERT), D_MODEL ** -0.5),
        'w_down': nrm(ks[24], (DEPTH, N_EXPERTS, D_EXPERT, D_MODEL), D_EXPERT ** -0.5),
    }

def reference(x_prompt, x_sample, cache_k, cache_v, state_gla, c, c_ctx, norm1, norm2, w_ada, b_ada, w_in,
              q_norm, k_norm, gla_w2, gla_b, gla_norm, w_pa, w_pb, w_out, router_w, router_bias,
              w_gate, w_up, w_down):
    def layer_params(l):
        return {'norm1': norm1[l], 'norm2': norm2[l], 'w_ada': w_ada[l], 'b_ada': b_ada[l], 'w_in': w_in[l],
                'q_norm': q_norm[l], 'k_norm': k_norm[l], 'gla_w2': gla_w2[l], 'gla_b': gla_b[l],
                'gla_norm': gla_norm[l], 'w_pa': w_pa[l], 'w_pb': w_pb[l], 'w_out': w_out[l],
                'w_gate': w_gate[l], 'w_up': w_up[l], 'w_down': w_down[l]}

    y_prompt = x_prompt
    ctx_keys, ctx_vals, ctx_states = [], [], []
    for l in range(DEPTH):
        y_prompt, k_l, v_l, s_f, s_b = trunk_layer(y_prompt, c_ctx[None, :], layer_params(l), router_w, router_bias)
        ctx_keys.append(k_l)
        ctx_vals.append(v_l)
        ctx_states.append(jnp.stack([s_f, s_b], axis=1))
    new_cache_k = jnp.stack(ctx_keys, axis=1)
    new_cache_v = jnp.stack(ctx_vals, axis=1)
    new_state_gla = jnp.stack(ctx_states, axis=1)

    rope = axial_rope_angles(x_sample.shape[1])
    y_sample = x_sample
    for l in range(DEPTH):
        y_sample, _, _, _, _ = trunk_layer(y_sample, c, layer_params(l), router_w, router_bias, rope=rope,
                                           ctx_k=cache_k[:, l], ctx_v=cache_v[:, l],
                                           s0_f=state_gla[:, l, 0], s0_b=state_gla[:, l, 1])
    return (y_prompt, y_sample, new_cache_k, new_cache_v, new_state_gla)


_drawn_inputs = setup_inputs


def setup_inputs(seed=0):
    import zlib

    import numpy as np

    out = dict(_drawn_inputs(seed))
    spreads = {}
    factors = {'q_norm': 7.451, 'k_norm': 2.742, 'cache_k': 8.0, 'cache_v': 8.0}
    for name, (base, spread) in spreads.items():
        noise = np.random.default_rng([zlib.crc32(name.encode()), seed]).standard_normal(out[name].shape)
        drawn = base * np.exp(spread * noise) if base else spread * noise
        out[name] = __import__('jax').numpy.asarray(drawn.astype(out[name].dtype))
    for name, factor in factors.items():
        out[name] = (out[name] * factor).astype(out[name].dtype)
    return out
```

```python
from contextlib import ExitStack

import numpy as np

import concourse.bass as bass
from concourse import mybir

F32 = mybir.dt.float32
I32 = mybir.dt.int32
ALU = mybir.AluOpType
ACT = mybir.ActivationFunctionType
AX = mybir.AxisListType.X

P = 128
T = 128
S = 2
NT = S * T
LAYERS = 2
D = 1024
KT = D // P
HD = 64
HEADS = 8
KVH = 2
G = HEADS // KVH
ROPE_THETA = 10000.0
GRID_W = 64
GH = 4
DK = 64
DV = 128
RANK = 16
NE = 16
NG = 4
EPG = NE // NG
FE = 512
FT = FE // P
EPS = 1e-6
NEG = -3.0e38

Q0, K0, V0, GQ0, GK0, GV0, GG0, LR0, GA0, GB0 = 0, 512, 640, 768, 1024, 1280, 1792, 2304, 2336, 3360
IN_W = 4384
RSQ = 5
TMW = LR0
IN_UNITS = [(0, 512), (512, 512), (1024, 512), (1536, 512), (2048, 288)]
GATE_UNITS = [(GA0, 512), (GA0 + 512, 512), (GB0, 512), (GB0 + 512, 512)]

RING = 6
UNIT = 4096
ADA = 12
DENSE = ADA + len(IN_UNITS) + len(GATE_UNITS) + 4
SLOTS = 64
PAIRS = NE // 2
PASS_END = PAIRS + 1

LEVELS = 7
LV_COLS = LEVELS * T
D_W = LV_COLS + 2 * T

CONSTS = [("ident", P), ("ones", P), ("dec_f", D_W), ("dec_b", D_W), ("mask", LV_COLS + T), ("before", P),
          ("slot", SLOTS), ("cos", HD), ("sin", HD), ("order_g", NG), ("order_e", NE), ("sel", S)]
PARAMS = [("cond", KT * S), ("b_ada", LAYERS * 48), ("norm1", LAYERS * KT), ("norm2", LAYERS * KT),
          ("bias_r", NE), ("w_r", KT * NE)]
LPARAMS = [("state", GH * DV), ("ck", P), ("cv", P), ("w2", 2 * GH * DK), ("qn", HD), ("kn", HD), ("gln", DV)]


def offsets(parts):
    at, out = 0, {}
    for name, n in parts:
        out[name] = (at, n)
        at += n
    return out, at


CO, CW = offsets(CONSTS)
PO, PW = offsets(PARAMS)
LO, LW = offsets(LPARAMS)

FILL = []
for _i in range(4):
    FILL += [("ada", 4 + 2 * _i), ("ada", 5 + 2 * _i), ("gate", 2 * _i), ("gate", 2 * _i + 1)]


def dense_order():
    out = [("ada", a) for a in range(4)] + [("in", n) for n in range(len(IN_UNITS))]
    for kind, n in FILL:
        if kind == "ada":
            out.append(("ada", n))
        elif n % 2 == 0:
            out.append(("gates", n // 2))
    return out + [("pa", 0), ("pb", 0), ("out", 0), ("out", 1)]


ORDER = dense_order()
assert len(ORDER) == DENSE
PLACE = {key: n for n, key in enumerate(ORDER)}


def build(nc, xT, consts, params, lparams, w_ada, w_in, w_pa, w_pb, w_out, w_gate, w_up, w_down,
          yT, new_k, new_v, new_state):
    ctx = ExitStack()
    with ctx:
        def sb(name, shape, dt=F32):
            return ctx.enter_context(nc.sbuf_tensor(name, shape, dt))

        def sem(name):
            return ctx.enter_context(nc.semaphore(name))

        ring = sb("ring", [P, RING, UNIT])
        cst = sb("cst", [P, CW])
        par = sb("par", [P, PW])
        lpar = sb("lpar", [P, LW])
        x = sb("x", [P, KT, NT])
        h = sb("h", [P, KT, NT])
        sga = sb("sga", [P, KT, NT])
        sgb = sb("sgb", [P, KT, NT])
        tm = sb("tm", [P, S, TMW])
        la = sb("la", [P, S, 2 * GH * DK])
        lrt = sb("lrt", [P, NT])
        ereg = sb("ereg", [P, 2, 1024])
        qe = sb("qe", [P, LEVELS, T])
        ke = sb("ke", [P, LEVELS, T])
        qk2 = sb("qk2", [P, 2, 2, T])
        st = sb("st", [P, T])
        qin = sb("qin", [P, T])
        kst = sb("kst", [P, T])
        sfin = sb("sfin", [P, GH, DV])
        ot = sb("ot", [P, 4, NT])
        ogt = sb("ogt", [P, 4, NT])
        adarow = sb("adarow", [P, 512])
        mod = sb("mod", [P, LAYERS, 48, S])
        modA = sb("modA", [P, LAYERS, 2, KT, S])
        cs = sb("cs", [P, KT, 32])
        rs = sb("rs", [P, NT])
        sm = sb("sm", [P, 128])
        npass = sb("npass", [1, LAYERS], I32)
        ps = ctx.enter_context(nc.psum_tensor("ps", [P, 8, 512], F32))

        def C(name):
            at, n = CO[name]
            return cst[:, at:at + n]

        def PR(name):
            at, n = PO[name]
            return par[:, at:at + n]

        def LP(name):
            at, n = LO[name]
            return lpar[:, at:at + n]

        ident, ones = C("ident"), C("ones")
        BIG_RMS = (rs[:, :], qk2[:, 0, :, :].rearrange("p a t -> p (a t)"), qk2[:, 1, :, :].rearrange("p a t -> p (a t)"))
        QK_RMS = (sm[:, 32:52], sm[:, 64:84], sm[:, 84:104])
        GLA_RMS = (sm[:, 52:56], sm[:, 104:108], sm[:, 108:112])
        qt = ogt[:, 0:2, :].rearrange("p a (b t) -> p (a b) t", b=2)
        kt_all = ogt[:, 2, :]
        prob = ereg[:, 0, :]
        probt = ereg[:, 1, :]
        tmf = tm[:, :, :].rearrange("p s n -> p (s n)")
        hg = tmf[:, 0:1024].rearrange("p (k n) -> p k n", k=KT)
        yy = tmf[:, 1024:2048]
        eg = tmf[:, 2048:2560].rearrange("p (a n) -> p a n", a=2)
        aa = tmf[:, 2560:3072].rearrange("p (a n) -> p a n", a=2)
        at_ = tmf[:, 3072:3584].rearrange("p (a n) -> p a n", a=FT)
        gwt = tmf[:, 3584:3840]
        gg = tmf[:, 3840:4096].rearrange("p (s n) -> p s n", s=S)
        gw = tmf[:, 4096:4352].rearrange("p (s n) -> p s n", s=S)
        h2tok = sgb[:, :, :].rearrange("p (s a) n -> p s (a n)", s=S)
        rt = rs[:, 0:6 * S * NE].rearrange("p (a s e) -> p a s e", a=6, s=S)
        posm = st[:, 0:S * (NE + 2)].rearrange("p (s e) -> p s e", s=S)
        gates = st[:, 64:64 + S * (NE + 2)].rearrange("p (s e) -> p s e", s=S)

        in_x, in_c, in_p, in_lp = sem("in_x"), sem("in_c"), sem("in_p"), sem("in_lp")
        dense_full = [sem(f"dense_full{u}") for u in range(RING)]
        m_add, m_shift = [[sem(f"{n}{l}") for l in range(LAYERS)] for n in ("m_add", "m_shift")]
        moe_full = [[sem(f"moe_full{l}_{u}") for u in range(RING)] for l in range(LAYERS)]
        cond_exp, cs_ready, zeroed = sem("cond_exp"), sem("cs_ready"), sem("zeroed")
        ada_rows, ada_copied, ada_cols, ada_mod = sem("ada_rows"), sem("ada_copied"), sem("ada_cols"), sem("ada_mod")
        sq_act, sq_dve, ssum, xr_ready = sem("sq_act"), sem("sq_dve"), sem("ssum"), sem("xr_ready")
        var_ready, rsq_ready = sem("var_ready"), sem("rsq_ready")
        h_dve, h_act = sem("h_dve"), sem("h_act")
        proj, proj_copied, proj_lr, lr_copied = sem("proj"), sem("proj_copied"), sem("proj_lr"), sem("lr_copied")
        la_mm, la_min, la_ln, la_ready = sem("la_mm"), sem("la_min"), sem("la_ln"), sem("la_ready")
        gg_exp, gg_ready = sem("gg_exp"), sem("gg_ready")
        k_normed, qk_ready = sem("k_normed"), sem("qk_ready")
        att_t, att_copied = sem("att_t"), sem("att_copied")
        scored, maxed, exped, normed = sem("scored"), sem("maxed"), sem("exped"), sem("normed")
        prob_t, prob_copied, att_o, att_o_copied = sem("prob_t"), sem("prob_copied"), sem("att_o"), sem("att_o_copied")
        gate_mm, gate_exp = sem("gate_mm"), sem("gate_exp")
        g_t, g_copied, g_dec, g_exp = sem("g_t"), sem("g_copied"), sem("g_dec"), sem("g_exp")
        g_qe, g_ke, g_lev, g_st, g_o, g_o_copied = (sem("g_qe"), sem("g_ke"), sem("g_lev"), sem("g_st"), sem("g_o"),
                                                    sem("g_o_copied"))
        g_kt, g_kt_copied, g_sf_copied = sem("g_kt"), sem("g_kt_copied"), sem("g_sf_copied")
        g_normed, g_nt, g_nt_copied = sem("g_normed"), sem("g_nt"), sem("g_nt_copied")
        pa_mm, pa_used, pb_mm, merged = sem("pa_mm"), sem("pa_used"), sem("pb_mm"), sem("merged")
        out_mm, x_mid, x_done = sem("out_mm"), sem("x_mid"), sem("x_done")
        r_log, r_exp_in, h2_t, h2_copied = sem("r_log"), sem("r_exp_in"), sem("h2_t"), sem("h2_copied")
        sel_ready, pos_mm, routed = sem("sel_ready"), sem("pos_mm"), sem("routed")

        def per_layer(name):
            return [sem(f"{name}{l}") for l in range(LAYERS)]

        m_onehot, m_gather, m_hg = per_layer("m_onehot"), per_layer("m_gather"), per_layer("m_hg")
        m_gwt, m_gwt_copied, m_gu, m_eg = per_layer("m_gwt"), per_layer("m_gwt_copied"), per_layer("m_gu"), per_layer("m_eg")
        m_act, m_at, m_at_copied = per_layer("m_act"), per_layer("m_at"), per_layer("m_at_copied")
        m_down, m_y, m_scat, m_x = per_layer("m_down"), per_layer("m_y"), per_layer("m_scat"), per_layer("m_x")
        kv_out, st_out, y_out = sem("kv_out"), sem("st_out"), sem("y_out")
        dve_step, act_step, pool_step = sem("dve_step"), sem("act_step"), sem("pool_step")

        def unit_src(l, key):
            kind, n = key
            rows = lambda w: w.rearrange("(k p) n -> p k n", p=P)
            if kind == "ada":
                return rows(w_ada[l])[:, :, n * 512:(n + 1) * 512]
            if kind in ("in", "gates"):
                at, w = (IN_UNITS if kind == "in" else GATE_UNITS)[n]
                return rows(w_in[l])[:, :, at:at + w]
            if kind == "out":
                return rows(w_out[l])[:, :, n * 512:(n + 1) * 512]
            return rows({"pa": w_pa, "pb": w_pb}[kind][l])

        def unit(l, key):
            n = l * DENSE + PLACE[key]
            kts = 4 if key[0] in ("pa", "pb") else KT
            w = IN_UNITS[key[1]][1] if key[0] == "in" else UNIT // kts
            return ring[:, n % RING, 0:kts * w].rearrange("p (k n) -> p k n", k=kts), n

        def moe_unit(u):
            if u < 4:
                return ring[:, u, :].rearrange("p (k n) -> p k n", k=KT)
            return ring[:, u, :].rearrange("p (k n) -> p k n", k=FT)

        def used(n):
            l, (kind, i) = n // DENSE, ORDER[n % DENSE]
            return {"ada": (ada_rows, ADA * l + i + 1),
                    "in": (proj, 10 * l + 2 * i + 2) if i < 4 else (proj_lr, l + 1),
                    "gates": (gate_mm, 8 * l + 2 * i + 2),
                    "pa": (pa_mm, 4 * l + 4), "pb": (pb_mm, 4 * l + 4), "out": (out_mm, 4 * l + 2 * i + 2)}[kind]

        block = ctx.enter_context(nc.Block())

        @block.sync
        def _(sp):
            sp.dma_start(par[:, :], params).then_inc(in_p, 16)
            sp.dma_start(cst[:, :], consts).then_inc(in_c, 16)
            sp.dma_start(x[:, :, :], xT).then_inc(in_x, 16)
            passes = None
            for l in range(LAYERS):
                for key in ORDER:
                    dst, n = unit(l, key)
                    if n >= RING:
                        sp.wait_ge(*used(n - RING))
                    if l and n - l * DENSE < RING:
                        sp.wait_ge((m_gu if n % RING < 4 else m_down)[l - 1], passes * (2 * PAIRS) + 1)
                    sp.dma_start(dst, unit_src(l, key)).then_inc(dense_full[n % RING], 16)
                sp.wait_ge(routed, l + 1)
                passes = sp.snap(sp.value_load(npass[0:1, l:l + 1], min_val=1, max_val=4))
                for u in range(RING):
                    sp.wait_ge(*used(max(n for n in range((l + 1) * DENSE) if n % RING == u)))
                with sp.Fori(0, passes) as pss:
                    with sp.Fori(0, PAIRS) as pr:
                        for u in range(RING):
                            sp.wait_ge((m_gu if u < 4 else m_down)[l], (pss * PAIRS + pr) * 2 + 1)
                            w = (w_gate, w_gate, w_up, w_up, w_down, w_down)[u]
                            src = w[l, bass.ds(pr * 2 + u % 2, 1)].rearrange("o (k p) n -> p (o k) n", p=P)
                            sp.dma_start(moe_unit(u), src).then_inc(moe_full[l][u], 16)
            sp.wait_ge(x_done, LAYERS)
            sp.dma_start(yT, x[:, :, :]).then_inc(y_out, 16)
            sp.wait_ge(y_out, 16)

        @block.tensor
        def _(pe):
            def full(l, key):
                w, n = unit(l, key)
                pe.wait_ge(dense_full[n % RING], 16 * (n // RING + 1))
                return w

            def ada_a(l, a):
                w = full(l, ("ada", a))
                if l or a:
                    pe.wait_ge(ada_copied, l * ADA + a)
                for k in range(KT):
                    j = 32 * (k % 4)
                    mm = pe.matmul(ps[j:j + 32, 7, :], cs[:, k, :], w[:, k, :], start=k < 4, stop=k >= 4)
                mm.then_inc(ada_rows, 1)

            def ada_b(l, a):
                pe.wait_ge(ada_copied, l * ADA + a + 1)
                if l or a:
                    pe.wait_ge(ada_mod, l * ADA + a)
                for i in range(4):
                    mm = pe.matmul(ps[:, 6, 2 * i:2 * i + 2], adarow[:, i * P:(i + 1) * P], C("sel"),
                                   start=True, stop=True)
                mm.then_inc(ada_cols, 1)

            def gate_chunk(l, c):
                w = full(l, ("gates", c // 2))
                if l or c:
                    pe.wait_ge(gate_exp, l * 8 + c)
                if c == 0:
                    pe.wait_ge(la_min, 2 * l + 2)
                for i in range(2):
                    m = (c % 2) * 2 + i
                    for k in range(KT):
                        mm = pe.matmul(ps[:, 5, i * NT:(i + 1) * NT], w[:, k, m * P:(m + 1) * P], h[:, k, :],
                                       start=k == 0, stop=k == KT - 1)
                mm.then_inc(gate_mm, 1)

            fills = []
            late = []

            def fill(l):
                while late:
                    ada_b(*late.pop())
                if fills:
                    kind, n = fills.pop(0)
                    if kind == "ada":
                        ada_a(l, n)
                        late.append((l, n))
                    else:
                        gate_chunk(l, n)

            def norm_sum(n):
                pe.wait_ge(sq_act, n + 1)
                pe.wait_ge(sq_dve, n + 1)
                for k in range(KT):
                    mm = pe.matmul(ps[:, 0, 0:NT], ones, sgb[:, k, :], start=k == 0, stop=k == KT - 1)
                mm.then_inc(ssum, 1)

            pe.wait_ge(in_c, 16)
            pe.wait_ge(in_p, 16)
            pe.wait_ge(cs_ready, 1)
            for l in range(LAYERS):
                if l:
                    pe.wait_ge(x_done, l)
                norm_sum(2 * l)
                for a in range(4):
                    ada_a(l, a)
                    ada_b(l, a)
                pe.wait_ge(h_dve, 2 * l + 1)
                pe.wait_ge(h_act, 2 * l + 1)
                for n in range(2 * len(IN_UNITS)):
                    w = full(l, ("in", n // 2))
                    if n >= 4:
                        pe.wait_ge(proj_copied, 10 * l + n - 3)
                    cols = min(512, TMW - IN_UNITS[n // 2][0])
                    for k in range(KT):
                        mm = pe.matmul(ps[:, n % 4, 0:cols], h[:, k, (n % 2) * T:(n % 2) * T + T], w[:, k, 0:cols],
                                       start=k == 0, stop=k == KT - 1)
                    mm.then_inc(proj, 1)
                for k in range(KT):
                    mm = pe.matmul(ps[0:32, 4, 0:NT], w[:, k, 256:288], h[:, k, :], start=k == 0, stop=k == KT - 1)
                mm.then_inc(proj_lr, 1)
                pe.wait_ge(lr_copied, l + 1)
                pe.wait_ge(in_lp, 16 * (l + 1))
                for s in range(S):
                    pe.matmul(ps[:, 4 + s, :], lrt[0:33, s * T:(s + 1) * T], LP("w2")[0:33, :],
                              start=True, stop=True).then_inc(la_mm, 1)
                fills[:] = list(FILL)
                fill(l)
                for s in range(S):
                    if s == 0:
                        pe.wait_ge(qk_ready, l + 1)
                        pe.wait_ge(proj_copied, 10 * (l + 1))
                    else:
                        pe.wait_ge(exped, 4 * l + 2)
                    for g in range(G):
                        mm = pe.transpose(ps[:, 0, g * P:(g + 1) * P], tm[:, s, Q0 + g * P:Q0 + (g + 1) * P], ident)
                    mm = pe.transpose(ps[:, 1, 0:P], tm[:, s, K0:V0], ident)
                    if s:
                        mm = pe.transpose(ps[:, 1, P:2 * P], LP("ck"), ident)
                    mm.then_inc(att_t, 1)
                    fill(l)
                    nb = 1 + s
                    nk = nb * T
                    for v in range(KVH):
                        b = 4 * l + 2 * s + v
                        if v == 0:
                            pe.wait_ge(att_copied, 2 * l + s + 1)
                        else:
                            pe.wait_ge(exped, b)
                        for g in range(G):
                            at = g * nk
                            mm = pe.matmul(ps[:, at // 512, at % 512:at % 512 + nk], qt[v * HD:(v + 1) * HD, g, :],
                                           kt_all[v * HD:(v + 1) * HD, 0:nk], start=True, stop=True)
                        mm.then_inc(scored, 1)
                        fill(l)
                        pe.wait_ge(normed, b + 1)
                        if b:
                            pe.wait_ge(prob_copied, b)
                        for j in range(G * nb):
                            mm = pe.transpose(ps[:, 2 + j // 4, (j % 4) * P:(j % 4 + 1) * P],
                                              prob[:, j * P:(j + 1) * P], ident)
                        mm.then_inc(prob_t, 1)
                        pe.wait_ge(prob_copied, b + 1)
                        if b:
                            pe.wait_ge(att_o_copied, b)
                        for g in range(G):
                            r = HD * (g % 2)
                            for j in range(nb):
                                val = (LP("cv") if j else tm[:, s, V0:GQ0])[:, v * HD:(v + 1) * HD]
                                mm = pe.matmul(ps[r:r + HD, 4, (g // 2) * T:(g // 2 + 1) * T], val,
                                               probt[:, (g * nb + j) * T:(g * nb + j + 1) * T],
                                               start=j == 0, stop=j == nb - 1)
                        mm.then_inc(att_o, 1)
                pe.wait_ge(att_o_copied, 4 * (l + 1))
                pe.wait_ge(la_ready, 2 * (l + 1))

                def gla_in(i):
                    s, hh = i // GH, i % GH
                    n = 8 * l + i
                    if i:
                        pe.wait_ge(g_o_copied, n - 1)
                        if i <= GH + 1:
                            pe.wait_ge(g_kt_copied, 4 * l + i - 1)
                    for j, at in enumerate((GQ0, GK0)):
                        for d in range(2):
                            mm = pe.matmul(ps[d * DK:(d + 1) * DK, 4, j * T:(j + 1) * T],
                                           tm[:, s, at + hh * DK:at + (hh + 1) * DK], ident, start=True, stop=True)
                    mm.then_inc(g_t, 1)
                    if i:
                        pe.wait_ge(g_exp, n)
                    last = ((512, 512, 0),) if s == 0 else ((512, 384, 0), (LV_COLS + T, T, 384))
                    for half, parts in enumerate((((0, 512, 0),), last)):
                        for at, w, to in parts:
                            for d, dec in enumerate((C("dec_f"), C("dec_b"))):
                                mm = pe.matmul(ps[d * DK:(d + 1) * DK, half, to:to + w],
                                               la[:, s, d * GH * DK + hh * DK:d * GH * DK + (hh + 1) * DK],
                                               dec[:, at:at + w], start=True, stop=True)
                    mm.then_inc(g_dec, 1)

                def gla_levels(i):
                    n = 8 * l + i
                    pe.wait_ge(g_qe, n + 1)
                    pe.wait_ge(g_ke, n + 1)
                    if i:
                        pe.wait_ge(g_st, n)
                    b = i % 2
                    for v in range(LEVELS + 1):
                        lhs, rhs = (ke[:, v, :], qe[:, v, :]) if v < LEVELS else (qk2[:, b, 1, :], qk2[:, b, 0, :])
                        mm = pe.matmul(ps[:, 2 + v // 4, (v % 4) * T:(v % 4 + 1) * T], lhs, rhs, start=True, stop=True)
                    mm.then_inc(g_lev, 1)

                def gla_keys(i):
                    pe.wait_ge(g_copied, 8 * l + i + 2)
                    pe.transpose(ps[:, 4, 384:512], kst[:, :], ident).then_inc(g_kt, 1)

                def gla_out(i):
                    s, hh = i // GH, i % GH
                    n = 8 * l + i
                    pe.wait_ge(g_st, n + 1)
                    pe.wait_ge(g_copied, 8 * l + min(i + 2, 8))
                    if i:
                        pe.wait_ge(g_o_copied, n)
                    if s == 0:
                        pe.wait_ge(g_kt_copied, 4 * l + i + 1)
                    val = tm[:, s, GV0 + hh * DV:GV0 + (hh + 1) * DV]
                    mm = pe.matmul(ps[:, 4, 256:384], st[:, :], val, start=True, stop=s == 0)
                    if s:
                        mm = pe.matmul(ps[:, 4, 256:384], qin[:, :], LP("state")[:, hh * DV:(hh + 1) * DV],
                                       start=False, stop=True)
                    else:
                        mm = pe.matmul(ps[:, 4, 384:512], lrt[:, 0:T], val, start=True, stop=True)
                    mm.then_inc(g_o, 1)

                gla_in(0)
                for i in range(8):
                    fill(l)
                    gla_levels(i)
                    if i < 7:
                        gla_in(i + 1)
                    if i < GH:
                        gla_keys(i)
                    fill(l)
                    gla_out(i)
                while fills or late:
                    fill(l)
                w = full(l, ("pa", 0))
                pe.wait_ge(g_exp, 8 * (l + 1))
                for m in range(4):
                    for i in range(2):
                        for k in range(4):
                            mm = pe.matmul(ps[:, m, i * NT:(i + 1) * NT], w[:, k, (2 * m + i) * P:(2 * m + i + 1) * P],
                                           ot[:, k, :], start=k == 0, stop=k == 3)
                    mm.then_inc(pa_mm, 1)
                pe.wait_ge(gate_exp, 8 * (l + 1))
                pe.wait_ge(g_o_copied, 8 * (l + 1))
                for s in range(S):
                    pe.wait_ge(g_normed, 2 * l + s + 1)
                    for k in range(4):
                        mm = pe.transpose(ps[:, 4 + s, k * P:(k + 1) * P], tm[:, s, k * P:(k + 1) * P], ident)
                    mm.then_inc(g_nt, 1)
                w = full(l, ("pb", 0))
                pe.wait_ge(g_nt_copied, 2 * (l + 1))
                for m in range(4):
                    pe.wait_ge(pa_used, 4 * l + m + 1)
                    for i in range(2):
                        for k in range(4):
                            mm = pe.matmul(ps[:, m, i * NT:(i + 1) * NT], w[:, k, (2 * m + i) * P:(2 * m + i + 1) * P],
                                           ogt[:, k, :], start=k == 0, stop=k == 3)
                    mm.then_inc(pb_mm, 1)
                pe.wait_ge(merged, 4 * (l + 1))
                pe.wait_ge(ada_mod, ADA * (l + 1))
                for m in range(4):
                    w = full(l, ("out", m // 2))
                    for i in range(2):
                        for k in range(KT):
                            c = (m % 2) * 2 + i
                            mm = pe.matmul(ps[:, 4 + m, i * NT:(i + 1) * NT], w[:, k, c * P:(c + 1) * P], sga[:, k, :],
                                           start=k == 0, stop=k == KT - 1)
                    mm.then_inc(out_mm, 1)
                norm_sum(2 * l + 1)
                pe.wait_ge(h_dve, 2 * l + 2)
                pe.wait_ge(h_act, 2 * l + 2)
                for s in range(S):
                    for k in range(KT):
                        mm = pe.matmul(ps[:, 1, s * NE:(s + 1) * NE], h[:, k, s * T:(s + 1) * T],
                                       PR("w_r")[:, k * NE:(k + 1) * NE], start=k == 0, stop=k == KT - 1)
                mm.then_inc(r_log, 1)
                for b in range(4):
                    for j in range(4):
                        s, k = (4 * b + j) // KT, (4 * b + j) % KT
                        mm = pe.transpose(ps[:, 2 + b, j * P:(j + 1) * P], h[:, k, s * T:(s + 1) * T], ident)
                    mm.then_inc(h2_t, 1)
                pe.wait_ge(sel_ready, l + 1)
                sel = rt[:, 0, :, :]
                for s in range(S):
                    if s:
                        pe.matmul(ps[:, 1, 64 + NE:64 + 2 * NE], ones, sel[:, 0, :], start=True, stop=False)
                    pe.matmul(ps[:, 1, 64 + s * NE:64 + (s + 1) * NE], C("before"), sel[:, s, :], start=s == 0, stop=True)
                for s in range(S):
                    mm = pe.matmul(ps[:, 1, 128:128 + NE], ones, sel[:, s, :], start=s == 0, stop=s == 1)
                mm.then_inc(pos_mm, 1)
                pe.wait_ge(h2_copied, 4 * (l + 1))
                pe.wait_ge(routed, l + 1)
                passes = pe.snap(pe.value_load(npass[0:1, l:l + 1], min_val=1, max_val=4))
                for s_ in (m_gather, m_gwt, m_gu, m_at, m_down, m_scat):
                    pe.sem_inc(s_[l], 1)
                with pe.Fori(0, passes) as pss:
                    with pe.Fori(0, PAIRS) as pr:
                        q = pss * PAIRS + pr
                        pe.wait_ge(m_onehot[l], pss * PASS_END + pr + 2)
                        pe.wait_ge(m_x[l], q * 4 + 1)
                        for b in range(2):
                            for j in range(4):
                                for s in range(S):
                                    k = 4 * b + j
                                    mm = pe.matmul(ps[:, 4 + b, j * P:(j + 1) * P], h2tok[:, s, k * P:(k + 1) * P],
                                                   gg[:, s, :], start=s == 0, stop=s == 1)
                            mm.then_inc(m_gather[l], 1)
                        pe.wait_ge(m_gwt_copied[l], q + 1)
                        for s in range(S):
                            mm = pe.transpose(ps[:, 7, s * P:(s + 1) * P], gw[:, s, :], ident)
                        mm.then_inc(m_gwt[l], 1)
                        pe.wait_ge(m_act[l], q * 2 + 1)
                        for half in range(2):
                            for j in range(2):
                                for e in range(2):
                                    if half == 0:
                                        pe.wait_ge(moe_full[l][2 * j + e], q * 16 + 16)
                                for k in range(KT):
                                    if half == 0 and j == 0 and k in (0, 4):
                                        pe.wait_ge(m_hg[l], q * 2 + 2 + k // 4)
                                    for e in range(2):
                                        r = e * SLOTS
                                        mm = pe.matmul(ps[r:r + SLOTS, half, j * 256:(j + 1) * 256], hg[:, k, r:r + SLOTS],
                                                       moe_unit(2 * j + e)[:, k, half * 256:(half + 1) * 256],
                                                       start=k == 0, stop=k == KT - 1)
                            mm.then_inc(m_gu[l], 1)
                        pe.wait_ge(m_y[l], q * 2 + 1)
                        for e in range(2):
                            pe.wait_ge(moe_full[l][4 + e], q * 16 + 16)

                        def down(k, n):
                            for e in range(2):
                                r = e * SLOTS
                                mm = pe.matmul(ps[r:r + SLOTS, 2 + n, :], at_[:, k, r:r + SLOTS],
                                               moe_unit(4 + e)[:, k, n * 512:(n + 1) * 512],
                                               start=k == 0, stop=k == FT - 1)
                            return mm

                        for half in range(2):
                            pe.wait_ge(m_act[l], q * 2 + 2 + half)
                            pe.wait_ge(m_at_copied[l], q * 2 + 1 + half)
                            for j in range(2):
                                mm = pe.transpose(ps[:, 6, (2 * half + j) * P:(2 * half + j + 1) * P],
                                                  aa[:, half, j * P:(j + 1) * P], ident)
                            mm.then_inc(m_at[l], 1)
                            pe.wait_ge(m_at_copied[l], q * 2 + 2 + half)
                            if half == 0:
                                for k in range(2):
                                    for n in range(2):
                                        down(k, n)
                            else:
                                for n in range(2):
                                    down(2, n)
                                    down(3, n).then_inc(m_down[l], 1)
                        pe.wait_ge(m_gwt_copied[l], q + 2)
                        for f in range(4):
                            if f % 2 == 0:
                                pe.wait_ge(m_y[l], q * 2 + 2 + f // 2)
                            if f >= 2:
                                pe.wait_ge(m_x[l], q * 4 + f)
                            for j in range(2):
                                k = 2 * f + j
                                mm = pe.matmul(ps[:, 4 + f % 2, j * NT:(j + 1) * NT], yy[:, k * P:(k + 1) * P], gwt,
                                               start=True, stop=True)
                            mm.then_inc(m_scat[l], 1)

        @block.scalar
        def _(act):
            steps = [0]

            def link(ins):
                steps[0] += 1
                ins.then_inc(act_step, 1)
                act.wait_ge(act_step, steps[0])

            def copy(out, in_, scale=1.0):
                return act.activation(out, in_, ACT.Copy, scale=scale)

            def inv_root(work, step):
                act.wait_ge(var_ready, step)
                link(act.activation(work[1], work[0], ACT.Ln))
                act.activation(work[1], work[1], ACT.Exp, scale=-0.5).then_inc(rsq_ready, 1)

            def squares(n):
                act.activation(sgb[:, 0:4, :], x[:, 0:4, :], ACT.Square).then_inc(sq_act, 1)

            def modulate(l, n):
                inv_root(BIG_RMS, RSQ * l + (1 if n == 0 else 5))
                act.wait_ge(xr_ready, 2 * l + n + 1)
                for k in range(4, KT):
                    for s in range(S):
                        c = slice(s * T, (s + 1) * T)
                        ins = act.activation(h[:, k, c], h[:, k, c], ACT.Identity, bias=mod[:, l, 24 * n + k, s:s + 1],
                                             scale=modA[:, l, n, k, s:s + 1])
                ins.then_inc(h_act, 1)

            def ada_copy(l, a):
                act.wait_ge(ada_rows, l * ADA + a + 1)
                if l or a:
                    act.wait_ge(ada_cols, l * ADA + a)
                copy(adarow[:, :], ps[:, 7, :]).then_inc(ada_copied, 1)

            def gate_exps(l, c):
                act.wait_ge(gate_mm, 8 * l + c + 1)
                if c == 0:
                    act.wait_ge(la_ready, 2 * l + 2)
                if c == 4:
                    act.wait_ge(gg_ready, l + 1)
                to = (sga if c < 4 else sgb)[:, 2 * (c % 4):2 * (c % 4) + 2, :]
                act.activation(to, ps[:, 5, :].rearrange("p (a n) -> p a n", a=2), ACT.Exp,
                               scale=-1.0).then_inc(gate_exp, 1)

            fills = []

            def fill(l):
                if fills:
                    kind, n = fills.pop(0)
                    (ada_copy if kind == "ada" else gate_exps)(l, n)

            act.wait_ge(in_p, 16)
            act.activation(sm[:, 0:16], PR("cond"), ACT.Exp, scale=-1.0).then_inc(cond_exp, 1)
            act.wait_ge(in_x, 16)
            for l in range(LAYERS):
                if l:
                    act.wait_ge(x_done, l)
                squares(2 * l)
                for a in range(4):
                    ada_copy(l, a)
                modulate(l, 0)
                for n in range(2 * len(IN_UNITS)):
                    act.wait_ge(proj, 10 * l + n + 1)
                    at = IN_UNITS[n // 2][0]
                    cols = min(512, TMW - at)
                    copy(tm[:, n % 2, at:at + cols], ps[:, n % 4, 0:cols]).then_inc(proj_copied, 1)
                act.wait_ge(proj_copied, 10 * (l + 1))
                act.activation(sgb[:, 0:4, :].rearrange("p (s a) n -> p s (a n)", s=S), tm[:, :, GG0:LR0], ACT.Exp,
                               scale=-1.0).then_inc(gg_exp, 1)
                for s in range(S):
                    tmp = sga[:, 2 * s:2 * s + 2, :]
                    act.wait_ge(la_min, 2 * l + s + 1)
                    link(act.activation(tmp, tmp, ACT.Exp))
                    act.activation(tmp, tmp, ACT.Ln, bias=1.0).then_inc(la_ln, 1)
                inv_root(QK_RMS, RSQ * l + 2)
                fills[:] = list(FILL)
                fill(l)
                for s in range(S):
                    act.wait_ge(att_t, 2 * l + s + 1)
                    if s:
                        act.wait_ge(scored, 4 * l + 2)
                    copy(ogt[:, 0:2, :], ps[:, 0, :].rearrange("p (a n) -> p a n", a=2))
                    copy(kt_all[:, 0:T * (1 + s)], ps[:, 1, 0:T * (1 + s)]).then_inc(att_copied, 1)
                    fill(l)
                    nb = 1 + s
                    nk = nb * T
                    for v in range(KVH):
                        b = 4 * l + 2 * s + v
                        act.wait_ge(maxed, b + 1)
                        if b:
                            act.wait_ge(prob_t, b)
                        for g in range(G):
                            at = g * nk
                            ins = act.activation(prob[:, at:at + nk], ps[:, at // 512, at % 512:at % 512 + nk], ACT.Exp,
                                                 bias=sm[:, 24 + g:25 + g], scale=HD ** -0.5,
                                                 accum_out=sm[:, 28 + g:29 + g])
                        ins.then_inc(exped, 1)
                        fill(l)
                        act.wait_ge(prob_t, b + 1)
                        if b:
                            act.wait_ge(att_o, b)
                        copy(probt[:, 0:G * nk].rearrange("p (b n) -> p b n", b=nb),
                             ps[:, 2:2 + nb, :]).then_inc(prob_copied, 1)
                        act.wait_ge(att_o, b + 1)
                        copy(ot[:, 2 * v:2 * v + 2, s * T:(s + 1) * T],
                             ps[:, 4, 0:2 * T].rearrange("p (a n) -> p a n", a=2)).then_inc(att_o_copied, 1)

                def gla_in(i):
                    n = 8 * l + i
                    act.wait_ge(g_t, n + 1)
                    if i >= 2:
                        act.wait_ge(g_lev, n - 1)
                    copy(qk2[:, i % 2, 0, :], ps[:, 4, 0:T], scale=DK ** -0.5)
                    copy(qk2[:, i % 2, 1, :], ps[:, 4, T:2 * T]).then_inc(g_copied, 1)
                    act.wait_ge(g_dec, n + 1)
                    if i >= 2:
                        act.wait_ge(g_qe, n - 1)
                        act.wait_ge(g_ke, n - 1)
                    act.activation(ereg[:, i % 2, :].rearrange("p (a n) -> p a n", a=2), ps[:, 0:2, :], ACT.Exp,
                                   scale=1.0 / 16.0).then_inc(g_exp, 1)

                def gla_kt(i):
                    if i < GH:
                        m = 4 * l + i
                        act.wait_ge(g_kt, m + 1)
                        if i:
                            act.wait_ge(g_o, 8 * l + i)
                        copy(lrt[:, 0:T], ps[:, 4, 384:512]).then_inc(g_kt_copied, 1)

                def gla_out(i):
                    s, hh = i // GH, i % GH
                    n = 8 * l + i
                    act.wait_ge(g_o, n + 1)
                    if s == 0:
                        if l and i == 0:
                            act.wait_ge(st_out, 16 * l)
                        copy(sfin[:, hh, :], ps[:, 4, 384:512]).then_inc(g_sf_copied, 1)
                    copy(tm[:, s, hh * DV:(hh + 1) * DV], ps[:, 4, 256:384]).then_inc(g_o_copied, 1)

                act.wait_ge(prob_t, 4 * (l + 1))
                act.wait_ge(att_o, 4 * (l + 1))
                gla_in(0)
                for i in range(8):
                    fill(l)
                    if i < 7:
                        gla_in(i + 1)
                    gla_kt(i)
                    fill(l)
                    gla_out(i)
                    if i == GH:
                        inv_root(GLA_RMS, RSQ * l + 3)
                while fills:
                    fill(l)
                inv_root(GLA_RMS, RSQ * l + 4)
                for s in range(S):
                    act.wait_ge(g_nt, 2 * l + s + 1)
                    copy(ogt[:, :, s * T:(s + 1) * T],
                         ps[:, 4 + s, :].rearrange("p (a n) -> p a n", a=4)).then_inc(g_nt_copied, 1)
                act.wait_ge(x_mid, l + 1)
                squares(2 * l + 1)
                modulate(l, 1)
                act.wait_ge(r_log, l + 1)
                act.activation(rt[:, 1, :, :], ps[:, 1, 0:2 * NE].rearrange("p (s e) -> p s e", s=S), ACT.Exp,
                               scale=-1.0).then_inc(r_exp_in, 1)
                for b in range(4):
                    act.wait_ge(h2_t, 4 * l + b + 1)
                    copy(sgb[:, 2 * b:2 * b + 2, :], ps[:, 2 + b, :].rearrange("p (a n) -> p a n", a=2)).then_inc(h2_copied, 1)
                act.wait_ge(kv_out, 32 * (l + 1))
                act.wait_ge(routed, l + 1)
                passes = act.snap(act.value_load(npass[0:1, l:l + 1], min_val=1, max_val=4))
                for s_ in (m_hg, m_gwt_copied, m_eg, m_at_copied, m_y):
                    act.sem_inc(s_[l], 1)
                with act.Fori(0, passes) as pss:
                    with act.Fori(0, PAIRS) as pr:
                        q = pss * PAIRS + pr
                        for b in range(2):
                            act.wait_ge(m_gather[l], q * 2 + 2 + b)
                            if b == 0:
                                act.wait_ge(m_gu[l], q * 2 + 1)
                            copy(hg[:, 4 * b:4 * b + 4, :],
                                 ps[:, 4 + b, :].rearrange("p (a n) -> p a n", a=4)).then_inc(m_hg[l], 1)
                        act.wait_ge(m_gwt[l], q + 2)
                        act.wait_ge(m_scat[l], q * 4 + 1)
                        copy(gwt, ps[:, 7, 0:NT]).then_inc(m_gwt_copied[l], 1)
                        for half in range(2):
                            act.wait_ge(m_gu[l], q * 2 + 2 + half)
                            act.wait_ge(m_act[l], q * 2 + 1)
                            act.activation(eg[:, half, :], ps[:, half, 0:256], ACT.Exp, scale=-1.0).then_inc(m_eg[l], 1)
                        for half in range(2):
                            act.wait_ge(m_at[l], q * 2 + 2 + half)
                            act.wait_ge(m_down[l], q * 2 + 1)
                            copy(at_[:, 2 * half:2 * half + 2, :],
                                 ps[:, 6, half * 256:(half + 1) * 256].rearrange("p (a n) -> p a n", a=2)
                                 ).then_inc(m_at_copied[l], 1)
                        for n in range(2):
                            act.wait_ge(m_down[l], q * 2 + 2 + n)
                            copy(yy[:, n * 512:(n + 1) * 512], ps[:, 2 + n, :]).then_inc(m_y[l], 1)

        @block.vector
        def _(dve):
            steps = [0]

            def link(ins):
                steps[0] += 1
                ins.then_inc(dve_step, 1)
                dve.wait_ge(dve_step, steps[0])

            def rows(ap, shape):
                return ap.unsqueeze(1).to_broadcast(shape)

            def each(ap, shape):
                return ap.unsqueeze(len(shape) - 1).to_broadcast(shape)

            def inv_rms(work, n, src, step):
                v, y, t = work
                dve.tensor_scalar(v, src, 1.0 / n, EPS, ALU.mult, ALU.add).then_inc(var_ready, 1)
                dve.wait_ge(rsq_ready, step)
                link(dve.tensor_tensor(t, y, y, ALU.mult))
                link(dve.tensor_tensor(t, t, v, ALU.mult))
                link(dve.tensor_scalar(t, t, -0.5, 1.5, ALU.mult, ALU.add))
                link(dve.tensor_tensor(v, y, t, ALU.mult))

            def one_over_one_plus(ap):
                link(dve.tensor_scalar(ap, ap, 1.0, None, ALU.add))
                link(dve.reciprocal(ap, ap))

            def squares():
                dve.tensor_tensor(sgb[:, 4:KT, :], x[:, 4:KT, :], x[:, 4:KT, :], ALU.mult).then_inc(sq_dve, 1)

            def gains(l, n):
                norm = PR("norm1" if n == 0 else "norm2")[:, l * KT:(l + 1) * KT]
                c = mod[:, l, 24 * n + 8:24 * n + 16, :]
                link(dve.tensor_scalar(modA[:, l, n, :, :], c, 1.0, None, ALU.add))
                link(dve.tensor_tensor(modA[:, l, n, :, :], modA[:, l, n, :, :], each(norm, [P, KT, S]), ALU.mult))

            def norm_mod(l, n):
                dve.wait_ge(ssum, 2 * l + n + 1)
                inv_rms(BIG_RMS, D, ps[:, 0, 0:NT], RSQ * l + (1 if n == 0 else 5))
                gains(l, n)
                dve.tensor_tensor(h[:, :, :], x[:, :, :], rows(rs[:, :], [P, KT, NT]), ALU.mult).then_inc(xr_ready, 1)
                dve.wait_ge(xr_ready, 2 * l + n + 1)
                for k in range(4):
                    for s in range(S):
                        c = slice(s * T, (s + 1) * T)
                        ins = dve.tensor_scalar(h[:, k, c], h[:, k, c], modA[:, l, n, k, s:s + 1],
                                                mod[:, l, 24 * n + k, s:s + 1], ALU.mult, ALU.add)
                ins.then_inc(h_dve, 1)

            def ada_bias(l, a):
                dve.wait_ge(ada_cols, l * ADA + a + 1)
                b = PR("b_ada")[:, l * 48 + 4 * a:l * 48 + 4 * a + 4]
                dve.tensor_tensor(mod[:, l, 4 * a:4 * a + 4, :], ps[:, 6, 0:8].rearrange("p (a s) -> p a s", s=S),
                                  each(b, [P, 4, S]), ALU.add).then_inc(ada_mod, 1)

            def gate_sig(l, c):
                dve.wait_ge(gate_exp, 8 * l + c + 1)
                one_over_one_plus((sga if c < 4 else sgb)[:, 2 * (c % 4):2 * (c % 4) + 2, :])

            fills, late = [], []

            def fill(l):
                while late:
                    ada_bias(*late.pop())
                if fills:
                    kind, n = fills.pop(0)
                    if kind == "ada":
                        late.append((l, n))
                    else:
                        gate_sig(l, n)

            link(dve.memset(cs[:, :, :], 0.0))
            dve.wait_ge(in_p, 16)
            dve.wait_ge(cond_exp, 1)
            one_over_one_plus(sm[:, 0:16])
            dve.tensor_tensor(cs[:, :, 0:S], PR("cond").rearrange("p (k s) -> p k s", s=S),
                              sm[:, 0:16].rearrange("p (k s) -> p k s", s=S), ALU.mult).then_inc(cs_ready, 1)
            dve.wait_ge(in_x, 16)
            dve.wait_ge(in_c, 16)
            for l in range(LAYERS):
                squares()
                for a in range(4):
                    ada_bias(l, a)
                dve.wait_ge(ada_mod, l * ADA + 4)
                norm_mod(l, 0)
                dve.wait_ge(proj_lr, l + 1)
                link(dve.memset(lrt[32:33, :], 1.0))
                dve.tensor_copy(lrt[0:32, :], ps[0:32, 4, 0:NT]).then_inc(lr_copied, 1)
                for s in range(S):
                    dve.wait_ge(la_mm, 2 * l + s + 1)
                    link(dve.tensor_scalar(la[:, s, :], ps[:, 4 + s, :], 0.0, None, ALU.min))
                    dve.scalar_tensor_tensor(sga[:, 2 * s:2 * s + 2, :].rearrange("p a n -> p (a n)"), la[:, s, :], 2.0,
                                             ps[:, 4 + s, :], ALU.mult, ALU.subtract).then_inc(la_min, 1)
                dve.wait_ge(proj_copied, 10 * (l + 1))
                dve.wait_ge(in_lp, 16 * (l + 1))
                qk = tm[:, :, 0:V0]
                tmp = ereg[:, :, :].rearrange("p a n -> p (a n)")[:, 0:S * V0].rearrange("p (s n) -> p s n", s=S)
                link(dve.tensor_tensor(tmp, qk, qk, ALU.mult))
                rq = sm[:, 32:52].rearrange("p (s n) -> p s n", s=S)
                link(dve.tensor_reduce(rq, tmp.rearrange("p s (h d) -> p s h d", d=HD), AX, ALU.add))
                inv_rms(QK_RMS, HD, sm[:, 32:52], RSQ * l + 2)
                for s in range(S):
                    v = tm[:, s, 0:V0].rearrange("p (h d) -> p h d", d=HD)
                    link(dve.tensor_tensor(v, v, each(rq[:, s, :], [P, 10, HD]), ALU.mult))
                    dve.tensor_tensor(v[:, 0:HEADS, :], v[:, 0:HEADS, :], rows(LP("qn"), [P, HEADS, HD]), ALU.mult)
                    dve.tensor_tensor(v[:, HEADS:10, :], v[:, HEADS:10, :], rows(LP("kn"), [P, KVH, HD]),
                                      ALU.mult).then_inc(k_normed, 1)
                    dve.wait_ge(k_normed, 2 * l + s + 1)
                v = tm[:, 1, 0:V0].rearrange("p (h d) -> p h d", d=HD)
                v5 = tm[:, 1, 0:V0].rearrange("p (h r c d) -> p h r c d", r=2, c=2, d=16)
                sn = C("sin").rearrange("p (r c d) -> p r c d", r=2, c=2)
                t1 = ereg[:, 0, 0:V0].rearrange("p (h d) -> p h d", d=HD)
                t2 = ereg[:, 1, 0:V0].rearrange("p (h r c d) -> p h r c d", r=2, c=2, d=16)
                dve.tensor_tensor(t1, v, rows(C("cos"), [P, 10, HD]), ALU.mult)
                for c in range(2):
                    ins = dve.tensor_tensor(t2[:, :, :, c, :], v5[:, :, :, 1 - c, :],
                                            sn[:, :, c, :].unsqueeze(1).to_broadcast([P, 10, 2, 16]), ALU.mult)
                link(ins)
                dve.tensor_tensor(tm[:, 1, 0:V0], ereg[:, 0, 0:V0], ereg[:, 1, 0:V0], ALU.add).then_inc(qk_ready, 1)
                for s in range(S):
                    dve.wait_ge(la_ln, 2 * l + s + 1)
                    dve.tensor_tensor(la[:, s, :].rearrange("p (a n) -> p a n", a=2),
                                      la[:, s, :].rearrange("p (a n) -> p a n", a=2), sga[:, 2 * s:2 * s + 2, :],
                                      ALU.subtract).then_inc(la_ready, 1)
                dve.wait_ge(gg_exp, l + 1)
                ge = sgb[:, 0:4, :].rearrange("p (s a) n -> p s (a n)", s=S)
                one_over_one_plus(ge)
                dve.tensor_tensor(tm[:, :, GG0:LR0], tm[:, :, GG0:LR0], ge, ALU.mult).then_inc(gg_ready, 1)
                fills[:] = list(FILL)
                fill(l)
                for s in range(S):
                    fill(l)
                    nb = 1 + s
                    nk = nb * T
                    for v in range(KVH):
                        b = 4 * l + 2 * s + v
                        dve.wait_ge(scored, b + 1)
                        if nb == 1:
                            sc = ps[:, 0, :].rearrange("p (g n) -> p g n", g=G)
                        else:
                            sc = ps[:, 0:2, :].rearrange("p a (g n) -> p (a g) n", g=2)
                        link(dve.tensor_reduce(sm[:, 20:24], sc, AX, ALU.max))
                        dve.tensor_scalar(sm[:, 24:28], sm[:, 20:24], -HD ** -0.5, None, ALU.mult).then_inc(maxed, 1)
                        fill(l)
                        dve.wait_ge(exped, b + 1)
                        link(dve.reciprocal(sm[:, 28:32], sm[:, 28:32]))
                        pv = prob[:, 0:G * nk].rearrange("p (g n) -> p g n", g=G)
                        dve.tensor_tensor(pv, pv, each(sm[:, 28:32], [P, G, nk]), ALU.mult).then_inc(normed, 1)

                def gla_q(i):
                    n = 8 * l + i
                    dve.wait_ge(g_exp, n + 1)
                    dve.wait_ge(g_copied, n + 1)
                    if n:
                        dve.wait_ge(g_lev, n)
                    if i == 0:
                        dve.wait_ge(zeroed, 2)
                    e, qs = ereg[:, i % 2, :], qk2[:, i % 2, 0, :]
                    for v in range(LEVELS):
                        ins = side(dve, qe, e, qs, v, 0)
                    if i >= GH:
                        if i > GH:
                            dve.wait_ge(g_o, n)
                        ins = dve.tensor_tensor(qin[:, :], qs, e[:, LV_COLS:LV_COLS + T], ALU.mult)
                    ins.then_inc(g_qe, 1)

                def gla_mask(i):
                    n = 8 * l + i
                    dve.wait_ge(g_lev, n + 1)
                    if i:
                        dve.wait_ge(g_o, n)
                    m = C("mask").rearrange("p (a n) -> p a n", a=2)
                    link(dve.tensor_tensor(ps[:, 2:4, :], ps[:, 2:4, :], m, ALU.mult))
                    dve.tensor_reduce(st[:, :], ps[:, 2:4, :].rearrange("p a (v t) -> p t (a v)", v=4), AX,
                                      ALU.add).then_inc(g_st, 1)

                def gla_norm(s):
                    dve.wait_ge(g_o_copied, 8 * l + 4 * s + 4)
                    o, t = tm[:, s, 0:512], tm[:, s, GQ0:GV0]
                    o3 = o.rearrange("p (h d) -> p h d", d=DV)
                    link(dve.tensor_tensor(t, o, o, ALU.mult))
                    link(dve.tensor_reduce(sm[:, 52:56], t.rearrange("p (h d) -> p h d", d=DV), AX, ALU.add))
                    inv_rms(GLA_RMS, DV, sm[:, 52:56], RSQ * l + 3 + s)
                    link(dve.tensor_tensor(o3, o3, each(sm[:, 52:56], [P, GH, DV]), ALU.mult))
                    link(dve.tensor_tensor(o3, o3, rows(LP("gln"), [P, GH, DV]), ALU.mult))
                    dve.tensor_tensor(o, o, tm[:, s, GG0:LR0], ALU.mult).then_inc(g_normed, 1)

                gla_q(0)
                for i in range(8):
                    fill(l)
                    gla_mask(i)
                    if i < 7:
                        gla_q(i + 1)
                    fill(l)
                    if i == GH:
                        gla_norm(0)
                while fills or late:
                    fill(l)
                for m in range(4):
                    dve.wait_ge(pa_mm, 4 * l + m + 1)
                    a = sga[:, 2 * m:2 * m + 2, :]
                    dve.tensor_tensor(a, a, ps[:, m, :].rearrange("p (a n) -> p a n", a=2), ALU.mult).then_inc(pa_used, 1)
                gla_norm(1)
                for m in range(4):
                    dve.wait_ge(pb_mm, 4 * l + m + 1)
                    a, b = sga[:, 2 * m:2 * m + 2, :], sgb[:, 2 * m:2 * m + 2, :]
                    link(dve.tensor_tensor(b, b, ps[:, m, :].rearrange("p (a n) -> p a n", a=2), ALU.mult))
                    dve.tensor_tensor(a, a, b, ALU.add).then_inc(merged, 1)
                dve.wait_ge(ada_mod, ADA * (l + 1))
                for m in range(4):
                    dve.wait_ge(out_mm, 4 * l + m + 1)
                    for i in range(2):
                        for s in range(S):
                            k, c = 2 * m + i, slice(s * T, (s + 1) * T)
                            ins = dve.scalar_tensor_tensor(x[:, k, c], ps[:, 4 + m, i * NT + s * T:i * NT + (s + 1) * T],
                                                           mod[:, l, 16 + k, s:s + 1], x[:, k, c], ALU.mult, ALU.add)
                ins.then_inc(x_mid, 1)
                dve.wait_ge(x_mid, l + 1)
                squares()
                norm_mod(l, 1)
                dve.wait_ge(r_exp_in, l + 1)
                sel, score, biased, t3, t4 = (rt[:, i, :, :] for i in (0, 1, 2, 3, 4))
                one_over_one_plus(score)
                link(dve.tensor_tensor(biased, score, rows(PR("bias_r"), [P, S, NE]), ALU.add))
                bg = rt[:, 2, :, :].rearrange("p s (g e) -> p (s g) e", g=NG)
                pairs = rs[:, 96:144].rearrange("p (g n) -> p g n", n=6)
                dve.tensor_tensor(pairs[:, :, 0:3], bg[:, :, 0:3], bg[:, :, 1:4], ALU.add)
                dve.tensor_tensor(pairs[:, :, 3:5], bg[:, :, 0:2], bg[:, :, 2:4], ALU.add)
                link(dve.tensor_tensor(pairs[:, :, 5:6], bg[:, :, 0:1], bg[:, :, 3:4], ALU.add))
                gs = sm[:, 0:8].rearrange("p (s g) -> p s g", s=S)
                link(dve.tensor_reduce(sm[:, 0:8], pairs, AX, ALU.max))

                def first_max(vals, flags, n, order):
                    link(dve.tensor_reduce(sm[:, 8:10], vals, AX, ALU.max))
                    link(dve.tensor_tensor(flags, vals, each(sm[:, 8:10], [P, S, n]), ALU.is_equal))
                    link(dve.tensor_tensor(flags, flags, rows(order, [P, S, n]), ALU.mult))
                    link(dve.tensor_reduce(sm[:, 8:10], flags, AX, ALU.max))
                    link(dve.tensor_tensor(flags, flags, each(sm[:, 8:10], [P, S, n]), ALU.is_equal))

                gf = sm[:, 10:18].rearrange("p (s g) -> p s g", s=S)
                first_max(gs, gf, NG, C("order_g"))
                link(dve.tensor_tensor(bg, bg, each(sm[:, 10:18], [P, S * NG, EPG]), ALU.mult))
                link(dve.tensor_scalar(sm[:, 10:18], sm[:, 10:18], -1.0, -NEG, ALU.add, ALU.mult))
                link(dve.tensor_tensor(bg, bg, each(sm[:, 10:18], [P, S * NG, EPG]), ALU.add))
                first_max(biased, t3, NE, C("order_e"))
                link(dve.tensor_scalar(t4, t3, NEG, None, ALU.mult))
                link(dve.tensor_tensor(biased, biased, t4, ALU.add))
                first_max(biased, t4, NE, C("order_e"))
                dve.tensor_tensor(sel, t3, t4, ALU.add).then_inc(sel_ready, 1)
                dve.wait_ge(sel_ready, l + 1)
                gt = gates[:, :, 0:NE]
                link(dve.tensor_tensor(gt, score, sel, ALU.mult))
                link(dve.tensor_reduce(sm[:, 8:10], gt, AX, ALU.add))
                link(dve.reciprocal(sm[:, 8:10], sm[:, 8:10]))
                link(dve.memset(gates[:, :, NE:NE + 2], 0.0))
                link(dve.tensor_tensor(gt, gt, each(sm[:, 8:10], [P, S, NE]), ALU.mult))
                dve.wait_ge(pos_mm, l + 1)
                pm = posm[:, :, 0:NE]
                link(dve.memset(posm[:, :, NE:NE + 2], -1.0))
                link(dve.tensor_scalar(pm, ps[:, 1, 64:64 + 2 * NE].rearrange("p (s e) -> p s e", s=S), 1.0, None, ALU.add))
                link(dve.tensor_tensor(pm, pm, sel, ALU.mult))
                link(dve.tensor_scalar(pm, pm, -1.0, None, ALU.add))
                link(dve.tensor_reduce(sm[:, 8:9], ps[:, 1, 128:128 + NE], AX, ALU.max))
                for j in range(3):
                    ins = dve.tensor_scalar(sm[:, 9 + j:10 + j], sm[:, 8:9], float(SLOTS * (j + 1)), None, ALU.is_gt)
                link(ins)
                link(dve.tensor_reduce(sm[:, 12:13], sm[:, 9:12], AX, ALU.add))
                link(dve.tensor_scalar(sm[:, 12:13], sm[:, 12:13], 1.0, None, ALU.add))
                dve.tensor_copy(npass[0:1, l:l + 1], sm[0:1, 12:13]).then_inc(routed, 1)
                dve.wait_ge(routed, l + 1)
                passes = dve.snap(dve.value_load(npass[0:1, l:l + 1], min_val=1, max_val=4))
                for s_ in (m_onehot, m_act, m_x):
                    dve.sem_inc(s_[l], 1)

                def onehots(pr, gathered):
                    dve.wait_ge(m_gather[l], gathered * 2 + 1)
                    dve.wait_ge(m_gwt[l], gathered + 1)
                    for s in range(S):
                        for e in range(2):
                            at = posm[:, s, bass.ds(pr * 2 + e, 1)]
                            c = slice(e * SLOTS, (e + 1) * SLOTS)
                            dve.tensor_scalar(gg[:, s, c], C("slot"), at, None, ALU.is_equal)
                            ins = dve.tensor_scalar(gw[:, s, c], C("slot"), at, gates[:, s, bass.ds(pr * 2 + e, 1)],
                                                    ALU.is_equal, ALU.mult)
                    ins.then_inc(m_onehot[l], 1)

                with dve.Fori(0, passes) as pss:
                    onehots(0, pss * PAIRS)
                    with dve.Fori(0, PAIRS) as pr:
                        q = pss * PAIRS + pr
                        for half in range(2):
                            dve.wait_ge(m_eg[l], q * 2 + 2 + half)
                            dve.wait_ge(m_at[l], q * 2 + 1)
                            g_, u_ = ps[:, half, 0:256], ps[:, half, 256:512]
                            e_ = eg[:, half, :]
                            dve.tensor_scalar(e_, e_, 1.0, None, ALU.add).then_inc(m_add[l], 1)
                            dve.wait_ge(m_add[l], q * 6 + 3 * half + 1)
                            dve.reciprocal(e_, e_).then_inc(m_add[l], 1)
                            dve.wait_ge(m_add[l], q * 6 + 3 * half + 2)
                            dve.tensor_tensor(e_, e_, g_, ALU.mult).then_inc(m_add[l], 1)
                            dve.wait_ge(m_add[l], q * 6 + 3 * half + 3)
                            dve.tensor_tensor(aa[:, half, :], e_, u_, ALU.mult).then_inc(m_act[l], 1)
                        onehots(pr + 1, q + 1)
                        for f in range(4):
                            dve.wait_ge(m_scat[l], q * 4 + f + 2)
                            for j in range(2):
                                for s in range(S):
                                    k, c = 2 * f + j, slice(s * T, (s + 1) * T)
                                    ins = dve.scalar_tensor_tensor(
                                        x[:, k, c], ps[:, 4 + f % 2, j * NT + s * T:j * NT + (s + 1) * T],
                                        mod[:, l, 40 + k, s:s + 1], x[:, k, c], ALU.mult, ALU.add)
                            ins.then_inc(m_x[l], 1)
                    dve.tensor_scalar(posm[:, :, :], posm[:, :, :], -float(SLOTS), None, ALU.add).then_inc(m_shift[l], 1)
                    dve.wait_ge(m_shift[l], pss + 1)
                dve.wait_ge(m_x[l], passes * (4 * PAIRS) + 1)
                dve.memset(sm[:, 0:1], 0.0).then_inc(x_done, 1)

        @block.gpsimd
        def _(pool):
            pool.memset(qe[:, :, :], 0.0).then_inc(zeroed, 1)
            pool.memset(ke[:, :, :], 0.0).then_inc(zeroed, 1)
            pool.wait_ge(zeroed, 2)
            for l in range(LAYERS):
                if l:
                    pool.wait_ge(x_done, l)
                pool.dma_start(lpar[:, :], lparams[l]).then_inc(in_lp, 16)
                pool.wait_ge(k_normed, 2 * l + 1)
                pool.dma_start(new_k[l], tm[:, 0, K0:V0]).then_inc(kv_out, 16)
                pool.dma_start(new_v[l], tm[:, 0, V0:GQ0]).then_inc(kv_out, 16)
                for i in range(8):
                    n = 8 * l + i
                    pool.wait_ge(g_exp, n + 1)
                    pool.wait_ge(g_copied, n + 1)
                    if n:
                        pool.wait_ge(g_ke, n)
                        pool.wait_ge(g_lev, n)
                    e, ks = ereg[:, i % 2, :], qk2[:, i % 2, 1, :]
                    for v in range(LEVELS):
                        ins = side(pool, ke, e, ks, v, 1)
                    if i < GH:
                        ins.then_inc(pool_step, 1)
                        pool.wait_ge(pool_step, 4 * l + i + 1)
                        if i or l:
                            pool.wait_ge(g_kt, 4 * l + i)
                        ins = pool.tensor_tensor(kst[:, :], ks, e[:, LV_COLS:LV_COLS + T], ALU.mult)
                    ins.then_inc(g_ke, 1)
                pool.wait_ge(g_sf_copied, 4 * (l + 1))
                pool.dma_start(new_state[l], sfin[:, :, :]).then_inc(st_out, 16)
            pool.wait_ge(kv_out, 32 * LAYERS)
            pool.wait_ge(st_out, 16 * LAYERS)


def side(eng, out, decay, vals, level, keys):
    half = P >> (level + 1)
    for d in range(2):
        r = slice(d * DK, (d + 1) * DK)
        right = (d + keys + 1) % 2
        def part(ap):
            v = ap.rearrange("p (b c n) -> p b c n", c=2, n=half)
            return v[:, :, right, :]
        ins = eng.tensor_tensor(part(out[r, level, :]), part(vals[r, :]), part(decay[r, level * T:(level + 1) * T]),
                                ALU.mult)
    return ins


def shape_constants():
    c = np.zeros((P, CW), np.float32)

    def put(name, v):
        at, n = CO[name]
        c[:, at:at + n] = v

    u = np.arange(P)[:, None]
    t = np.arange(P)[None, :]
    put("ident", u == t)
    put("ones", 1.0)
    f, b, m = [], [], []
    for v in range(LEVELS):
        half = P >> (v + 1)
        mid = t // (2 * half) * (2 * half) + half
        right = t >= mid
        f.append(np.where(right, (u >= mid) & (u <= t), (u > t) & (u < mid)))
        b.append(np.where(right, (u >= mid) & (u < t), (u >= t) & (u < mid)))
        m.append((u // (2 * half) == t // (2 * half)) & (u // half != t // half))
    put("dec_f", np.concatenate(f + [u > t, u <= t], 1))
    put("dec_b", np.concatenate(b + [u < t, u >= t], 1))
    put("mask", np.concatenate(m + [u == t], 1))
    put("before", u < t)
    put("slot", np.arange(SLOTS)[None])
    inv = (np.float32(ROPE_THETA) ** (-np.arange(0, HD // 2, 2, dtype=np.float32) / np.float32(HD // 2))).astype(np.float32)
    row = (np.arange(T) // int(GRID_W)).astype(np.float32)[:, None] * inv
    col = (np.arange(T) % int(GRID_W)).astype(np.float32)[:, None] * inv
    put("cos", np.concatenate([np.cos(row), np.cos(row), np.cos(col), np.cos(col)], 1))
    put("sin", np.concatenate([-np.sin(row), np.sin(row), -np.sin(col), np.sin(col)], 1))
    put("order_g", np.arange(NG, 0, -1)[None])
    put("order_e", np.arange(NE, 0, -1)[None])
    put("sel", (u % 32) == np.arange(S)[None])
    return c


def kernel(**inputs):
    import concourse.bacc as bacc
    from concourse.bass_utils import run_bass_kernel_spmd

    a = {k: np.asarray(v) for k, v in inputs.items()}
    L = LAYERS

    def chan(v):
        v = v.reshape(v.shape[:-1] + (v.shape[-1] // P, P))
        return np.moveaxis(v, -1, 0)

    xs = np.concatenate([a["x_prompt"][0], a["x_sample"][0]], 0)
    xT = np.ascontiguousarray(xs.T.reshape(KT, P, NT).transpose(1, 0, 2))
    cond = np.stack([a["c_ctx"], a["c"][0]], 0)
    params = np.concatenate([
        chan(cond).transpose(0, 2, 1).reshape(P, -1),
        chan(a["b_ada"]).reshape(P, -1),
        chan(a["norm1"]).reshape(P, -1),
        chan(a["norm2"]).reshape(P, -1),
        np.broadcast_to(a["router_bias"], (P, NE)),
        a["router_w"].reshape(KT, P, NE).transpose(1, 0, 2).reshape(P, -1)], 1)
    lparams = np.zeros((L, P, LW), np.float32)
    for l in range(L):
        def put(name, v, rows=P):
            at, n = LO[name]
            lparams[l, 0:rows, at:at + n] = v
        put("state", a["state_gla"][0, l].transpose(0, 2, 1, 3).reshape(P, GH * DV))
        put("ck", a["cache_k"][0, l].reshape(P, P))
        put("cv", a["cache_v"][0, l].reshape(P, P))
        at, n = LO["w2"]
        lparams[l, 0:RANK, at:at + n // 2] = a["gla_w2"][l, 0]
        lparams[l, RANK:2 * RANK, at + n // 2:at + n] = a["gla_w2"][l, 1]
        lparams[l, 2 * RANK, at:at + n] = a["gla_b"][l].reshape(-1)
        put("qn", a["q_norm"][l][None])
        put("kn", a["k_norm"][l][None])
        put("gln", a["gla_norm"][l][None])
    arrays = {"xT": xT, "consts": shape_constants(), "params": np.ascontiguousarray(params), "lparams": lparams}
    for name in ("w_ada", "w_in", "w_pa", "w_pb", "w_out", "w_gate", "w_up", "w_down"):
        arrays[name] = np.ascontiguousarray(a[name])
    q = a["w_in"][:, :, Q0:K0].reshape(L, D, KVH, G, HD).transpose(0, 1, 3, 2, 4).reshape(L, D, K0)
    arrays["w_in"] = np.concatenate([q, a["w_in"][:, :, K0:]], 2)
    outs = [("yT", (P, KT, NT)), ("new_k", (L, T, P)), ("new_v", (L, T, P)), ("new_state", (L, P, GH, DV))]

    nc = bacc.Bacc("TRN2", target_bir_lowering=False, num_devices=1)
    args = [nc.dram_tensor(n, v.shape, F32, kind="ExternalInput").ap() for n, v in arrays.items()]
    args += [nc.dram_tensor(n, s, F32, kind="ExternalOutput").ap() for n, s in outs]
    build(nc, *args)
    r = run_bass_kernel_spmd(nc, [arrays], core_ids=[0]).results[0]
    y = np.asarray(r["yT"]).transpose(2, 1, 0).reshape(NT, D)
    state = np.asarray(r["new_state"]).reshape(L, 2, DK, GH, DV).transpose(0, 1, 3, 2, 4)
    return (y[None, 0:T], y[None, T:NT], np.asarray(r["new_k"]).reshape(1, L, T, KVH, HD),
            np.asarray(r["new_v"]).reshape(1, L, T, KVH, HD), np.ascontiguousarray(state)[None])
```

```python
from contextlib import ExitStack

import numpy as np

import concourse.bass as bass
from concourse import mybir

F32 = mybir.dt.float32
I32 = mybir.dt.int32
ALU = mybir.AluOpType
ACT = mybir.ActivationFunctionType
AX = mybir.AxisListType.X

P = 128
T = 128
S = 2
NT = S * T
LAYERS = 2
D = 1024
KT = D // P
HD = 64
HEADS = 8
KVH = 2
G = HEADS // KVH
ROPE_THETA = 10000.0
GRID_W = 64
GH = 4
DK = 64
DV = 128
RANK = 16
NE = 16
NG = 4
EPG = NE // NG
FE = 512
FT = FE // P
EPS = 1e-6
NEG = -3.0e38

Q0, K0, V0, GQ0, GK0, GV0, GG0, LR0, GA0, GB0 = 0, 512, 640, 768, 1024, 1280, 1792, 2304, 2336, 3360
IN_W = 4384
EXP_LN = "natural_log_exp_and_others"
RSQ = 5
TMW = LR0
IN_UNITS = [(0, 512), (512, 512), (1024, 512), (1536, 512), (2048, 288)]
GATE_UNITS = [(GA0, 512), (GA0 + 512, 512), (GB0, 512), (GB0 + 512, 512)]

RING = 6
UNIT = 4096
ADA = 12
SLOTS = 64
PAIRS = NE // 2
PASS_END = PAIRS + 1

LEVELS = 7
LV_COLS = LEVELS * T
D_W = LV_COLS + 2 * T

CONSTS = [("ident", P), ("ones", P), ("dec_f", D_W), ("dec_b", D_W), ("mask", LV_COLS + T), ("before", P),
          ("slot", SLOTS), ("cos", HD), ("sin", HD), ("order_g", NG), ("order_e", NE), ("sel", S)]
PARAMS = [("cond", KT * S), ("b_ada", LAYERS * 48), ("norm1", LAYERS * KT), ("norm2", LAYERS * KT),
          ("bias_r", NE), ("w_r", KT * NE)]
LPARAMS = [("state", GH * DV), ("ck", P), ("cv", P), ("w2", 2 * GH * DK), ("qn", HD), ("kn", HD), ("gln", DV)]


def offsets(parts):
    at, out = 0, {}
    for name, n in parts:
        out[name] = (at, n)
        at += n
    return out, at


CO, CW = offsets(CONSTS)
PO, PW = offsets(PARAMS)
LO, LW = offsets(LPARAMS)

FILL = [("gate", c) for c in range(8)]
for _i in range(4):
    FILL += [("ada", 4 + _i), ("pa", _i)]
FILL += [("ada", a) for a in range(8, ADA)]
EARLY = 2


def dense_order():
    out = [(0, "ada", a) for a in range(4)]
    for l in range(LAYERS):
        out += [(l, "in", n) for n in range(len(IN_UNITS))]
        for kind, n in FILL:
            if kind == "ada" or (kind, n) == ("pa", 0):
                out.append((l, kind, n))
            elif kind == "gate" and n % 2 == 0:
                out.append((l, "gates", n // 2))
        out += [(l, "pb", 0), (l, "out", 0), (l, "out", 1)]
        if l + 1 < LAYERS:
            out += [(l + 1, "ada", a) for a in range(4)]
    return out


ORDER = dense_order()
PLACE = {key: n for n, key in enumerate(ORDER)}
BEFORE = [max(n for n, key in enumerate(ORDER) if key[0] == l and key[1] == "out") + 1 + (4 if l + 1 < LAYERS else 0)
          for l in range(LAYERS)]


def build(nc, xT, consts, params, lparams, w_ada, w_in, w_pa, w_pb, w_out, w_gate, w_up, w_down,
          yT, new_k, new_v, new_state):
    ctx = ExitStack()
    with ctx:
        def sb(name, shape, dt=F32):
            return ctx.enter_context(nc.sbuf_tensor(name, shape, dt))

        def sem(name):
            return ctx.enter_context(nc.semaphore(name))

        ring = sb("ring", [P, RING, UNIT])
        cst = sb("cst", [P, CW])
        par = sb("par", [P, PW])
        lpar = sb("lpar", [P, LW])
        x = sb("x", [P, KT, NT])
        h = sb("h", [P, KT, NT])
        sga = sb("sga", [P, KT, NT])
        sgb = sb("sgb", [P, KT, NT])
        tm = sb("tm", [P, S, TMW])
        la = sb("la", [P, S, 2 * GH * DK])
        lrt = sb("lrt", [P, NT])
        ereg = sb("ereg", [P, 2, 1024])
        qe = sb("qe", [P, LEVELS, T])
        ke = sb("ke", [P, LEVELS, T])
        qk2 = sb("qk2", [P, 2, 2, T])
        st = sb("st", [P, T])
        qin = sb("qin", [P, T])
        kst = sb("kst", [P, T])
        sfin = sb("sfin", [P, GH, DV])
        ot = sb("ot", [P, 4, NT])
        ogt = sb("ogt", [P, 4, NT])
        adarow = sb("adarow", [P, 512])
        mod = sb("mod", [P, LAYERS, 48, S])
        modA = sb("modA", [P, LAYERS, 2, KT, S])
        cs = sb("cs", [P, KT, 32])
        rs = sb("rs", [P, NT])
        sm = sb("sm", [P, 128])
        npass = sb("npass", [1, LAYERS], I32)
        ps = ctx.enter_context(nc.psum_tensor("ps", [P, 8, 512], F32))

        def C(name):
            at, n = CO[name]
            return cst[:, at:at + n]

        def PR(name):
            at, n = PO[name]
            return par[:, at:at + n]

        def LP(name):
            at, n = LO[name]
            return lpar[:, at:at + n]

        ident, ones = C("ident"), C("ones")
        BIG_RMS = (rs[:, :], qk2[:, 0, :, :].rearrange("p a t -> p (a t)"), qk2[:, 1, :, :].rearrange("p a t -> p (a t)"))
        QK_RMS = (sm[:, 32:52], sm[:, 64:84], sm[:, 84:104])
        GLA_RMS = (sm[:, 52:56], sm[:, 104:108], sm[:, 108:112])
        qt = ogt[:, 0:2, :].rearrange("p a (b t) -> p (a b) t", b=2)
        kt_all = ogt[:, 2, :]
        prob = ereg[:, 0, :]
        probt = ereg[:, 1, :]
        tmf = tm[:, :, :].rearrange("p s n -> p (s n)")
        hg = tmf[:, 0:1024].rearrange("p (k n) -> p k n", k=KT)
        yy = tmf[:, 1024:2048]
        eg = tmf[:, 2048:2560].rearrange("p (a n) -> p a n", a=2)
        aa = tmf[:, 2560:3072].rearrange("p (a n) -> p a n", a=2)
        at_ = tmf[:, 3072:3584].rearrange("p (a n) -> p a n", a=FT)
        gwt = tmf[:, 3584:3840]
        gg = tmf[:, 3840:4096].rearrange("p (s n) -> p s n", s=S)
        gw = tmf[:, 4096:4352].rearrange("p (s n) -> p s n", s=S)
        h2tok = sgb[:, :, :].rearrange("p (s a) n -> p s (a n)", s=S)
        rt = rs[:, 0:6 * S * NE].rearrange("p (a s e) -> p a s e", a=6, s=S)
        posm = st[:, 0:S * (NE + 2)].rearrange("p (s e) -> p s e", s=S)
        gates = st[:, 64:64 + S * (NE + 2)].rearrange("p (s e) -> p s e", s=S)

        in_x, in_c, in_p, in_lp = sem("in_x"), sem("in_c"), sem("in_p"), sem("in_lp")
        dense_full = [sem(f"dense_full{u}") for u in range(RING)]
        m_silu, m_shift = [[sem(f"{n}{l}") for l in range(LAYERS)] for n in ("m_silu", "m_shift")]
        moe_full = [[sem(f"moe_full{l}_{u}") for u in range(RING)] for l in range(LAYERS)]
        cond_exp, cs_ready, zeroed = sem("cond_exp"), sem("cs_ready"), sem("zeroed")
        ada_rows, ada_copied, ada_cols, ada_mod = sem("ada_rows"), sem("ada_copied"), sem("ada_cols"), sem("ada_mod")
        sq_act, sq_dve, ssum, xr_ready = sem("sq_act"), sem("sq_dve"), sem("ssum"), sem("xr_ready")
        gain_ready = sem("gain_ready")
        var_ready, rsq_ready = sem("var_ready"), sem("rsq_ready")
        h_dve, h_act = sem("h_dve"), sem("h_act")
        proj, proj_copied, proj_lr, lr_copied = sem("proj"), sem("proj_copied"), sem("proj_lr"), sem("lr_copied")
        la_mm, la_min, la_ln, la_ready = sem("la_mm"), sem("la_min"), sem("la_ln"), sem("la_ready")
        gg_exp, gg_ready = sem("gg_exp"), sem("gg_ready")
        k_normed, qk_ready = sem("k_normed"), sem("qk_ready")
        att_t, att_copied = sem("att_t"), sem("att_copied")
        scored, maxed, exped, normed = sem("scored"), sem("maxed"), sem("exped"), sem("normed")
        prob_t, prob_copied, att_o, att_o_copied = sem("prob_t"), sem("prob_copied"), sem("att_o"), sem("att_o_copied")
        gate_mm, gate_exp, gate_sig = sem("gate_mm"), sem("gate_exp"), sem("gate_sig")
        g_t, g_copied, g_dec, g_exp = sem("g_t"), sem("g_copied"), sem("g_dec"), sem("g_exp")
        g_qe, g_ke, g_lev, g_st, g_o, g_o_copied = (sem("g_qe"), sem("g_ke"), sem("g_lev"), sem("g_st"), sem("g_o"),
                                                    sem("g_o_copied"))
        g_kt, g_kt_copied, g_sf_copied = sem("g_kt"), sem("g_kt_copied"), sem("g_sf_copied")
        g_normed, g_nt, g_nt_copied = sem("g_normed"), sem("g_nt"), sem("g_nt_copied")
        pa_mm, pa_used, pb_mm, merged = sem("pa_mm"), sem("pa_used"), sem("pb_mm"), sem("merged")
        out_mm, x_mid, x_done = sem("out_mm"), sem("x_mid"), sem("x_done")
        r_log, r_exp_in, h2_t, h2_copied = sem("r_log"), sem("r_exp_in"), sem("h2_t"), sem("h2_copied")
        sel_ready, pos_mm, routed = sem("sel_ready"), sem("pos_mm"), sem("routed")

        def per_layer(name):
            return [sem(f"{name}{l}") for l in range(LAYERS)]

        m_onehot, m_gather, m_hg = per_layer("m_onehot"), per_layer("m_gather"), per_layer("m_hg")
        m_gwt, m_gwt_copied, m_sig = per_layer("m_gwt"), per_layer("m_gwt_copied"), per_layer("m_sig")
        m_gu = [[sem(f"m_gu{l}_{half}") for half in range(2)] for l in range(LAYERS)]
        m_dn = [[sem(f"m_dn{l}_{half}") for half in range(2)] for l in range(LAYERS)]
        m_act, m_at, m_at_copied = per_layer("m_act"), per_layer("m_at"), per_layer("m_at_copied")
        m_dy, m_y, m_scat, m_x = per_layer("m_dy"), per_layer("m_y"), per_layer("m_scat"), per_layer("m_x")
        kv_out, st_out, y_out = sem("kv_out"), sem("st_out"), sem("y_out")
        dve_step, act_step, pool_step = sem("dve_step"), sem("act_step"), sem("pool_step")

        def unit_src(key):
            _, kind, n = key
            l = key[0]
            rows = lambda w: w.rearrange("(k p) n -> p k n", p=P)
            if kind == "ada":
                return rows(w_ada[l])[:, :, n * 512:(n + 1) * 512]
            if kind in ("in", "gates"):
                at, w = (IN_UNITS if kind == "in" else GATE_UNITS)[n]
                return rows(w_in[l])[:, :, at:at + w]
            if kind == "out":
                return rows(w_out[l])[:, :, n * 512:(n + 1) * 512]
            return rows({"pa": w_pa, "pb": w_pb}[kind][l])

        def unit(key):
            n = PLACE[key]
            kts = 4 if key[1] in ("pa", "pb") else KT
            w = IN_UNITS[key[2]][1] if key[1] == "in" else UNIT // kts
            return ring[:, n % RING, 0:kts * w].rearrange("p (k n) -> p k n", k=kts), n

        gu_units = ring[:, 0:4, :].rearrange("p (h e) (j k n) -> p h e j k n", e=2, j=2, k=KT)
        down_units = ring[:, 4:6, :].rearrange("p h (e k n) -> p h e k n", e=2, k=FT // 2)

        def used(n):
            l, kind, i = ORDER[n]
            return {"ada": (ada_rows, ADA * l + i + 1),
                    "in": (proj, 10 * l + 2 * i + 2) if i < 4 else (proj_lr, l + 1),
                    "gates": (gate_mm, 8 * l + 2 * i + 2),
                    "pa": (pa_mm, 4 * l + 4), "pb": (pb_mm, 4 * l + 4), "out": (out_mm, 4 * l + 2 * i + 2)}[kind]

        block = ctx.enter_context(nc.Block())

        @block.sync
        def _(sp):
            sp.dma_start(par[:, :], params).then_inc(in_p, 16)
            sp.dma_start(x[:, :, :], xT).then_inc(in_x, 16)
            sp.dma_start(cst[:, :], consts).then_inc(in_c, 16)

            def pair(l, pr, waits):
                for u in range(RING):
                    sp.wait_ge(*waits[u])
                    for j in range(2):
                        if u < 4:
                            hh, e = u // 2, u % 2
                            src = (w_gate, w_up)[j][l, bass.ds(pr * 2 + e, 1)].rearrange("o (k p) n -> p (o k) n", p=P)
                            src, dst = src[:, :, hh * 256:(hh + 1) * 256], gu_units[:, hh, e, j]
                        else:
                            src = w_down[l, bass.ds(pr * 2 + j, 1)].rearrange("o (k p) n -> p (o k) n", p=P)
                            src, dst = src[:, 2 * (u - 4):2 * (u - 4) + 2, :], down_units[:, u - 4, j]
                        sp.dma_start(dst, src).then_inc(moe_full[l][u], 16)

            def expert_use(l, q):
                return [(m_gu[l][0], q + 1)] * 2 + [(m_gu[l][1], q + 1)] * 2 + [(m_dn[l][0], q + 1), (m_dn[l][1], q + 1)]

            n = 0
            for l in range(LAYERS):
                while n < BEFORE[l]:
                    dst, _ = unit(ORDER[n])
                    if n >= RING:
                        sp.wait_ge(*used(n - RING))
                    if l and n - BEFORE[l - 1] < RING:
                        sp.wait_ge(*expert_use(l - 1, passes * PAIRS)[n % RING])
                    sp.dma_start(dst, unit_src(ORDER[n])).then_inc(dense_full[n % RING], 16)
                    n += 1
                pair(l, 0, [used(max(m for m in range(n) if m % RING == u)) for u in range(RING)])
                with sp.Fori(1, PAIRS) as pr:
                    pair(l, pr, expert_use(l, pr))
                sp.wait_ge(routed, l + 1)
                passes = sp.snap(sp.value_load(npass[0:1, l:l + 1], min_val=1, max_val=4))
                with sp.If(passes - 1):
                    with sp.Fori(1, passes) as pss:
                        with sp.Fori(0, PAIRS) as pr:
                            pair(l, pr, expert_use(l, pss * PAIRS + pr))
            sp.wait_ge(x_done, LAYERS)
            sp.dma_start(yT, x[:, :, :]).then_inc(y_out, 16)
            sp.wait_ge(y_out, 16)

        @block.tensor
        def _(pe):
            def full(*key):
                w, n = unit(key)
                pe.wait_ge(dense_full[n % RING], 16 * (n // RING + 1))
                return w

            def ada_a(l, a):
                w = full(l, "ada", a)
                if l or a:
                    pe.wait_ge(ada_copied, l * ADA + a)
                for k in range(KT):
                    j = 32 * (k % 4)
                    mm = pe.matmul(ps[j:j + 32, 7, :], cs[:, k, :], w[:, k, :], start=k < 4, stop=k >= 4)
                mm.then_inc(ada_rows, 1)

            def ada_b(l, a):
                pe.wait_ge(ada_copied, l * ADA + a + 1)
                if l or a:
                    pe.wait_ge(ada_mod, l * ADA + a)
                for i in range(4):
                    mm = pe.matmul(ps[:, 6, 2 * i:2 * i + 2], adarow[:, i * P:(i + 1) * P], C("sel"),
                                   start=True, stop=True)
                mm.then_inc(ada_cols, 1)

            def gate_chunk(l, c):
                w = full(l, "gates", c // 2)
                if l or c:
                    pe.wait_ge(gate_exp, l * 8 + c)
                if c == 0:
                    pe.wait_ge(la_min, 2 * l + 2)
                for i in range(2):
                    m = (c % 2) * 2 + i
                    for k in range(KT):
                        mm = pe.matmul(ps[:, 5, i * NT:(i + 1) * NT], w[:, k, m * P:(m + 1) * P], h[:, k, :],
                                       start=k == 0, stop=k == KT - 1)
                mm.then_inc(gate_mm, 1)

            def pa_chunk(l, m):
                w = full(l, "pa", 0)
                if m == 0:
                    pe.wait_ge(gate_exp, 8 * (l + 1))
                else:
                    pe.wait_ge(pa_used, 4 * l + m)
                for i in range(2):
                    for k in range(4):
                        mm = pe.matmul(ps[:, 5, i * NT:(i + 1) * NT], w[:, k, (2 * m + i) * P:(2 * m + i + 1) * P],
                                       ot[:, k, :], start=k == 0, stop=k == 3)
                mm.then_inc(pa_mm, 1)

            fills = []
            late = []

            def fill(l):
                while late:
                    ada_b(*late.pop())
                if fills:
                    kind, n = fills.pop(0)
                    if kind == "ada":
                        ada_a(l, n)
                        late.append((l, n))
                    else:
                        (gate_chunk if kind == "gate" else pa_chunk)(l, n)

            def norm_sum(n):
                pe.wait_ge(sq_act, n + 1)
                pe.wait_ge(sq_dve, n + 1)
                for k in range(KT):
                    mm = pe.matmul(ps[:, 0, 0:NT], ones, sgb[:, k, :], start=k == 0, stop=k == KT - 1)
                mm.then_inc(ssum, 1)

            pe.wait_ge(in_c, 16)
            pe.wait_ge(in_p, 16)
            pe.wait_ge(cs_ready, 1)
            for l in range(LAYERS):
                if l:
                    pe.wait_ge(x_done, l)
                norm_sum(2 * l)
                if l == 0:
                    for a in range(4):
                        ada_a(l, a)
                        ada_b(l, a)
                pe.wait_ge(h_dve, 2 * l + 1)
                pe.wait_ge(h_act, 2 * l + 1)
                for n in range(2 * len(IN_UNITS)):
                    w = full(l, "in", n // 2)
                    if n >= 4:
                        pe.wait_ge(proj_copied, 10 * l + n - 3)
                    cols = min(512, TMW - IN_UNITS[n // 2][0])
                    for k in range(KT):
                        mm = pe.matmul(ps[:, n % 4, 0:cols], h[:, k, (n % 2) * T:(n % 2) * T + T], w[:, k, 0:cols],
                                       start=k == 0, stop=k == KT - 1)
                    mm.then_inc(proj, 1)
                for k in range(KT):
                    mm = pe.matmul(ps[0:32, 4, 0:NT], w[:, k, 256:288], h[:, k, :], start=k == 0, stop=k == KT - 1)
                mm.then_inc(proj_lr, 1)
                pe.wait_ge(lr_copied, l + 1)
                pe.wait_ge(in_lp, 16 * (l + 1))
                for s in range(S):
                    pe.matmul(ps[:, 4 + s, :], lrt[0:33, s * T:(s + 1) * T], LP("w2")[0:33, :],
                              start=True, stop=True).then_inc(la_mm, 1)
                fills[:] = list(FILL)
                for _ in range(EARLY):
                    fill(l)
                for s in range(S):
                    if s == 0:
                        pe.wait_ge(qk_ready, l + 1)
                        pe.wait_ge(proj_copied, 10 * (l + 1))
                    else:
                        pe.wait_ge(exped, 4 * l + 2)
                    for g in range(G):
                        mm = pe.transpose(ps[:, 0, g * P:(g + 1) * P], tm[:, s, Q0 + g * P:Q0 + (g + 1) * P], ident)
                    mm = pe.transpose(ps[:, 1, 0:P], tm[:, s, K0:V0], ident)
                    if s:
                        mm = pe.transpose(ps[:, 1, P:2 * P], LP("ck"), ident)
                    mm.then_inc(att_t, 1)
                    fill(l)
                    nb = 1 + s
                    nk = nb * T
                    for v in range(KVH):
                        b = 4 * l + 2 * s + v
                        if v == 0:
                            pe.wait_ge(att_copied, 2 * l + s + 1)
                        else:
                            pe.wait_ge(exped, b)
                        for g in range(G):
                            at = g * nk
                            mm = pe.matmul(ps[:, at // 512, at % 512:at % 512 + nk], qt[v * HD:(v + 1) * HD, g, :],
                                           kt_all[v * HD:(v + 1) * HD, 0:nk], start=True, stop=True)
                        mm.then_inc(scored, 1)
                        fill(l)
                        pe.wait_ge(normed, b + 1)
                        if b:
                            pe.wait_ge(prob_copied, b)
                        for j in range(G * nb):
                            mm = pe.transpose(ps[:, 2 + j // 4, (j % 4) * P:(j % 4 + 1) * P],
                                              prob[:, j * P:(j + 1) * P], ident)
                        mm.then_inc(prob_t, 1)
                        pe.wait_ge(prob_copied, b + 1)
                        if b:
                            pe.wait_ge(att_o_copied, b)
                        for g in range(G):
                            r = HD * (g % 2)
                            for j in range(nb):
                                val = (LP("cv") if j else tm[:, s, V0:GQ0])[:, v * HD:(v + 1) * HD]
                                mm = pe.matmul(ps[r:r + HD, 4, (g // 2) * T:(g // 2 + 1) * T], val,
                                               probt[:, (g * nb + j) * T:(g * nb + j + 1) * T],
                                               start=j == 0, stop=j == nb - 1)
                        mm.then_inc(att_o, 1)
                pe.wait_ge(att_o_copied, 4 * (l + 1))
                pe.wait_ge(la_ready, 2 * (l + 1))

                def gla_in(i):
                    s, hh = i // GH, i % GH
                    n = 8 * l + i
                    if i:
                        pe.wait_ge(g_o_copied, n - 1)
                        if i <= GH + 1:
                            pe.wait_ge(g_kt_copied, 4 * l + i - 1)
                    for j, at in enumerate((GQ0, GK0)):
                        for d in range(2):
                            mm = pe.matmul(ps[d * DK:(d + 1) * DK, 4, j * T:(j + 1) * T],
                                           tm[:, s, at + hh * DK:at + (hh + 1) * DK], ident, start=True, stop=True)
                    mm.then_inc(g_t, 1)
                    if i:
                        pe.wait_ge(g_exp, n)
                    last = ((512, 512, 0),) if s == 0 else ((512, 384, 0), (LV_COLS + T, T, 384))
                    for half, parts in enumerate((((0, 512, 0),), last)):
                        for at, w, to in parts:
                            for d, dec in enumerate((C("dec_f"), C("dec_b"))):
                                mm = pe.matmul(ps[d * DK:(d + 1) * DK, half, to:to + w],
                                               la[:, s, d * GH * DK + hh * DK:d * GH * DK + (hh + 1) * DK],
                                               dec[:, at:at + w], start=True, stop=True)
                    mm.then_inc(g_dec, 1)

                def gla_levels(i):
                    n = 8 * l + i
                    pe.wait_ge(g_qe, n + 1)
                    pe.wait_ge(g_ke, n + 1)
                    if i:
                        pe.wait_ge(g_st, n)
                    b = i % 2
                    for v in range(LEVELS + 1):
                        lhs, rhs = (ke[:, v, :], qe[:, v, :]) if v < LEVELS else (qk2[:, b, 1, :], qk2[:, b, 0, :])
                        mm = pe.matmul(ps[:, 2 + v // 4, (v % 4) * T:(v % 4 + 1) * T], lhs, rhs, start=True, stop=True)
                    mm.then_inc(g_lev, 1)

                def gla_keys(i):
                    pe.wait_ge(g_copied, 8 * l + i + 2)
                    pe.transpose(ps[:, 4, 384:512], kst[:, :], ident).then_inc(g_kt, 1)

                def gla_out(i):
                    s, hh = i // GH, i % GH
                    n = 8 * l + i
                    pe.wait_ge(g_st, n + 1)
                    pe.wait_ge(g_copied, 8 * l + min(i + 2, 8))
                    if i:
                        pe.wait_ge(g_o_copied, n)
                    if s == 0:
                        pe.wait_ge(g_kt_copied, 4 * l + i + 1)
                    val = tm[:, s, GV0 + hh * DV:GV0 + (hh + 1) * DV]
                    mm = pe.matmul(ps[:, 4, 256:384], st[:, :], val, start=True, stop=s == 0)
                    if s:
                        mm = pe.matmul(ps[:, 4, 256:384], qin[:, :], LP("state")[:, hh * DV:(hh + 1) * DV],
                                       start=False, stop=True)
                    else:
                        mm = pe.matmul(ps[:, 4, 384:512], lrt[:, 0:T], val, start=True, stop=True)
                    mm.then_inc(g_o, 1)

                gla_in(0)
                for i in range(8):
                    fill(l)
                    gla_levels(i)
                    if i < 7:
                        gla_in(i + 1)
                    if i < GH:
                        gla_keys(i)
                    fill(l)
                    gla_out(i)
                while fills or late:
                    fill(l)
                pe.wait_ge(pa_used, 4 * (l + 1))
                pe.wait_ge(g_exp, 8 * (l + 1))
                pe.wait_ge(g_o_copied, 8 * (l + 1))
                for s in range(S):
                    pe.wait_ge(g_normed, 2 * l + s + 1)
                    for k in range(4):
                        mm = pe.transpose(ps[:, 4 + s, k * P:(k + 1) * P], tm[:, s, k * P:(k + 1) * P], ident)
                    mm.then_inc(g_nt, 1)
                w = full(l, "pb", 0)
                pe.wait_ge(g_nt_copied, 2 * (l + 1))
                for m in range(4):
                    for i in range(2):
                        for k in range(4):
                            mm = pe.matmul(ps[:, m, i * NT:(i + 1) * NT], w[:, k, (2 * m + i) * P:(2 * m + i + 1) * P],
                                           ogt[:, k, :], start=k == 0, stop=k == 3)
                    mm.then_inc(pb_mm, 1)
                pe.wait_ge(merged, 4 * (l + 1))
                pe.wait_ge(ada_mod, ADA * (l + 1))
                for m in range(4):
                    w = full(l, "out", m // 2)
                    for i in range(2):
                        for k in range(KT):
                            c = (m % 2) * 2 + i
                            mm = pe.matmul(ps[:, 4 + m, i * NT:(i + 1) * NT], w[:, k, c * P:(c + 1) * P], sga[:, k, :],
                                           start=k == 0, stop=k == KT - 1)
                    mm.then_inc(out_mm, 1)
                norm_sum(2 * l + 1)
                if l + 1 < LAYERS:
                    ada_a(l + 1, 0)
                pe.wait_ge(h_dve, 2 * l + 2)
                pe.wait_ge(h_act, 2 * l + 2)
                for s in range(S):
                    for k in range(KT):
                        mm = pe.matmul(ps[:, 1, s * NE:(s + 1) * NE], h[:, k, s * T:(s + 1) * T],
                                       PR("w_r")[:, k * NE:(k + 1) * NE], start=k == 0, stop=k == KT - 1)
                mm.then_inc(r_log, 1)
                for b in range(4):
                    for j in range(4):
                        s, k = (4 * b + j) // KT, (4 * b + j) % KT
                        mm = pe.transpose(ps[:, 2 + b, j * P:(j + 1) * P], h[:, k, s * T:(s + 1) * T], ident)
                    mm.then_inc(h2_t, 1)
                if l + 1 < LAYERS:
                    ada_b(l + 1, 0)
                    ada_a(l + 1, 1)
                pe.wait_ge(sel_ready, l + 1)
                sel = rt[:, 0, :, :]
                for s in range(S):
                    if s:
                        pe.matmul(ps[:, 1, 64 + NE:64 + 2 * NE], ones, sel[:, 0, :], start=True, stop=False)
                    pe.matmul(ps[:, 1, 64 + s * NE:64 + (s + 1) * NE], C("before"), sel[:, s, :], start=s == 0, stop=True)
                for s in range(S):
                    mm = pe.matmul(ps[:, 1, 128:128 + NE], ones, sel[:, s, :], start=s == 0, stop=s == 1)
                mm.then_inc(pos_mm, 1)
                if l + 1 < LAYERS:
                    ada_b(l + 1, 1)
                    for a in range(2, 4):
                        ada_a(l + 1, a)
                        ada_b(l + 1, a)
                pe.wait_ge(h2_copied, 4 * (l + 1))
                pe.wait_ge(routed, l + 1)
                passes = pe.snap(pe.value_load(npass[0:1, l:l + 1], min_val=1, max_val=4))
                for s_ in (m_gather[l], m_gwt[l], *m_gu[l], m_at[l], *m_dn[l], m_scat[l]):
                    pe.sem_inc(s_, 1)
                if l + 1 < LAYERS:
                    pe.wait_ge(ada_mod, ADA * (l + 1) + 4)
                with pe.Fori(0, passes) as pss:
                    with pe.Fori(0, PAIRS) as pr:
                        q = pss * PAIRS + pr
                        pe.wait_ge(m_onehot[l], pss * PASS_END + pr + 2)
                        pe.wait_ge(m_x[l], q * 4 + 1)
                        for b in range(2):
                            for j in range(4):
                                for s in range(S):
                                    k = 4 * b + j
                                    mm = pe.matmul(ps[:, 4 + b, j * P:(j + 1) * P], h2tok[:, s, k * P:(k + 1) * P],
                                                   gg[:, s, :], start=s == 0, stop=s == 1)
                            mm.then_inc(m_gather[l], 1)
                        pe.wait_ge(m_gwt_copied[l], q + 1)
                        for s in range(S):
                            mm = pe.transpose(ps[:, 7, s * P:(s + 1) * P], gw[:, s, :], ident)
                        mm.then_inc(m_gwt[l], 1)
                        pe.wait_ge(m_act[l], q * 2 + 1)
                        for half in range(2):
                            for j in range(2):
                                if j == 0:
                                    for e in range(2):
                                        pe.wait_ge(moe_full[l][2 * half + e], q * 32 + 32)
                                for k in range(KT):
                                    if half == 0 and j == 0 and k in (0, 4):
                                        pe.wait_ge(m_hg[l], q * 2 + 2 + k // 4)
                                    for e in range(2):
                                        r = e * SLOTS
                                        mm = pe.matmul(ps[r:r + SLOTS, half, j * 256:(j + 1) * 256], hg[:, k, r:r + SLOTS],
                                                       gu_units[:, half, e, j, k, :],
                                                       start=k == 0, stop=k == KT - 1)
                            mm.then_inc(m_gu[l][half], 1)
                        pe.wait_ge(m_y[l], q * 2 + 1)

                        def down(k, n):
                            for e in range(2):
                                r = e * SLOTS
                                mm = pe.matmul(ps[r:r + SLOTS, 2 + n, :], at_[:, k, r:r + SLOTS],
                                               down_units[:, k // 2, e, k % 2, n * 512:(n + 1) * 512],
                                               start=k == 0, stop=k == FT - 1)
                            return mm

                        for half in range(2):
                            pe.wait_ge(m_act[l], q * 2 + 2 + half)
                            pe.wait_ge(m_at_copied[l], q * 2 + 1 + half)
                            for j in range(2):
                                mm = pe.transpose(ps[:, 6, (2 * half + j) * P:(2 * half + j + 1) * P],
                                                  aa[:, half, j * P:(j + 1) * P], ident)
                            mm.then_inc(m_at[l], 1)
                            pe.wait_ge(m_at_copied[l], q * 2 + 2 + half)
                            pe.wait_ge(moe_full[l][4 + half], q * 32 + 32)
                            if half == 0:
                                for k in range(2):
                                    for n in range(2):
                                        mm = down(k, n)
                                mm.then_inc(m_dn[l][0], 1)
                            else:
                                for n in range(2):
                                    down(2, n)
                                    down(3, n).then_inc((m_dy[l], m_dn[l][1])[n], 1)
                        pe.wait_ge(m_gwt_copied[l], q + 2)
                        for f in range(4):
                            if f % 2 == 0:
                                pe.wait_ge(m_y[l], q * 2 + 2 + f // 2)
                            if f >= 2:
                                pe.wait_ge(m_x[l], q * 4 + f)
                            for j in range(2):
                                k = 2 * f + j
                                mm = pe.matmul(ps[:, 4 + f % 2, j * NT:(j + 1) * NT], yy[:, k * P:(k + 1) * P], gwt,
                                               start=True, stop=True)
                            mm.then_inc(m_scat[l], 1)

        @block.scalar
        def _(act):
            steps = [0]

            def link(ins):
                steps[0] += 1
                ins.then_inc(act_step, 1)
                act.wait_ge(act_step, steps[0])

            def copy(out, in_, scale=1.0):
                return act.activation(out, in_, ACT.Copy, scale=scale)

            def inv_root(work, step):
                act.wait_ge(var_ready, step)
                link(act.activation(work[1], work[0], ACT.Ln))
                act.activation(work[1], work[1], ACT.Exp, scale=-0.5).then_inc(rsq_ready, 1)

            def squares(n):
                act.activation(sgb[:, 0:4, :], x[:, 0:4, :], ACT.Square).then_inc(sq_act, 1)

            def modulate(l, n):
                act.wait_ge(xr_ready, 2 * (2 * l + n) + 1)
                act.wait_ge(gain_ready, 2 * l + n + 1)
                for k in range(4, KT):
                    for s in range(S):
                        c = slice(s * T, (s + 1) * T)
                        ins = act.activation(h[:, k, c], h[:, k, c], ACT.Identity, bias=mod[:, l, 24 * n + k, s:s + 1],
                                             scale=modA[:, l, n, k, s:s + 1])
                ins.then_inc(h_act, 1)

            def ada_copy(l, a):
                act.wait_ge(ada_rows, l * ADA + a + 1)
                if l or a:
                    act.wait_ge(ada_cols, l * ADA + a)
                copy(adarow[:, :], ps[:, 7, :]).then_inc(ada_copied, 1)

            def gate_copy(l, c):
                act.wait_ge(gate_mm, 8 * l + c + 1)
                if c == 0:
                    act.wait_ge(la_ready, 2 * l + 2)
                if c == 4:
                    act.wait_ge(gg_ready, l + 1)
                to = (sga if c < 4 else sgb)[:, 2 * (c % 4):2 * (c % 4) + 2, :]
                copy(to, ps[:, 5, :].rearrange("p (a n) -> p a n", a=2)).then_inc(gate_exp, 1)
                if c == 7:
                    act.wait_ge(gate_exp, 8 * (l + 1))
                    act.activation(sga[:, :, :], sga[:, :, :], ACT.Sigmoid)
                    act.activation(sgb[:, :, :], sgb[:, :, :], ACT.Sigmoid).then_inc(gate_sig, 1)
                    act.preload_act_table_set(EXP_LN)

            fills = []

            def fill(l):
                if fills:
                    kind, n = fills.pop(0)
                    if kind != "pa":
                        (ada_copy if kind == "ada" else gate_copy)(l, n)

            act.preload_act_table_set(EXP_LN)
            act.wait_ge(in_p, 16)
            act.activation(sm[:, 0:16], PR("cond"), ACT.Exp, scale=-1.0).then_inc(cond_exp, 1)
            act.wait_ge(in_x, 16)
            for l in range(LAYERS):
                if l:
                    act.preload_act_table_set(EXP_LN)
                    act.wait_ge(x_done, l)
                squares(2 * l)
                inv_root(BIG_RMS, RSQ * l + 1)
                if l == 0:
                    for a in range(4):
                        ada_copy(l, a)
                modulate(l, 0)
                for n in range(2 * len(IN_UNITS)):
                    if n == 6:
                        inv_root(QK_RMS, RSQ * l + 2)
                    act.wait_ge(proj, 10 * l + n + 1)
                    at = IN_UNITS[n // 2][0]
                    cols = min(512, TMW - at)
                    copy(tm[:, n % 2, at:at + cols], ps[:, n % 4, 0:cols]).then_inc(proj_copied, 1)
                act.wait_ge(proj_copied, 10 * (l + 1))
                act.activation(sgb[:, 0:4, :].rearrange("p (s a) n -> p s (a n)", s=S), tm[:, :, GG0:LR0],
                               ACT.Sigmoid).then_inc(gg_exp, 1)
                act.preload_act_table_set(EXP_LN)
                for s in range(S):
                    tmp = sga[:, 2 * s:2 * s + 2, :]
                    act.wait_ge(la_min, 2 * l + s + 1)
                    link(act.activation(tmp, tmp, ACT.Exp))
                    act.activation(tmp, tmp, ACT.Ln, bias=1.0).then_inc(la_ln, 1)
                fills[:] = list(FILL)
                for _ in range(EARLY):
                    fill(l)
                for s in range(S):
                    act.wait_ge(att_t, 2 * l + s + 1)
                    if s:
                        act.wait_ge(scored, 4 * l + 2)
                    copy(ogt[:, 0:2, :], ps[:, 0, :].rearrange("p (a n) -> p a n", a=2))
                    copy(kt_all[:, 0:T * (1 + s)], ps[:, 1, 0:T * (1 + s)]).then_inc(att_copied, 1)
                    fill(l)
                    nb = 1 + s
                    nk = nb * T
                    for v in range(KVH):
                        b = 4 * l + 2 * s + v
                        act.wait_ge(maxed, b + 1)
                        if b:
                            act.wait_ge(prob_t, b)
                        for g in range(G):
                            at = g * nk
                            ins = act.activation(prob[:, at:at + nk], ps[:, at // 512, at % 512:at % 512 + nk], ACT.Exp,
                                                 bias=sm[:, 24 + g:25 + g], scale=HD ** -0.5,
                                                 accum_out=sm[:, 28 + g:29 + g])
                        ins.then_inc(exped, 1)
                        fill(l)
                        act.wait_ge(prob_t, b + 1)
                        if b:
                            act.wait_ge(att_o, b)
                        copy(probt[:, 0:G * nk].rearrange("p (b n) -> p b n", b=nb),
                             ps[:, 2:2 + nb, :]).then_inc(prob_copied, 1)
                        act.wait_ge(att_o, b + 1)
                        copy(ot[:, 2 * v:2 * v + 2, s * T:(s + 1) * T],
                             ps[:, 4, 0:2 * T].rearrange("p (a n) -> p a n", a=2)).then_inc(att_o_copied, 1)

                def gla_in(i):
                    n = 8 * l + i
                    act.wait_ge(g_t, n + 1)
                    if i >= 2:
                        act.wait_ge(g_lev, n - 1)
                    copy(qk2[:, i % 2, 0, :], ps[:, 4, 0:T], scale=DK ** -0.5)
                    copy(qk2[:, i % 2, 1, :], ps[:, 4, T:2 * T]).then_inc(g_copied, 1)
                    act.wait_ge(g_dec, n + 1)
                    if i >= 2:
                        act.wait_ge(g_qe, n - 1)
                        act.wait_ge(g_ke, n - 1)
                    act.activation(ereg[:, i % 2, :].rearrange("p (a n) -> p a n", a=2), ps[:, 0:2, :], ACT.Exp,
                                   scale=1.0 / 16.0).then_inc(g_exp, 1)

                def gla_kt(i):
                    if i < GH:
                        m = 4 * l + i
                        act.wait_ge(g_kt, m + 1)
                        if i:
                            act.wait_ge(g_o, 8 * l + i)
                        copy(lrt[:, 0:T], ps[:, 4, 384:512]).then_inc(g_kt_copied, 1)

                def gla_out(i):
                    s, hh = i // GH, i % GH
                    n = 8 * l + i
                    act.wait_ge(g_o, n + 1)
                    if s == 0:
                        if l and i == 0:
                            act.wait_ge(st_out, 16 * l)
                        copy(sfin[:, hh, :], ps[:, 4, 384:512]).then_inc(g_sf_copied, 1)
                    copy(tm[:, s, hh * DV:(hh + 1) * DV], ps[:, 4, 256:384]).then_inc(g_o_copied, 1)

                act.wait_ge(prob_t, 4 * (l + 1))
                act.wait_ge(att_o, 4 * (l + 1))
                gla_in(0)
                for i in range(8):
                    fill(l)
                    if i < 7:
                        gla_in(i + 1)
                    gla_kt(i)
                    fill(l)
                    gla_out(i)
                    if i == GH:
                        inv_root(GLA_RMS, RSQ * l + 3)
                while fills:
                    fill(l)
                inv_root(GLA_RMS, RSQ * l + 4)
                for s in range(S):
                    act.wait_ge(g_nt, 2 * l + s + 1)
                    copy(ogt[:, :, s * T:(s + 1) * T],
                         ps[:, 4 + s, :].rearrange("p (a n) -> p a n", a=4)).then_inc(g_nt_copied, 1)
                act.wait_ge(x_mid, l + 1)
                squares(2 * l + 1)
                inv_root(BIG_RMS, RSQ * l + 5)
                if l + 1 < LAYERS:
                    ada_copy(l + 1, 0)
                modulate(l, 1)
                act.wait_ge(r_log, l + 1)
                act.activation(rt[:, 1, :, :], ps[:, 1, 0:2 * NE].rearrange("p (s e) -> p s e", s=S), ACT.Exp,
                               scale=-1.0).then_inc(r_exp_in, 1)
                for b in range(4):
                    act.wait_ge(h2_t, 4 * l + b + 1)
                    copy(sgb[:, 2 * b:2 * b + 2, :], ps[:, 2 + b, :].rearrange("p (a n) -> p a n", a=2)).then_inc(h2_copied, 1)
                if l + 1 < LAYERS:
                    for a in range(1, 4):
                        ada_copy(l + 1, a)
                act.wait_ge(kv_out, 32 * (l + 1))
                act.wait_ge(routed, l + 1)
                passes = act.snap(act.value_load(npass[0:1, l:l + 1], min_val=1, max_val=4))
                for s_ in (m_hg, m_gwt_copied, m_sig, m_at_copied, m_y):
                    act.sem_inc(s_[l], 1)
                act.preload_act_table(ACT.Sigmoid)
                with act.Fori(0, passes) as pss:
                    with act.Fori(0, PAIRS) as pr:
                        q = pss * PAIRS + pr
                        for b in range(2):
                            act.wait_ge(m_gather[l], q * 2 + 2 + b)
                            if b == 0:
                                act.wait_ge(m_gu[l][1], q + 1)
                            copy(hg[:, 4 * b:4 * b + 4, :],
                                 ps[:, 4 + b, :].rearrange("p (a n) -> p a n", a=4)).then_inc(m_hg[l], 1)
                        act.wait_ge(m_gwt[l], q + 2)
                        act.wait_ge(m_scat[l], q * 4 + 1)
                        copy(gwt, ps[:, 7, 0:NT]).then_inc(m_gwt_copied[l], 1)
                        for half in range(2):
                            act.wait_ge(m_gu[l][half], q + 2)
                            act.wait_ge(m_act[l], q * 2 + 1)
                            act.activation(eg[:, half, :], ps[:, half, 0:256], ACT.Sigmoid).then_inc(m_sig[l], 1)
                        for half in range(2):
                            act.wait_ge(m_at[l], q * 2 + 2 + half)
                            act.wait_ge(m_dn[l][half], q + 1)
                            copy(at_[:, 2 * half:2 * half + 2, :],
                                 ps[:, 6, half * 256:(half + 1) * 256].rearrange("p (a n) -> p a n", a=2)
                                 ).then_inc(m_at_copied[l], 1)
                        for n in range(2):
                            act.wait_ge(*((m_dy[l], q + 1), (m_dn[l][1], q + 2))[n])
                            copy(yy[:, n * 512:(n + 1) * 512], ps[:, 2 + n, :]).then_inc(m_y[l], 1)

        @block.vector
        def _(dve):
            steps = [0]

            def link(ins):
                steps[0] += 1
                ins.then_inc(dve_step, 1)
                dve.wait_ge(dve_step, steps[0])

            def rows(ap, shape):
                return ap.unsqueeze(1).to_broadcast(shape)

            def each(ap, shape):
                return ap.unsqueeze(len(shape) - 1).to_broadcast(shape)

            def inv_rms(work, n, src, step):
                v, y, t = work
                dve.tensor_scalar(v, src, 1.0 / n, EPS, ALU.mult, ALU.add).then_inc(var_ready, 1)
                dve.wait_ge(rsq_ready, step)
                link(dve.tensor_tensor(t, y, y, ALU.mult))
                link(dve.tensor_tensor(t, t, v, ALU.mult))
                link(dve.tensor_scalar(t, t, -0.5, 1.5, ALU.mult, ALU.add))
                link(dve.tensor_tensor(v, y, t, ALU.mult))

            def one_over_one_plus(ap):
                link(dve.tensor_scalar(ap, ap, 1.0, None, ALU.add))
                link(dve.reciprocal(ap, ap))

            def squares():
                dve.tensor_tensor(sgb[:, 4:KT, :], x[:, 4:KT, :], x[:, 4:KT, :], ALU.mult).then_inc(sq_dve, 1)

            def gains(l, n):
                norm = PR("norm1" if n == 0 else "norm2")[:, l * KT:(l + 1) * KT]
                c = mod[:, l, 24 * n + 8:24 * n + 16, :]
                link(dve.tensor_scalar(modA[:, l, n, :, :], c, 1.0, None, ALU.add))
                dve.tensor_tensor(modA[:, l, n, :, :], modA[:, l, n, :, :], each(norm, [P, KT, S]),
                                  ALU.mult).then_inc(gain_ready, 1)
                dve.wait_ge(gain_ready, 2 * l + n + 1)

            def norm_sum(l, n):
                dve.wait_ge(ssum, 2 * l + n + 1)
                inv_rms(BIG_RMS, D, ps[:, 0, 0:NT], RSQ * l + (1 if n == 0 else 5))
                for k in (4, 0):
                    dve.tensor_tensor(h[:, k:k + 4, :], x[:, k:k + 4, :], rows(rs[:, :], [P, 4, NT]),
                                      ALU.mult).then_inc(xr_ready, 1)

            def norm_mod(l, n):
                dve.wait_ge(ada_mod, l * ADA + (4 if n == 0 else 10))
                gains(l, n)
                dve.wait_ge(xr_ready, 2 * (2 * l + n + 1))
                for k in range(4):
                    for s in range(S):
                        c = slice(s * T, (s + 1) * T)
                        ins = dve.tensor_scalar(h[:, k, c], h[:, k, c], modA[:, l, n, k, s:s + 1],
                                                mod[:, l, 24 * n + k, s:s + 1], ALU.mult, ALU.add)
                ins.then_inc(h_dve, 1)

            def ada_bias(l, a):
                dve.wait_ge(ada_cols, l * ADA + a + 1)
                b = PR("b_ada")[:, l * 48 + 4 * a:l * 48 + 4 * a + 4]
                dve.tensor_tensor(mod[:, l, 4 * a:4 * a + 4, :], ps[:, 6, 0:8].rearrange("p (a s) -> p a s", s=S),
                                  each(b, [P, 4, S]), ALU.add).then_inc(ada_mod, 1)

            def merge_a(l, m):
                dve.wait_ge(gate_sig, l + 1)
                dve.wait_ge(pa_mm, 4 * l + m + 1)
                a = sga[:, 2 * m:2 * m + 2, :]
                dve.tensor_tensor(a, a, ps[:, 5, :].rearrange("p (a n) -> p a n", a=2), ALU.mult).then_inc(pa_used, 1)

            fills, late = [], []

            def fill(l):
                while late:
                    ada_bias(*late.pop())
                if fills:
                    kind, n = fills.pop(0)
                    if kind == "ada":
                        late.append((l, n))
                    elif kind == "pa":
                        merge_a(l, n)

            link(dve.memset(cs[:, :, :], 0.0))
            dve.wait_ge(in_p, 16)
            dve.wait_ge(cond_exp, 1)
            one_over_one_plus(sm[:, 0:16])
            dve.tensor_tensor(cs[:, :, 0:S], PR("cond").rearrange("p (k s) -> p k s", s=S),
                              sm[:, 0:16].rearrange("p (k s) -> p k s", s=S), ALU.mult).then_inc(cs_ready, 1)
            dve.wait_ge(in_x, 16)
            dve.wait_ge(in_c, 16)
            for l in range(LAYERS):
                squares()
                norm_sum(l, 0)
                if l == 0:
                    for a in range(4):
                        ada_bias(l, a)
                norm_mod(l, 0)
                dve.wait_ge(proj_copied, 10 * l + 4)
                dve.wait_ge(in_lp, 16 * (l + 1))
                qk = tm[:, :, 0:V0]
                tmp = ereg[:, :, :].rearrange("p a n -> p (a n)")[:, 0:S * V0].rearrange("p (s n) -> p s n", s=S)
                link(dve.tensor_tensor(tmp, qk, qk, ALU.mult))
                rq = sm[:, 32:52].rearrange("p (s n) -> p s n", s=S)
                link(dve.tensor_reduce(rq, tmp.rearrange("p s (h d) -> p s h d", d=HD), AX, ALU.add))
                inv_rms(QK_RMS, HD, sm[:, 32:52], RSQ * l + 2)
                for s in range(S):
                    v = tm[:, s, 0:V0].rearrange("p (h d) -> p h d", d=HD)
                    link(dve.tensor_tensor(v, v, each(rq[:, s, :], [P, 10, HD]), ALU.mult))
                    dve.tensor_tensor(v[:, 0:HEADS, :], v[:, 0:HEADS, :], rows(LP("qn"), [P, HEADS, HD]), ALU.mult)
                    dve.tensor_tensor(v[:, HEADS:10, :], v[:, HEADS:10, :], rows(LP("kn"), [P, KVH, HD]),
                                      ALU.mult).then_inc(k_normed, 1)
                    dve.wait_ge(k_normed, 2 * l + s + 1)
                v = tm[:, 1, 0:V0].rearrange("p (h d) -> p h d", d=HD)
                v5 = tm[:, 1, 0:V0].rearrange("p (h r c d) -> p h r c d", r=2, c=2, d=16)
                sn = C("sin").rearrange("p (r c d) -> p r c d", r=2, c=2)
                t1 = ereg[:, 0, 0:V0].rearrange("p (h d) -> p h d", d=HD)
                t2 = ereg[:, 1, 0:V0].rearrange("p (h r c d) -> p h r c d", r=2, c=2, d=16)
                dve.tensor_tensor(t1, v, rows(C("cos"), [P, 10, HD]), ALU.mult)
                for c in range(2):
                    ins = dve.tensor_tensor(t2[:, :, :, c, :], v5[:, :, :, 1 - c, :],
                                            sn[:, :, c, :].unsqueeze(1).to_broadcast([P, 10, 2, 16]), ALU.mult)
                link(ins)
                dve.tensor_tensor(tm[:, 1, 0:V0], ereg[:, 0, 0:V0], ereg[:, 1, 0:V0], ALU.add).then_inc(qk_ready, 1)
                dve.wait_ge(proj_lr, l + 1)
                link(dve.memset(lrt[32:33, :], 1.0))
                dve.tensor_copy(lrt[0:32, :], ps[0:32, 4, 0:NT]).then_inc(lr_copied, 1)
                for s in range(S):
                    dve.wait_ge(la_mm, 2 * l + s + 1)
                    link(dve.tensor_scalar(la[:, s, :], ps[:, 4 + s, :], 0.0, None, ALU.min))
                    dve.scalar_tensor_tensor(sga[:, 2 * s:2 * s + 2, :].rearrange("p a n -> p (a n)"), la[:, s, :], 2.0,
                                             ps[:, 4 + s, :], ALU.mult, ALU.subtract).then_inc(la_min, 1)
                for s in range(S):
                    dve.wait_ge(la_ln, 2 * l + s + 1)
                    dve.tensor_tensor(la[:, s, :].rearrange("p (a n) -> p a n", a=2),
                                      la[:, s, :].rearrange("p (a n) -> p a n", a=2), sga[:, 2 * s:2 * s + 2, :],
                                      ALU.subtract).then_inc(la_ready, 1)
                dve.wait_ge(gg_exp, l + 1)
                ge = sgb[:, 0:4, :].rearrange("p (s a) n -> p s (a n)", s=S)
                dve.tensor_tensor(tm[:, :, GG0:LR0], tm[:, :, GG0:LR0], ge, ALU.mult).then_inc(gg_ready, 1)
                fills[:] = list(FILL)
                for _ in range(EARLY):
                    fill(l)
                for s in range(S):
                    fill(l)
                    nb = 1 + s
                    nk = nb * T
                    for v in range(KVH):
                        b = 4 * l + 2 * s + v
                        dve.wait_ge(scored, b + 1)
                        if nb == 1:
                            sc = ps[:, 0, :].rearrange("p (g n) -> p g n", g=G)
                        else:
                            sc = ps[:, 0:2, :].rearrange("p a (g n) -> p (a g) n", g=2)
                        link(dve.tensor_reduce(sm[:, 20:24], sc, AX, ALU.max))
                        dve.tensor_scalar(sm[:, 24:28], sm[:, 20:24], -HD ** -0.5, None, ALU.mult).then_inc(maxed, 1)
                        fill(l)
                        dve.wait_ge(exped, b + 1)
                        link(dve.reciprocal(sm[:, 28:32], sm[:, 28:32]))
                        pv = prob[:, 0:G * nk].rearrange("p (g n) -> p g n", g=G)
                        dve.tensor_tensor(pv, pv, each(sm[:, 28:32], [P, G, nk]), ALU.mult).then_inc(normed, 1)

                def gla_q(i):
                    n = 8 * l + i
                    dve.wait_ge(g_exp, n + 1)
                    dve.wait_ge(g_copied, n + 1)
                    if n:
                        dve.wait_ge(g_lev, n)
                    if i == 0:
                        dve.wait_ge(zeroed, 2)
                    e, qs = ereg[:, i % 2, :], qk2[:, i % 2, 0, :]
                    for v in range(LEVELS):
                        ins = side(dve, qe, e, qs, v, 0)
                    if i >= GH:
                        if i > GH:
                            dve.wait_ge(g_o, n)
                        ins = dve.tensor_tensor(qin[:, :], qs, e[:, LV_COLS:LV_COLS + T], ALU.mult)
                    ins.then_inc(g_qe, 1)

                def gla_mask(i):
                    n = 8 * l + i
                    dve.wait_ge(g_lev, n + 1)
                    if i:
                        dve.wait_ge(g_o, n)
                    m = C("mask").rearrange("p (a n) -> p a n", a=2)
                    link(dve.tensor_tensor(ps[:, 2:4, :], ps[:, 2:4, :], m, ALU.mult))
                    dve.tensor_reduce(st[:, :], ps[:, 2:4, :].rearrange("p a (v t) -> p t (a v)", v=4), AX,
                                      ALU.add).then_inc(g_st, 1)

                def gla_norm(s):
                    dve.wait_ge(g_o_copied, 8 * l + 4 * s + 4)
                    o, t = tm[:, s, 0:512], tm[:, s, GQ0:GV0]
                    o3 = o.rearrange("p (h d) -> p h d", d=DV)
                    link(dve.tensor_tensor(t, o, o, ALU.mult))
                    link(dve.tensor_reduce(sm[:, 52:56], t.rearrange("p (h d) -> p h d", d=DV), AX, ALU.add))
                    inv_rms(GLA_RMS, DV, sm[:, 52:56], RSQ * l + 3 + s)
                    link(dve.tensor_tensor(o3, o3, each(sm[:, 52:56], [P, GH, DV]), ALU.mult))
                    link(dve.tensor_tensor(o3, o3, rows(LP("gln"), [P, GH, DV]), ALU.mult))
                    dve.tensor_tensor(o, o, tm[:, s, GG0:LR0], ALU.mult).then_inc(g_normed, 1)

                gla_q(0)
                for i in range(8):
                    fill(l)
                    gla_mask(i)
                    if i < 7:
                        gla_q(i + 1)
                    fill(l)
                    if i == GH:
                        gla_norm(0)
                while fills or late:
                    fill(l)
                gla_norm(1)
                for m in range(4):
                    dve.wait_ge(pb_mm, 4 * l + m + 1)
                    a, b = sga[:, 2 * m:2 * m + 2, :], sgb[:, 2 * m:2 * m + 2, :]
                    if m == 0:
                        dve.wait_ge(pa_used, 4 * (l + 1))
                    link(dve.tensor_tensor(b, b, ps[:, m, :].rearrange("p (a n) -> p a n", a=2), ALU.mult))
                    dve.tensor_tensor(a, a, b, ALU.add).then_inc(merged, 1)
                dve.wait_ge(ada_mod, ADA * (l + 1))
                for m in range(4):
                    dve.wait_ge(out_mm, 4 * l + m + 1)
                    for i in range(2):
                        for s in range(S):
                            k, c = 2 * m + i, slice(s * T, (s + 1) * T)
                            ins = dve.scalar_tensor_tensor(x[:, k, c], ps[:, 4 + m, i * NT + s * T:i * NT + (s + 1) * T],
                                                           mod[:, l, 16 + k, s:s + 1], x[:, k, c], ALU.mult, ALU.add)
                ins.then_inc(x_mid, 1)
                dve.wait_ge(x_mid, l + 1)
                squares()
                norm_sum(l, 1)
                norm_mod(l, 1)
                dve.wait_ge(r_exp_in, l + 1)
                sel, score, biased, t3, t4 = (rt[:, i, :, :] for i in (0, 1, 2, 3, 4))
                one_over_one_plus(score)
                link(dve.tensor_tensor(biased, score, rows(PR("bias_r"), [P, S, NE]), ALU.add))
                bg = rt[:, 2, :, :].rearrange("p s (g e) -> p (s g) e", g=NG)
                pairs = rs[:, 96:144].rearrange("p (g n) -> p g n", n=6)
                dve.tensor_tensor(pairs[:, :, 0:3], bg[:, :, 0:3], bg[:, :, 1:4], ALU.add)
                dve.tensor_tensor(pairs[:, :, 3:5], bg[:, :, 0:2], bg[:, :, 2:4], ALU.add)
                link(dve.tensor_tensor(pairs[:, :, 5:6], bg[:, :, 0:1], bg[:, :, 3:4], ALU.add))
                gs = sm[:, 0:8].rearrange("p (s g) -> p s g", s=S)
                link(dve.tensor_reduce(sm[:, 0:8], pairs, AX, ALU.max))

                def first_max(vals, flags, n, order):
                    link(dve.tensor_reduce(sm[:, 8:10], vals, AX, ALU.max))
                    link(dve.tensor_tensor(flags, vals, each(sm[:, 8:10], [P, S, n]), ALU.is_equal))
                    link(dve.tensor_tensor(flags, flags, rows(order, [P, S, n]), ALU.mult))
                    link(dve.tensor_reduce(sm[:, 8:10], flags, AX, ALU.max))
                    link(dve.tensor_tensor(flags, flags, each(sm[:, 8:10], [P, S, n]), ALU.is_equal))

                gf = sm[:, 10:18].rearrange("p (s g) -> p s g", s=S)
                first_max(gs, gf, NG, C("order_g"))
                link(dve.tensor_tensor(bg, bg, each(sm[:, 10:18], [P, S * NG, EPG]), ALU.mult))
                link(dve.tensor_scalar(sm[:, 10:18], sm[:, 10:18], -1.0, -NEG, ALU.add, ALU.mult))
                link(dve.tensor_tensor(bg, bg, each(sm[:, 10:18], [P, S * NG, EPG]), ALU.add))
                first_max(biased, t3, NE, C("order_e"))
                link(dve.tensor_scalar(t4, t3, NEG, None, ALU.mult))
                link(dve.tensor_tensor(biased, biased, t4, ALU.add))
                first_max(biased, t4, NE, C("order_e"))
                dve.tensor_tensor(sel, t3, t4, ALU.add).then_inc(sel_ready, 1)
                if l + 1 < LAYERS:
                    ada_bias(l + 1, 0)
                dve.wait_ge(sel_ready, l + 1)
                gt = gates[:, :, 0:NE]
                link(dve.tensor_tensor(gt, score, sel, ALU.mult))
                link(dve.tensor_reduce(sm[:, 8:10], gt, AX, ALU.add))
                link(dve.reciprocal(sm[:, 8:10], sm[:, 8:10]))
                link(dve.memset(gates[:, :, NE:NE + 2], 0.0))
                link(dve.tensor_tensor(gt, gt, each(sm[:, 8:10], [P, S, NE]), ALU.mult))
                dve.wait_ge(pos_mm, l + 1)
                pm = posm[:, :, 0:NE]
                link(dve.memset(posm[:, :, NE:NE + 2], -1.0))
                link(dve.tensor_scalar(pm, ps[:, 1, 64:64 + 2 * NE].rearrange("p (s e) -> p s e", s=S), 1.0, None, ALU.add))
                link(dve.tensor_tensor(pm, pm, sel, ALU.mult))
                link(dve.tensor_scalar(pm, pm, -1.0, None, ALU.add))
                link(dve.tensor_reduce(sm[:, 8:9], ps[:, 1, 128:128 + NE], AX, ALU.max))
                for j in range(3):
                    ins = dve.tensor_scalar(sm[:, 9 + j:10 + j], sm[:, 8:9], float(SLOTS * (j + 1)), None, ALU.is_gt)
                link(ins)
                link(dve.tensor_reduce(sm[:, 12:13], sm[:, 9:12], AX, ALU.add))
                link(dve.tensor_scalar(sm[:, 12:13], sm[:, 12:13], 1.0, None, ALU.add))
                dve.tensor_copy(npass[0:1, l:l + 1], sm[0:1, 12:13]).then_inc(routed, 1)
                if l + 1 < LAYERS:
                    for a in range(1, 4):
                        ada_bias(l + 1, a)
                dve.wait_ge(routed, l + 1)
                passes = dve.snap(dve.value_load(npass[0:1, l:l + 1], min_val=1, max_val=4))
                for s_ in (m_onehot, m_act, m_x):
                    dve.sem_inc(s_[l], 1)

                def onehots(pr, gathered):
                    dve.wait_ge(m_gather[l], gathered * 2 + 1)
                    dve.wait_ge(m_gwt[l], gathered + 1)
                    for s in range(S):
                        for e in range(2):
                            at = posm[:, s, bass.ds(pr * 2 + e, 1)]
                            c = slice(e * SLOTS, (e + 1) * SLOTS)
                            dve.tensor_scalar(gg[:, s, c], C("slot"), at, None, ALU.is_equal)
                            ins = dve.tensor_scalar(gw[:, s, c], C("slot"), at, gates[:, s, bass.ds(pr * 2 + e, 1)],
                                                    ALU.is_equal, ALU.mult)
                    ins.then_inc(m_onehot[l], 1)

                with dve.Fori(0, passes) as pss:
                    onehots(0, pss * PAIRS)
                    with dve.Fori(0, PAIRS) as pr:
                        q = pss * PAIRS + pr
                        for half in range(2):
                            dve.wait_ge(m_sig[l], q * 2 + 2 + half)
                            dve.wait_ge(m_at[l], q * 2 + 1)
                            g_, u_ = ps[:, half, 0:256], ps[:, half, 256:512]
                            e_ = eg[:, half, :]
                            dve.tensor_tensor(e_, e_, g_, ALU.mult).then_inc(m_silu[l], 1)
                            dve.wait_ge(m_silu[l], q * 2 + 1 + half)
                            dve.tensor_tensor(aa[:, half, :], e_, u_, ALU.mult).then_inc(m_act[l], 1)
                        onehots(pr + 1, q + 1)
                        for f in range(4):
                            dve.wait_ge(m_scat[l], q * 4 + f + 2)
                            for j in range(2):
                                for s in range(S):
                                    k, c = 2 * f + j, slice(s * T, (s + 1) * T)
                                    ins = dve.scalar_tensor_tensor(
                                        x[:, k, c], ps[:, 4 + f % 2, j * NT + s * T:j * NT + (s + 1) * T],
                                        mod[:, l, 40 + k, s:s + 1], x[:, k, c], ALU.mult, ALU.add)
                            ins.then_inc(m_x[l], 1)
                    dve.tensor_scalar(posm[:, :, :], posm[:, :, :], -float(SLOTS), None, ALU.add).then_inc(m_shift[l], 1)
                    dve.wait_ge(m_shift[l], pss + 1)
                dve.wait_ge(m_x[l], passes * (4 * PAIRS) + 1)
                dve.memset(sm[:, 0:1], 0.0).then_inc(x_done, 1)

        @block.gpsimd
        def _(pool):
            pool.memset(qe[:, :, :], 0.0).then_inc(zeroed, 1)
            pool.memset(ke[:, :, :], 0.0).then_inc(zeroed, 1)
            pool.wait_ge(zeroed, 2)
            for l in range(LAYERS):
                if l:
                    pool.wait_ge(x_done, l)
                pool.dma_start(lpar[:, :], lparams[l]).then_inc(in_lp, 16)
                pool.wait_ge(k_normed, 2 * l + 1)
                pool.dma_start(new_k[l], tm[:, 0, K0:V0]).then_inc(kv_out, 16)
                pool.dma_start(new_v[l], tm[:, 0, V0:GQ0]).then_inc(kv_out, 16)
                for i in range(8):
                    n = 8 * l + i
                    pool.wait_ge(g_exp, n + 1)
                    pool.wait_ge(g_copied, n + 1)
                    if n:
                        pool.wait_ge(g_ke, n)
                        pool.wait_ge(g_lev, n)
                    e, ks = ereg[:, i % 2, :], qk2[:, i % 2, 1, :]
                    for v in range(LEVELS):
                        ins = side(pool, ke, e, ks, v, 1)
                    if i < GH:
                        ins.then_inc(pool_step, 1)
                        pool.wait_ge(pool_step, 4 * l + i + 1)
                        if i or l:
                            pool.wait_ge(g_kt, 4 * l + i)
                        ins = pool.tensor_tensor(kst[:, :], ks, e[:, LV_COLS:LV_COLS + T], ALU.mult)
                    ins.then_inc(g_ke, 1)
                pool.wait_ge(g_sf_copied, 4 * (l + 1))
                pool.dma_start(new_state[l], sfin[:, :, :]).then_inc(st_out, 16)
            pool.wait_ge(kv_out, 32 * LAYERS)
            pool.wait_ge(st_out, 16 * LAYERS)


def side(eng, out, decay, vals, level, keys):
    half = P >> (level + 1)
    for d in range(2):
        r = slice(d * DK, (d + 1) * DK)
        right = (d + keys + 1) % 2
        def part(ap):
            v = ap.rearrange("p (b c n) -> p b c n", c=2, n=half)
            return v[:, :, right, :]
        ins = eng.tensor_tensor(part(out[r, level, :]), part(vals[r, :]), part(decay[r, level * T:(level + 1) * T]),
                                ALU.mult)
    return ins


def shape_constants():
    c = np.zeros((P, CW), np.float32)

    def put(name, v):
        at, n = CO[name]
        c[:, at:at + n] = v

    u = np.arange(P)[:, None]
    t = np.arange(P)[None, :]
    put("ident", u == t)
    put("ones", 1.0)
    f, b, m = [], [], []
    for v in range(LEVELS):
        half = P >> (v + 1)
        mid = t // (2 * half) * (2 * half) + half
        right = t >= mid
        f.append(np.where(right, (u >= mid) & (u <= t), (u > t) & (u < mid)))
        b.append(np.where(right, (u >= mid) & (u < t), (u >= t) & (u < mid)))
        m.append((u // (2 * half) == t // (2 * half)) & (u // half != t // half))
    put("dec_f", np.concatenate(f + [u > t, u <= t], 1))
    put("dec_b", np.concatenate(b + [u < t, u >= t], 1))
    put("mask", np.concatenate(m + [u == t], 1))
    put("before", u < t)
    put("slot", np.arange(SLOTS)[None])
    inv = (np.float32(ROPE_THETA) ** (-np.arange(0, HD // 2, 2, dtype=np.float32) / np.float32(HD // 2))).astype(np.float32)
    row = (np.arange(T) // int(GRID_W)).astype(np.float32)[:, None] * inv
    col = (np.arange(T) % int(GRID_W)).astype(np.float32)[:, None] * inv
    put("cos", np.concatenate([np.cos(row), np.cos(row), np.cos(col), np.cos(col)], 1))
    put("sin", np.concatenate([-np.sin(row), np.sin(row), -np.sin(col), np.sin(col)], 1))
    put("order_g", np.arange(NG, 0, -1)[None])
    put("order_e", np.arange(NE, 0, -1)[None])
    put("sel", (u % 32) == np.arange(S)[None])
    return c


def kernel(**inputs):
    import concourse.bacc as bacc
    from concourse.bass_utils import run_bass_kernel_spmd

    a = {k: np.asarray(v) for k, v in inputs.items()}
    L = LAYERS

    def chan(v):
        v = v.reshape(v.shape[:-1] + (v.shape[-1] // P, P))
        return np.moveaxis(v, -1, 0)

    xs = np.concatenate([a["x_prompt"][0], a["x_sample"][0]], 0)
    xT = np.ascontiguousarray(xs.T.reshape(KT, P, NT).transpose(1, 0, 2))
    cond = np.stack([a["c_ctx"], a["c"][0]], 0)
    params = np.concatenate([
        chan(cond).transpose(0, 2, 1).reshape(P, -1),
        chan(a["b_ada"]).reshape(P, -1),
        chan(a["norm1"]).reshape(P, -1),
        chan(a["norm2"]).reshape(P, -1),
        np.broadcast_to(a["router_bias"], (P, NE)),
        a["router_w"].reshape(KT, P, NE).transpose(1, 0, 2).reshape(P, -1)], 1)
    lparams = np.zeros((L, P, LW), np.float32)
    for l in range(L):
        def put(name, v, rows=P):
            at, n = LO[name]
            lparams[l, 0:rows, at:at + n] = v
        put("state", a["state_gla"][0, l].transpose(0, 2, 1, 3).reshape(P, GH * DV))
        put("ck", a["cache_k"][0, l].reshape(P, P))
        put("cv", a["cache_v"][0, l].reshape(P, P))
        at, n = LO["w2"]
        lparams[l, 0:RANK, at:at + n // 2] = a["gla_w2"][l, 0]
        lparams[l, RANK:2 * RANK, at + n // 2:at + n] = a["gla_w2"][l, 1]
        lparams[l, 2 * RANK, at:at + n] = a["gla_b"][l].reshape(-1)
        put("qn", a["q_norm"][l][None])
        put("kn", a["k_norm"][l][None])
        put("gln", a["gla_norm"][l][None])
    arrays = {"xT": xT, "consts": shape_constants(), "params": np.ascontiguousarray(params), "lparams": lparams}
    for name in ("w_ada", "w_in", "w_pa", "w_pb", "w_out", "w_gate", "w_up", "w_down"):
        arrays[name] = np.ascontiguousarray(a[name])
    q = a["w_in"][:, :, Q0:K0].reshape(L, D, KVH, G, HD).transpose(0, 1, 3, 2, 4).reshape(L, D, K0)
    arrays["w_in"] = np.concatenate([q, a["w_in"][:, :, K0:]], 2)
    outs = [("yT", (P, KT, NT)), ("new_k", (L, T, P)), ("new_v", (L, T, P)), ("new_state", (L, P, GH, DV))]

    nc = bacc.Bacc("TRN2", target_bir_lowering=False, num_devices=1)
    args = [nc.dram_tensor(n, v.shape, F32, kind="ExternalInput").ap() for n, v in arrays.items()]
    args += [nc.dram_tensor(n, s, F32, kind="ExternalOutput").ap() for n, s in outs]
    build(nc, *args)
    r = run_bass_kernel_spmd(nc, [arrays], core_ids=[0]).results[0]
    y = np.asarray(r["yT"]).transpose(2, 1, 0).reshape(NT, D)
    state = np.asarray(r["new_state"]).reshape(L, 2, DK, GH, DV).transpose(0, 1, 3, 2, 4)
    return (y[None, 0:T], y[None, T:NT], np.asarray(r["new_k"]).reshape(1, L, T, KVH, HD),
            np.asarray(r["new_v"]).reshape(1, L, T, KVH, HD), np.ascontiguousarray(state)[None])
```

```python
from contextlib import ExitStack

import numpy as np

import concourse.bass as bass
from concourse import mybir

F32 = mybir.dt.float32
I32 = mybir.dt.int32
ALU = mybir.AluOpType
ACT = mybir.ActivationFunctionType
AX = mybir.AxisListType.X

P = 128
T = 128
S = 2
NT = S * T
LAYERS = 2
D = 1024
KT = D // P
HD = 64
HEADS = 8
KVH = 2
G = HEADS // KVH
ROPE_THETA = 10000.0
GRID_W = 64
GH = 4
DK = 64
DV = 128
RANK = 16
NE = 16
NG = 4
EPG = NE // NG
FE = 512
FT = FE // P
EPS = 1e-6
NEG = -3.0e38

Q0, K0, V0, GQ0, GK0, GV0, GG0, LR0, GA0, GB0 = 0, 512, 640, 768, 1024, 1280, 1792, 2304, 2336, 3360
IN_W = 4384
EXP_LN = "natural_log_exp_and_others"
RSQ = 5
TMW = LR0
IN_UNITS = [(0, 512), (512, 512), (1024, 512), (1536, 512), (2048, 288)]
GATE_UNITS = [(GA0, 512), (GA0 + 512, 512), (GB0, 512), (GB0 + 512, 512)]

RING = 6
UNIT = 4096
ADA = 12
SLOTS = 64
PAIRS = NE // 2
MORE_PAIR = 4
MORE = (0, 1, 2)
PASS_END = PAIRS + 1

LEVELS = 7
LV_COLS = LEVELS * T
KE_DVE = 3
D_W = LV_COLS + 2 * T

CONSTS = [("ident", P), ("ones", P), ("before", P), ("slot", SLOTS), ("cos", HD), ("sin", HD), ("order_g", NG),
          ("order_e", NE), ("dec_f", D_W), ("dec_b", D_W), ("mask", LV_COLS + T)]
PARAMS = [("cond", KT * S), ("b_ada", LAYERS * 48), ("norm1", LAYERS * KT), ("norm2", LAYERS * KT),
          ("bias_r", NE), ("w_r", KT * 32)]
LPARAMS = [("state", GH * DV), ("ck", P), ("cv", P), ("w2", 2 * GH * DK), ("qn", HD), ("kn", HD), ("gln", DV)]


def offsets(parts):
    at, out = 0, {}
    for name, n in parts:
        out[name] = (at, n)
        at += n
    return out, at


CO, CW = offsets(CONSTS)
C_LATE = CO["dec_f"][0]
PO, PW = offsets(PARAMS)
LO, LW = offsets(LPARAMS)

HOLE = ("none", 0)


def fill_list(l):
    gates = [("gate", c) for c in range(8)]
    ada = [("ada", a) for a in range(ADA)]
    pa = [("pa", m) for m in range(4)]
    if l + 1 < LAYERS:
        heads = [ada[4], pa[0], pa[1], HOLE, ada[5], HOLE, pa[2], HOLE, pa[3], HOLE, ada[6], ada[7], ada[8], ada[9]]
        return gates + [HOLE] + heads + [ada[10], ada[11]]
    heads = [pa[0], HOLE, pa[1], HOLE, pa[2], HOLE, pa[3], HOLE, ada[6], HOLE, ada[7], HOLE, ada[8], HOLE]
    return gates + [HOLE] + heads + [ada[9]]


def early_units(l):
    return [4, 5] if l else []


def window(l):
    return [(l + 1, a) for a in range(4)] if l + 1 < LAYERS else [(l, ADA - 2), (l, ADA - 1)]


def ada_before_experts(l):
    return ADA * (l + 1) if l + 1 < LAYERS else ADA * (l + 1) - 2


EARLY = 1


def dense_order():
    out = [(0, "ada", a) for a in range(4)]
    for l in range(LAYERS):
        out += [(l, "ada", a) for a in early_units(l)]
        out += [(l, "in", n) for n in range(len(IN_UNITS))]
        for kind, n in fill_list(l):
            if kind == "ada" or (kind, n) == ("pa", 0):
                out.append((l, kind, n))
            elif kind == "gate" and n % 2 == 0:
                out.append((l, "gates", n // 2))
        out += [(l, "pb", 0), (l, "out", 0), (l, "out", 1)]
        out += [(ll, "ada", a) for ll, a in window(l)]
    return out


ORDER = dense_order()
PLACE = {key: n for n, key in enumerate(ORDER)}
BEFORE = [PLACE[(w[0], "ada", w[1])] + 1 for w in (window(l)[-1] for l in range(LAYERS))]


def build(nc, xT, consts, params, lparams, w_ada, w_in, w_pa, w_pb, w_out, w_gate, w_up, w_down,
          yT, new_k, new_v, new_state):
    ctx = ExitStack()
    with ctx:
        def sb(name, shape, dt=F32):
            return ctx.enter_context(nc.sbuf_tensor(name, shape, dt))

        def sem(name):
            return ctx.enter_context(nc.semaphore(name))

        ring = sb("ring", [P, RING, UNIT])
        cst = sb("cst", [P, CW])
        par = sb("par", [P, PW])
        mixer = sb("mixer", [P, 2 * S * GH * DK + 2 * LV_COLS + LW])
        x = sb("x", [P, KT, NT])
        more = sb("more", [P, 2, UNIT])
        sgb = sb("sgb", [P, KT, NT])
        tm = sb("tm", [P, S, TMW])
        lrt = sb("lrt", [P, NT])
        qk2 = sb("qk2", [P, 2, 2, T])
        st = sb("st", [P, T])
        qin = sb("qin", [P, T])
        kst = sb("kst", [P, T])
        sfin = sb("sfin", [P, GH, DV])
        adarow = sb("adarow", [P, 512])
        mod = sb("mod", [P, LAYERS, 48, S])
        modA = sb("modA", [P, 2, KT, S])
        cs = sb("cs", [P, KT, 32])
        rs = sb("rs", [P, NT])
        sm = sb("sm", [P, 112])
        npass = sb("npass", [1, LAYERS], I32)
        ps = ctx.enter_context(nc.psum_tensor("ps", [P, 8, 512], F32))

        la_cols = 2 * S * GH * DK
        la = mixer[:, 0:la_cols].rearrange("p (s n) -> p s n", s=S)
        qe, ke = (mixer[:, la_cols + i * LV_COLS:la_cols + (i + 1) * LV_COLS].rearrange("p (v t) -> p v t", t=T)
                  for i in range(2))
        lpar = mixer[:, la_cols + 2 * LV_COLS:]
        ereg = more[:, 0, 0:2048].rearrange("p (a n) -> p a n", a=2)
        ot = more[:, 0, 2048:3072].rearrange("p (k n) -> p k n", k=4)
        ogt = more[:, 0, 3072:4096].rearrange("p (k n) -> p k n", k=4)
        h = more[:, 1, 0:2048].rearrange("p (k n) -> p k n", k=KT)
        sga = more[:, 1, 2048:4096].rearrange("p (k n) -> p k n", k=KT)

        def C(name):
            at, n = CO[name]
            return cst[:, at:at + n]

        def PR(name):
            at, n = PO[name]
            return par[:, at:at + n]

        def LP(name):
            at, n = LO[name]
            return lpar[:, at:at + n]

        ident, ones = C("ident"), C("ones")
        BIG_RMS = (rs[:, :], qk2[:, 0, :, :].rearrange("p a t -> p (a t)"), qk2[:, 1, :, :].rearrange("p a t -> p (a t)"))
        QK_RMS = (sm[:, 32:52], sm[:, 64:84], sm[:, 84:104])
        GLA_RMS = (sm[:, 52:56], sm[:, 104:108], sm[:, 108:112])
        qt = ogt[:, 0:2, :].rearrange("p a (b t) -> p (a b) t", b=2)
        kt_all = ogt[:, 2, :]
        prob = ereg[:, 0, :]
        probt = ereg[:, 1, :]
        tmf = tm[:, :, :].rearrange("p s n -> p (s n)")
        hg = tmf[:, 0:1024].rearrange("p (k n) -> p k n", k=KT)
        yy = tmf[:, 1024:2048]
        eg = tmf[:, 2048:2560].rearrange("p (a n) -> p a n", a=2)
        aa = tmf[:, 2560:3072].rearrange("p (a n) -> p a n", a=2)
        at_ = tmf[:, 3072:3584].rearrange("p (a n) -> p a n", a=FT)
        gwt = tmf[:, 3584:3840]
        gg = tmf[:, 3840:4096].rearrange("p (s n) -> p s n", s=S)
        gw = tmf[:, 4096:4352].rearrange("p (s n) -> p s n", s=S)
        h2tok = sgb[:, :, :].rearrange("p (s a) n -> p s (a n)", s=S)
        rrow = la[:, 0, 0:NT]
        rt = rs[:, 0:6 * S * NE].rearrange("p (a s e) -> p a s e", a=6, s=S)
        posm = st[:, 0:S * (NE + 2)].rearrange("p (s e) -> p s e", s=S)
        gates = st[:, 64:64 + S * (NE + 2)].rearrange("p (s e) -> p s e", s=S)

        in_x, in_c, in_d, in_p, in_lp = sem("in_x"), sem("in_c"), sem("in_d"), sem("in_p"), sem("in_lp")
        dense_full = [sem(f"dense_full{u}") for u in range(RING)]
        m_silu, m_shift = [[sem(f"{n}{l}") for l in range(LAYERS)] for n in ("m_silu", "m_shift")]
        moe_full = [[sem(f"moe_full{l}_{u}") for u in range(RING)] for l in range(LAYERS)]
        more_full = [[sem(f"more_full{l}_{u}") for u in MORE] for l in range(LAYERS)]
        cond_exp, cs_ready, zeroed = sem("cond_exp"), sem("cs_ready"), sem("zeroed")
        ada_rows, ada_copied, ada_cols, ada_mod = sem("ada_rows"), sem("ada_copied"), sem("ada_cols"), sem("ada_mod")
        sq_act, sq_dve, ssum, xr_ready = sem("sq_act"), sem("sq_dve"), sem("ssum"), sem("xr_ready")
        gain_ready = sem("gain_ready")
        var_ready, rsq_ready = sem("var_ready"), sem("rsq_ready")
        h_dve, h_act = sem("h_dve"), sem("h_act")
        proj, proj_copied, proj_lr, lr_copied = sem("proj"), sem("proj_copied"), sem("proj_lr"), sem("lr_copied")
        la_mm, la_min, la_ln, la_ready = sem("la_mm"), sem("la_min"), sem("la_ln"), sem("la_ready")
        gg_exp, gg_ready = sem("gg_exp"), sem("gg_ready")
        k_normed, qk_ready = sem("k_normed"), sem("qk_ready")
        att_t, att_copied = sem("att_t"), sem("att_copied")
        scored, maxed, exped, normed = sem("scored"), sem("maxed"), sem("exped"), sem("normed")
        prob_t, prob_copied, att_o, att_o_copied = sem("prob_t"), sem("prob_copied"), sem("att_o"), sem("att_o_copied")
        gate_mm, gate_exp, gate_sig = sem("gate_mm"), sem("gate_exp"), sem("gate_sig")
        g_t, g_copied, g_dec, g_exp = sem("g_t"), sem("g_copied"), sem("g_dec"), sem("g_exp")
        g_qe, g_ke, g_lev, g_st, g_o, g_o_copied = (sem("g_qe"), sem("g_ke"), sem("g_lev"), sem("g_st"), sem("g_o"),
                                                    sem("g_o_copied"))
        g_kt, g_kt_copied, g_sf_copied = sem("g_kt"), sem("g_kt_copied"), sem("g_sf_copied")
        g_normed, g_nt, g_nt_copied = sem("g_normed"), sem("g_nt"), sem("g_nt_copied")
        pa_mm, pa_used, pb_mm, merged = sem("pa_mm"), sem("pa_used"), sem("pb_mm"), sem("merged")
        out_mm, x_mid, x_done = sem("out_mm"), sem("x_mid"), sem("x_done")
        r_rows, r_copied, r_sum = sem("r_rows"), sem("r_copied"), sem("r_sum")
        r_log, r_exp_in, h2_t, h2_copied = sem("r_log"), sem("r_exp_in"), sem("h2_t"), sem("h2_copied")
        sel_ready, pos_mm, routed = sem("sel_ready"), sem("pos_mm"), sem("routed")

        def per_layer(name):
            return [sem(f"{name}{l}") for l in range(LAYERS)]

        m_onehot, m_gather, m_hg = per_layer("m_onehot"), per_layer("m_gather"), per_layer("m_hg")
        m_gwt, m_gwt_copied, m_sig = per_layer("m_gwt"), per_layer("m_gwt_copied"), per_layer("m_sig")
        m_gu = [[sem(f"m_gu{l}_{half}") for half in range(2)] for l in range(LAYERS)]
        m_dn = [[sem(f"m_dn{l}_{half}") for half in range(2)] for l in range(LAYERS)]
        m_act, m_at, m_at_copied = per_layer("m_act"), per_layer("m_at"), per_layer("m_at_copied")
        m_dy, m_y, m_scat, m_x = per_layer("m_dy"), per_layer("m_y"), per_layer("m_scat"), per_layer("m_x")
        kv_out, st_out, y_out = sem("kv_out"), sem("st_out"), sem("y_out")
        dve_step, act_step, pool_step = sem("dve_step"), sem("act_step"), sem("pool_step")

        def unit_src(key):
            _, kind, n = key
            l = key[0]
            rows = lambda w: w.rearrange("(k p) n -> p k n", p=P)
            if kind == "ada":
                return rows(w_ada[l])[:, :, n * 512:(n + 1) * 512]
            if kind in ("in", "gates"):
                at, w = (IN_UNITS if kind == "in" else GATE_UNITS)[n]
                return rows(w_in[l])[:, :, at:at + w]
            if kind == "out":
                return rows(w_out[l])[:, :, n * 512:(n + 1) * 512]
            return rows({"pa": w_pa, "pb": w_pb}[kind][l])

        def unit(key):
            n = PLACE[key]
            kts = 4 if key[1] in ("pa", "pb") else KT
            w = IN_UNITS[key[2]][1] if key[1] == "in" else UNIT // kts
            return ring[:, n % RING, 0:kts * w].rearrange("p (k n) -> p k n", k=kts), n

        def expert_space(l, u, in_more):
            if in_more and u in MORE:
                return (more[:, 0, :], more[:, 1, :], mixer[:, NT:NT + UNIT])[u]
            return ring[:, (BEFORE[l] + u) % RING, :]

        def gu_unit(l, half, e, in_more):
            return expert_space(l, 2 * half + e, in_more).rearrange("p (j k n) -> p j k n", j=2, k=KT)

        def down_unit(l, half):
            return expert_space(l, 4 + half, False).rearrange("p (e k n) -> p e k n", e=2, k=FT // 2)

        def used(n):
            l, kind, i = ORDER[n]
            return {"ada": (ada_rows, ADA * l + i + 1),
                    "in": (proj, 10 * l + 2 * i + 2),
                    "gates": (gate_mm, 8 * l + 2 * i + 2),
                    "pa": (pa_mm, 4 * l + 4), "pb": (pb_mm, 4 * l + 4), "out": (out_mm, 4 * l + 2 * i + 2)}[kind]

        block = ctx.enter_context(nc.Block())

        @block.sync
        def _(sp):
            sp.dma_start(par[:, :], params).then_inc(in_p, 16)
            sp.dma_start(x[:, :, :], xT).then_inc(in_x, 16)
            sp.dma_start(cst[:, 0:C_LATE], consts[:, 0:C_LATE]).then_inc(in_c, 16)

            def expert_unit(l, pr, u, full, in_more=False):
                for j in range(2):
                    if u < 4:
                        hh, e = u // 2, u % 2
                        src = (w_gate, w_up)[j][l, bass.ds(pr * 2 + e, 1)].rearrange("o (k p) n -> p (o k) n", p=P)
                        src, dst = src[:, :, hh * 256:(hh + 1) * 256], gu_unit(l, hh, e, in_more)[:, j]
                    else:
                        src = w_down[l, bass.ds(pr * 2 + j, 1)].rearrange("o (k p) n -> p (o k) n", p=P)
                        src, dst = src[:, 2 * (u - 4):2 * (u - 4) + 2, :], down_unit(l, u - 4)[:, j]
                    sp.dma_start(dst, src).then_inc(full, 16)

            def pair(l, pr, waits, first=0):
                for u in range(first, RING):
                    sp.wait_ge(*waits[u])
                    expert_unit(l, pr, u, moe_full[l][u])

            def more_unit(l, u):
                expert_unit(l, MORE_PAIR, u, more_full[l][u], True)

            def expert_use(l, q):
                return [(m_gu[l][0], q + 1)] * 2 + [(m_gu[l][1], q + 1)] * 2 + [(m_dn[l][0], q + 1), (m_dn[l][1], q + 1)]

            def pass_end(l, q):
                m = len(MORE)
                pair(l, MORE_PAIR, expert_use(l, q + MORE_PAIR), m)
                pair(l, MORE_PAIR + 1, expert_use(l, q + MORE_PAIR)[:m] + expert_use(l, q + MORE_PAIR + 1)[m:])
                with sp.Fori(MORE_PAIR + 2, PAIRS) as pr:
                    pair(l, pr, expert_use(l, q + pr))

            n = 0
            for l in range(LAYERS):
                while n < BEFORE[l]:
                    dst, _ = unit(ORDER[n])
                    if n >= RING:
                        sp.wait_ge(*used(n - RING))
                    if l and n - BEFORE[l - 1] < RING:
                        sp.wait_ge(*expert_use(l - 1, passes * PAIRS)[n - BEFORE[l - 1]])
                    sp.dma_start(dst, unit_src(ORDER[n])).then_inc(dense_full[n % RING], 16)
                    n += 1
                    if n == RING:
                        sp.dma_start(cst[:, C_LATE:CW], consts[:, C_LATE:CW]).then_inc(in_d, 16)
                sp.wait_ge(merged, 4 * (l + 1))
                more_unit(l, 0)
                more_unit(l, 2)
                pair(l, 0, [used(n - RING + u) for u in range(RING)])
                sp.wait_ge(h2_t, 4 * (l + 1))
                more_unit(l, 1)
                with sp.Fori(1, MORE_PAIR) as pr:
                    pair(l, pr, expert_use(l, pr))
                pass_end(l, 0)
                sp.wait_ge(routed, l + 1)
                passes = sp.snap(sp.value_load(npass[0:1, l:l + 1], min_val=1, max_val=4))
                with sp.If(passes - 1):
                    with sp.Fori(1, passes) as pss:
                        sp.wait_ge(m_gu[l][1], pss * PAIRS)
                        for u in MORE:
                            more_unit(l, u)
                        with sp.Fori(0, MORE_PAIR) as pr:
                            pair(l, pr, expert_use(l, pss * PAIRS + pr))
                        pass_end(l, pss * PAIRS)
            sp.wait_ge(x_done, LAYERS)
            sp.dma_start(yT, x[:, :, :]).then_inc(y_out, 16)
            sp.wait_ge(y_out, 16)

        @block.tensor
        def _(pe):
            def full(*key):
                w, n = unit(key)
                pe.wait_ge(dense_full[n % RING], 16 * (n // RING + 1))
                return w

            def ada_a(l, a):
                w = full(l, "ada", a)
                if l or a:
                    pe.wait_ge(ada_copied, l * ADA + a)
                for k in range(KT):
                    j = 32 * (k % 4)
                    mm = pe.matmul(ps[j:j + 32, 7, :], cs[:, k, :], w[:, k, :], start=k < 4, stop=k >= 4)
                mm.then_inc(ada_rows, 1)

            def ada_b(l, a):
                pe.wait_ge(ada_copied, l * ADA + a + 1)
                if l or a:
                    pe.wait_ge(ada_mod, l * ADA + a)
                for i in range(4):
                    mm = pe.transpose(ps[:, 6, i * P:(i + 1) * P], adarow[:, i * P:(i + 1) * P], ident)
                mm.then_inc(ada_cols, 1)

            def gate_chunk(l, c):
                w = full(l, "gates", c // 2)
                if l or c:
                    pe.wait_ge(gate_exp, l * 8 + c)
                for i in range(2):
                    m = (c % 2) * 2 + i
                    for k in range(KT):
                        mm = pe.matmul(ps[:, 5, i * NT:(i + 1) * NT], w[:, k, m * P:(m + 1) * P], h[:, k, :],
                                       start=k == 0, stop=k == KT - 1)
                mm.then_inc(gate_mm, 1)

            def pa_chunk(l, m):
                w = full(l, "pa", 0)
                if m == 0:
                    pe.wait_ge(gate_exp, 8 * (l + 1))
                else:
                    pe.wait_ge(pa_used, 4 * l + m)
                for i in range(2):
                    for k in range(4):
                        mm = pe.matmul(ps[:, 5, i * NT:(i + 1) * NT], w[:, k, (2 * m + i) * P:(2 * m + i + 1) * P],
                                       ot[:, k, :], start=k == 0, stop=k == 3)
                mm.then_inc(pa_mm, 1)

            fills = []
            late = []

            def flush():
                while late:
                    ada_b(*late.pop())

            def fill(l):
                flush()
                if fills:
                    kind, n = fills.pop(0)
                    if kind == "ada":
                        ada_a(l, n)
                        late.append((l, n))
                    elif kind == "gate":
                        gate_chunk(l, n)
                    elif kind == "pa":
                        pa_chunk(l, n)

            def norm_sum(k0, k1):
                for k in range(k0, k1):
                    mm = pe.matmul(ps[:, 0, 0:NT], ones, h[:, k, :], start=k == 0, stop=k == KT - 1)
                if k1 == KT:
                    mm.then_inc(ssum, 1)

            def norm_sum_mid(l, m):
                pe.wait_ge(sq_act, 6 * l + 3 + m)
                norm_sum(2 * m, 2 * m + 2)

            pe.wait_ge(in_c, 16)
            pe.wait_ge(in_p, 16)
            pe.wait_ge(cs_ready, 1)
            for l in range(LAYERS):
                pe.wait_ge(sq_act, 6 * l + 1)
                norm_sum(0, 4)
                pe.wait_ge(sq_act, 6 * l + 2)
                norm_sum(4, 6)
                pe.wait_ge(sq_dve, l + 1)
                norm_sum(6, KT)
                for a in early_units(l):
                    flush()
                    ada_a(l, a)
                    late.append((l, a))
                if l == 0:
                    for a in range(4):
                        ada_a(l, a)
                        ada_b(l, a)
                if l:
                    pe.wait_ge(x_done, l)
                for n in range(2 * len(IN_UNITS)):
                    w = full(l, "in", n // 2)
                    if n == 8:
                        for k in range(KT):
                            mm = pe.matmul(ps[0:32, 4, 0:NT], w[:, k, 256:288], h[:, k, :], start=k == 0, stop=k == KT - 1)
                        mm.then_inc(proj_lr, 1)
                    if n >= 4:
                        pe.wait_ge(proj_copied, 10 * l + n - 3)
                    cols = min(512, TMW - IN_UNITS[n // 2][0])
                    for i, k in enumerate((0, 4, 1, 5, 2, 6, 3, 7)):
                        if n == 0:
                            pe.wait_ge((h_dve, h_act)[i % 2], 8 * l + i // 2 + 1)
                        mm = pe.matmul(ps[:, n % 4, 0:cols], h[:, k, (n % 2) * T:(n % 2) * T + T], w[:, k, 0:cols],
                                       start=i == 0, stop=i == KT - 1)
                    mm.then_inc(proj, 1)
                    if n == 1:
                        flush()
                pe.wait_ge(lr_copied, l + 1)
                pe.wait_ge(in_lp, 16 * (l + 1))
                pe.wait_ge(ada_mod, ADA * l + 4 + len(early_units(l)))
                for s in range(S):
                    pe.matmul(ps[:, 4 + 2 * s, :], lrt[0:33, s * T:(s + 1) * T], LP("w2")[0:33, :],
                              start=True, stop=True).then_inc(la_mm, 1)
                fills[:] = fill_list(l)
                for _ in range(EARLY):
                    fill(l)
                for s in range(S):
                    if s == 0:
                        pe.wait_ge(qk_ready, l + 1)
                        pe.wait_ge(proj_copied, 10 * (l + 1))
                    else:
                        pe.wait_ge(exped, 4 * l + 2)
                    for g in range(G):
                        mm = pe.transpose(ps[:, 0, g * P:(g + 1) * P], tm[:, s, Q0 + g * P:Q0 + (g + 1) * P], ident)
                    mm = pe.transpose(ps[:, 1, 0:P], tm[:, s, K0:V0], ident)
                    if s:
                        mm = pe.transpose(ps[:, 1, P:2 * P], LP("ck"), ident)
                    mm.then_inc(att_t, 1)
                    fill(l)
                    nb = 1 + s
                    nk = nb * T
                    for v in range(KVH):
                        b = 4 * l + 2 * s + v
                        if v == 0:
                            pe.wait_ge(att_copied, 2 * l + s + 1)
                        else:
                            pe.wait_ge(exped, b)
                        for g in range(G):
                            at = g * nk
                            mm = pe.matmul(ps[:, at // 512, at % 512:at % 512 + nk], qt[v * HD:(v + 1) * HD, g, :],
                                           kt_all[v * HD:(v + 1) * HD, 0:nk], start=True, stop=True)
                        mm.then_inc(scored, 1)
                        fill(l)
                        pe.wait_ge(normed, b + 1)
                        if b:
                            pe.wait_ge(prob_copied, b)
                        for j in range(G * nb):
                            mm = pe.transpose(ps[:, 2 + j // 4, (j % 4) * P:(j % 4 + 1) * P],
                                              prob[:, j * P:(j + 1) * P], ident)
                        mm.then_inc(prob_t, 1)
                        pe.wait_ge(prob_copied, b + 1)
                        if b:
                            pe.wait_ge(att_o_copied, b)
                        if b == 4 * l:
                            pe.wait_ge(la_min, 2 * l + 1)
                        for g in range(G):
                            r = HD * (g % 2)
                            for j in range(nb):
                                val = (LP("cv") if j else tm[:, s, V0:GQ0])[:, v * HD:(v + 1) * HD]
                                mm = pe.matmul(ps[r:r + HD, 4, (g // 2) * T:(g // 2 + 1) * T], val,
                                               probt[:, (g * nb + j) * T:(g * nb + j + 1) * T],
                                               start=j == 0, stop=j == nb - 1)
                        mm.then_inc(att_o, 1)
                pe.wait_ge(att_o_copied, 4 * (l + 1))
                pe.wait_ge(la_ready, 2 * (l + 1))
                pe.wait_ge(in_d, 16)

                def gla_in(i):
                    s, hh = i // GH, i % GH
                    n = 8 * l + i
                    if i:
                        pe.wait_ge(g_o_copied, n - 1)
                        if i <= GH + 1:
                            pe.wait_ge(g_kt_copied, 4 * l + i - 1)
                    for j, at in enumerate((GQ0, GK0)):
                        for d in range(2):
                            mm = pe.matmul(ps[d * DK:(d + 1) * DK, 4, j * T:(j + 1) * T],
                                           tm[:, s, at + hh * DK:at + (hh + 1) * DK], ident, start=True, stop=True)
                    mm.then_inc(g_t, 1)
                    if i:
                        pe.wait_ge(g_exp, n)
                    last = ((512, 512, 0),) if s == 0 else ((512, 384, 0), (LV_COLS + T, T, 384))
                    for half, parts in enumerate((((0, 512, 0),), last)):
                        for at, w, to in parts:
                            for d, dec in enumerate((C("dec_f"), C("dec_b"))):
                                mm = pe.matmul(ps[d * DK:(d + 1) * DK, half, to:to + w],
                                               la[:, s, d * GH * DK + hh * DK:d * GH * DK + (hh + 1) * DK],
                                               dec[:, at:at + w], start=True, stop=True)
                    mm.then_inc(g_dec, 1)

                def gla_levels(i):
                    n = 8 * l + i
                    pe.wait_ge(g_qe, n + 1)
                    pe.wait_ge(g_ke, n + 1)
                    if i:
                        pe.wait_ge(g_st, n)
                    b = i % 2
                    for v in range(LEVELS + 1):
                        lhs, rhs = (ke[:, v, :], qe[:, v, :]) if v < LEVELS else (qk2[:, b, 1, :], qk2[:, b, 0, :])
                        mm = pe.matmul(ps[:, 2 + v // 4, (v % 4) * T:(v % 4 + 1) * T], lhs, rhs, start=True, stop=True)
                        if v % 4 == 3:
                            mm.then_inc(g_lev, 1)

                def gla_keys(i):
                    pe.wait_ge(g_copied, 8 * l + i + 2)
                    pe.transpose(ps[:, 4, 384:512], kst[:, :], ident).then_inc(g_kt, 1)

                def gla_out(i):
                    s, hh = i // GH, i % GH
                    n = 8 * l + i
                    pe.wait_ge(g_st, n + 1)
                    pe.wait_ge(g_copied, 8 * l + min(i + 2, 8))
                    if i:
                        pe.wait_ge(g_o_copied, n)
                    if s == 0:
                        pe.wait_ge(g_kt_copied, 4 * l + i + 1)
                    val = tm[:, s, GV0 + hh * DV:GV0 + (hh + 1) * DV]
                    mm = pe.matmul(ps[:, 4, 256:384], st[:, :], val, start=True, stop=s == 0)
                    if s:
                        mm = pe.matmul(ps[:, 4, 256:384], qin[:, :], LP("state")[:, hh * DV:(hh + 1) * DV],
                                       start=False, stop=True)
                    else:
                        mm = pe.matmul(ps[:, 4, 384:512], lrt[:, 0:T], val, start=True, stop=True)
                    mm.then_inc(g_o, 1)

                gla_in(0)
                for i in range(8):
                    fill(l)
                    gla_levels(i)
                    if i < 7:
                        gla_in(i + 1)
                    if i < GH:
                        gla_keys(i)
                    fill(l)
                    gla_out(i)
                while fills:
                    fill(l)
                pe.wait_ge(pa_used, 4 * (l + 1))
                pe.wait_ge(g_exp, 8 * (l + 1))
                pe.wait_ge(g_o_copied, 8 * (l + 1))
                for s in range(S):
                    pe.wait_ge(g_normed, 2 * l + s + 1)
                    for k in range(4):
                        mm = pe.transpose(ps[:, 4 + s, k * P:(k + 1) * P], tm[:, s, k * P:(k + 1) * P], ident)
                    mm.then_inc(g_nt, 1)
                flush()
                w = full(l, "pb", 0)
                pe.wait_ge(g_nt_copied, 2 * (l + 1))
                for m in range(4):
                    for i in range(2):
                        for k in range(4):
                            mm = pe.matmul(ps[:, m, i * NT:(i + 1) * NT], w[:, k, (2 * m + i) * P:(2 * m + i + 1) * P],
                                           ogt[:, k, :], start=k == 0, stop=k == 3)
                    mm.then_inc(pb_mm, 1)
                pe.wait_ge(merged, 4 * (l + 1))
                pe.wait_ge(ada_mod, ada_before_experts(l))
                for m in range(4):
                    w = full(l, "out", m // 2)
                    for i in range(2):
                        for k in range(KT):
                            c = (m % 2) * 2 + i
                            mm = pe.matmul(ps[:, 4 + m, i * NT:(i + 1) * NT], w[:, k, c * P:(c + 1) * P], sga[:, k, :],
                                           start=k == 0, stop=k == KT - 1)
                    mm.then_inc(out_mm, 1)
                    if m:
                        norm_sum_mid(l, m - 1)
                norm_sum_mid(l, 3)
                win = window(l)
                ada_a(*win[0])
                ada_b(*win[0])
                ada_a(*win[1])
                pe.wait_ge(h_dve, 8 * (l + 1))
                pe.wait_ge(h_act, 8 * (l + 1))
                for k in range(KT):
                    j = 32 * (k % 4)
                    mm = pe.matmul(ps[j:j + 32, 1, 0:NT], PR("w_r")[:, k * 32:(k + 1) * 32], h[:, k, :],
                                   start=k < 4, stop=k >= 4)
                mm.then_inc(r_rows, 1)
                for b in range(4):
                    for j in range(4):
                        s, k = (4 * b + j) // KT, (4 * b + j) % KT
                        mm = pe.transpose(ps[:, 2 + b, j * P:(j + 1) * P], h[:, k, s * T:(s + 1) * T], ident)
                    mm.then_inc(h2_t, 1)
                    if b == 0:
                        pe.wait_ge(r_copied, l + 1)
                        for s in range(S):
                            mm = pe.transpose(ps[:, 1, NT + s * T:NT + (s + 1) * T], rrow[:, s * T:(s + 1) * T], ident)
                        mm.then_inc(r_log, 1)
                ada_b(*win[1])
                for w in win[2:3]:
                    ada_a(*w)
                pe.wait_ge(sel_ready, l + 1)
                sel = rt[:, 0, :, :]
                for s in range(S):
                    if s:
                        pe.matmul(ps[:, 1, 64 + NE:64 + 2 * NE], ones, sel[:, 0, :], start=True, stop=False)
                    pe.matmul(ps[:, 1, 64 + s * NE:64 + (s + 1) * NE], C("before"), sel[:, s, :], start=s == 0, stop=True)
                for s in range(S):
                    mm = pe.matmul(ps[:, 1, 128:128 + NE], ones, sel[:, s, :], start=s == 0, stop=s == 1)
                mm.then_inc(pos_mm, 1)
                if win[2:]:
                    ada_b(*win[2])
                    ada_a(*win[3])
                    ada_b(*win[3])
                pe.wait_ge(h2_copied, 4 * (l + 1))
                pe.wait_ge(routed, l + 1)
                passes = pe.snap(pe.value_load(npass[0:1, l:l + 1], min_val=1, max_val=4))
                for s_ in (m_gather[l], m_gwt[l], *m_gu[l], m_at[l], *m_dn[l], m_scat[l]):
                    pe.sem_inc(s_, 1)
                pe.wait_ge(ada_mod, ada_before_experts(l) + len(win))
                def gather(pss, pr, b):
                    if b == 0:
                        pe.wait_ge(m_onehot[l], pss * PASS_END + pr + 2)
                    for j in range(4):
                        for s in range(S):
                            k = 4 * b + j
                            mm = pe.matmul(ps[:, 4 + b, j * P:(j + 1) * P], h2tok[:, s, k * P:(k + 1) * P], gg[:, s, :],
                                           start=s == 0, stop=s == 1)
                    mm.then_inc(m_gather[l], 1)

                def turn_gates(q):
                    pe.wait_ge(m_gwt_copied[l], q + 1)
                    for s in range(S):
                        mm = pe.transpose(ps[:, 7, s * P:(s + 1) * P], gw[:, s, :], ident)
                    mm.then_inc(m_gwt[l], 1)

                def expert_pair(pss, pr, in_more=False, later=False, last=False):
                    q = pss * PAIRS + pr
                    for half in range(2):
                        pe.wait_ge(m_act[l], q * 2 + 1)
                        for e in range(2):
                            u = 2 * half + e
                            if u not in MORE:
                                pe.wait_ge(moe_full[l][u], q * 32 + 32)
                            elif in_more:
                                pe.wait_ge(more_full[l][u], pss * 32 + 32)
                            else:
                                loads = pr if later else pr + 1
                                pe.wait_ge(moe_full[l][u], pss * (32 * (PAIRS - 1)) + loads * 32)
                        for k in range(KT):
                            if half == 0 and k in (0, 4):
                                pe.wait_ge(m_hg[l], q * 2 + 2 + k // 4)
                            for e in range(2):
                                r = e * SLOTS
                                mm = pe.matmul(ps[r:r + SLOTS, half, :].rearrange("p (j n) -> p j n", j=2), hg[:, k, r:r + SLOTS],
                                               gu_unit(l, half, e, in_more)[:, :, k, :], start=k == 0, stop=k == KT - 1)
                        mm.then_inc(m_gu[l][half], 1)
                    pe.wait_ge(m_x[l], q * 4 + 1)
                    pe.wait_ge(m_y[l], q * 2 + 1)

                    def down(k, n):
                        for e in range(2):
                            r = e * SLOTS
                            mm = pe.matmul(ps[r:r + SLOTS, 2 + n, :], at_[:, k, r:r + SLOTS],
                                           down_unit(l, k // 2)[:, e, k % 2, n * 512:(n + 1) * 512],
                                           start=k == 0, stop=k == FT - 1)
                        return mm

                    for half in range(2):
                        pe.wait_ge(m_act[l], q * 2 + 2 + half)
                        pe.wait_ge(m_at_copied[l], q * 2 + 1 + half)
                        for j in range(2):
                            mm = pe.transpose(ps[:, 6, (2 * half + j) * P:(2 * half + j + 1) * P],
                                              aa[:, half, j * P:(j + 1) * P], ident)
                        mm.then_inc(m_at[l], 1)
                        if not last:
                            gather(pss, pr + 1, half)
                        pe.wait_ge(m_at_copied[l], q * 2 + 2 + half)
                        pe.wait_ge(moe_full[l][4 + half], q * 32 + 32)
                        if half == 0:
                            for k in range(2):
                                for n in range(2):
                                    mm = down(k, n)
                            mm.then_inc(m_dn[l][0], 1)
                        else:
                            for n in range(2):
                                down(2, n)
                                down(3, n).then_inc((m_dy[l], m_dn[l][1])[n], 1)
                    if not last:
                        turn_gates(q + 1)
                        pe.wait_ge(m_hg[l], q * 2 + 5)
                    pe.wait_ge(m_gwt_copied[l], q + 2)
                    for f in range(4):
                        if f % 2 == 0:
                            pe.wait_ge(m_y[l], q * 2 + 2 + f // 2)
                        if f >= 2:
                            pe.wait_ge(m_x[l], q * 4 + f)
                        for j in range(2):
                            k = 2 * f + j
                            mm = pe.matmul(ps[:, 4 + f % 2, j * NT:(j + 1) * NT], yy[:, k * P:(k + 1) * P], gwt,
                                           start=True, stop=True)
                        mm.then_inc(m_scat[l], 1)

                with pe.Fori(0, passes) as pss:
                    pe.wait_ge(m_x[l], pss * (PAIRS * 4) + 1)
                    for b in range(2):
                        gather(pss, 0, b)
                    turn_gates(pss * PAIRS)
                    with pe.Fori(0, MORE_PAIR) as pr:
                        expert_pair(pss, pr)
                    expert_pair(pss, MORE_PAIR, in_more=True)
                    with pe.Fori(MORE_PAIR + 1, PAIRS - 1) as pr:
                        expert_pair(pss, pr, later=True)
                    expert_pair(pss, PAIRS - 1, later=True, last=True)

        @block.scalar
        def _(act):
            steps = [0]

            def link(ins):
                steps[0] += 1
                ins.then_inc(act_step, 1)
                act.wait_ge(act_step, steps[0])

            def copy(out, in_, scale=1.0):
                return act.activation(out, in_, ACT.Copy, scale=scale)

            def inv_root(work, step):
                act.wait_ge(var_ready, step)
                link(act.activation(work[1], work[0], ACT.Ln))
                act.activation(work[1], work[1], ACT.Exp, scale=-0.5).then_inc(rsq_ready, 1)

            def squares(k0, k1):
                act.activation(h[:, k0:k1, :], x[:, k0:k1, :], ACT.Square).then_inc(sq_act, 1)

            def modulate(l, n):
                act.wait_ge(gain_ready, 2 * l + n + 1)
                for k in range(4, KT):
                    if k % 2 == 0:
                        act.wait_ge(xr_ready, 4 * (2 * l + n) + k - 3)
                    for s in range(S):
                        c = slice(s * T, (s + 1) * T)
                        ins = act.activation(h[:, k, c], h[:, k, c], ACT.Identity, bias=mod[:, l, 24 * n + k, s:s + 1],
                                             scale=modA[:, n, k, s:s + 1])
                    ins.then_inc(h_act, 1)

            def ada_copy(l, a):
                act.wait_ge(ada_rows, l * ADA + a + 1)
                if l or a:
                    act.wait_ge(ada_cols, l * ADA + a)
                copy(adarow[:, :], ps[:, 7, :]).then_inc(ada_copied, 1)

            def gate_copy(l, c):
                act.wait_ge(gate_mm, 8 * l + c + 1)
                if c == 0:
                    act.wait_ge(la_ready, 2 * l + 2)
                if c == 4:
                    act.wait_ge(gg_ready, l + 1)
                to = (sga if c < 4 else sgb)[:, 2 * (c % 4):2 * (c % 4) + 2, :]
                copy(to, ps[:, 5, :].rearrange("p (a n) -> p a n", a=2)).then_inc(gate_exp, 1)

            def gate_sigmoids(l):
                act.wait_ge(gate_exp, 8 * (l + 1))
                act.activation(sga[:, :, :], sga[:, :, :], ACT.Sigmoid)
                act.activation(sgb[:, :, :], sgb[:, :, :], ACT.Sigmoid).then_inc(gate_sig, 1)
                act.preload_act_table_set(EXP_LN)

            fills = []

            def fill(l):
                if fills:
                    kind, n = fills.pop(0)
                    if kind == "ada":
                        ada_copy(l, n)
                    elif kind == "gate":
                        gate_copy(l, n)
                    elif kind == "pa" and n == 0:
                        gate_sigmoids(l)

            act.preload_act_table_set(EXP_LN)
            act.wait_ge(in_p, 16)
            act.activation(sm[:, 0:16], PR("cond"), ACT.Exp, scale=-1.0).then_inc(cond_exp, 1)
            act.wait_ge(in_x, 16)
            for l in range(LAYERS):
                if l:
                    act.preload_act_table_set(EXP_LN)
                    act.wait_ge(m_x[l - 1], passes * (4 * PAIRS))
                squares(0, 4)
                squares(4, 6)
                if l:
                    act.wait_ge(x_done, l)
                inv_root(BIG_RMS, RSQ * l + 1)
                for a in early_units(l):
                    ada_copy(l, a)
                if l == 0:
                    for a in range(4):
                        ada_copy(l, a)
                modulate(l, 0)
                for n in range(2 * len(IN_UNITS)):
                    if n == 6:
                        inv_root(QK_RMS, RSQ * l + 2)
                    act.wait_ge(proj, 10 * l + n + 1)
                    at = IN_UNITS[n // 2][0]
                    cols = min(512, TMW - at)
                    copy(tm[:, n % 2, at:at + cols], ps[:, n % 4, 0:cols]).then_inc(proj_copied, 1)
                act.wait_ge(proj_copied, 10 * (l + 1))
                act.activation(sgb[:, 0:4, :].rearrange("p (s a) n -> p s (a n)", s=S), tm[:, :, GG0:LR0],
                               ACT.Sigmoid).then_inc(gg_exp, 1)
                act.preload_act_table_set(EXP_LN)
                for s in range(S):
                    tmp = sga[:, 2 * s:2 * s + 2, :]
                    act.wait_ge(la_min, 2 * l + s + 1)
                    link(act.activation(tmp, tmp, ACT.Exp))
                    act.activation(tmp, tmp, ACT.Ln, bias=1.0).then_inc(la_ln, 1)
                fills[:] = fill_list(l)
                for _ in range(EARLY):
                    fill(l)
                for s in range(S):
                    act.wait_ge(att_t, 2 * l + s + 1)
                    if s:
                        act.wait_ge(scored, 4 * l + 2)
                    copy(ogt[:, 0:2, :], ps[:, 0, :].rearrange("p (a n) -> p a n", a=2))
                    copy(kt_all[:, 0:T * (1 + s)], ps[:, 1, 0:T * (1 + s)]).then_inc(att_copied, 1)
                    fill(l)
                    nb = 1 + s
                    nk = nb * T
                    for v in range(KVH):
                        b = 4 * l + 2 * s + v
                        act.wait_ge(maxed, b + 1)
                        if b:
                            act.wait_ge(prob_t, b)
                        for g in range(G):
                            at = g * nk
                            ins = act.activation(prob[:, at:at + nk], ps[:, at // 512, at % 512:at % 512 + nk], ACT.Exp,
                                                 bias=sm[:, 24 + g:25 + g], scale=HD ** -0.5,
                                                 accum_out=sm[:, 28 + g:29 + g])
                        ins.then_inc(exped, 1)
                        fill(l)
                        act.wait_ge(prob_t, b + 1)
                        if b:
                            act.wait_ge(att_o, b)
                        copy(probt[:, 0:G * nk].rearrange("p (b n) -> p b n", b=nb),
                             ps[:, 2:2 + nb, :]).then_inc(prob_copied, 1)
                        act.wait_ge(att_o, b + 1)
                        copy(ot[:, 2 * v:2 * v + 2, s * T:(s + 1) * T],
                             ps[:, 4, 0:2 * T].rearrange("p (a n) -> p a n", a=2)).then_inc(att_o_copied, 1)

                def gla_in(i):
                    n = 8 * l + i
                    act.wait_ge(g_t, n + 1)
                    if i >= 2:
                        act.wait_ge(g_lev, 2 * (n - 1))
                    copy(qk2[:, i % 2, 0, :], ps[:, 4, 0:T], scale=DK ** -0.5)
                    copy(qk2[:, i % 2, 1, :], ps[:, 4, T:2 * T]).then_inc(g_copied, 1)
                    act.wait_ge(g_dec, n + 1)
                    if i >= 2:
                        act.wait_ge(g_qe, n - 1)
                        act.wait_ge(g_ke, n - 1)
                    act.activation(ereg[:, i % 2, :].rearrange("p (a n) -> p a n", a=2), ps[:, 0:2, :], ACT.Exp,
                                   scale=1.0 / 16.0).then_inc(g_exp, 1)

                def gla_kt(i):
                    if i < GH:
                        m = 4 * l + i
                        act.wait_ge(g_kt, m + 1)
                        if i:
                            act.wait_ge(g_o, 8 * l + i)
                        copy(lrt[:, 0:T], ps[:, 4, 384:512]).then_inc(g_kt_copied, 1)

                def gla_out(i):
                    s, hh = i // GH, i % GH
                    n = 8 * l + i
                    act.wait_ge(g_o, n + 1)
                    if s == 0:
                        if l and i == 0:
                            act.wait_ge(st_out, 16 * l)
                        copy(sfin[:, hh, :], ps[:, 4, 384:512]).then_inc(g_sf_copied, 1)
                    copy(tm[:, s, hh * DV:(hh + 1) * DV], ps[:, 4, 256:384]).then_inc(g_o_copied, 1)

                act.wait_ge(prob_t, 4 * (l + 1))
                act.wait_ge(att_o, 4 * (l + 1))
                gla_in(0)
                for i in range(8):
                    fill(l)
                    if i < 7:
                        gla_in(i + 1)
                    gla_kt(i)
                    fill(l)
                    gla_out(i)
                    if i == GH:
                        inv_root(GLA_RMS, RSQ * l + 3)
                fill(l)
                inv_root(GLA_RMS, RSQ * l + 4)
                while fills:
                    fill(l)
                for s in range(S):
                    act.wait_ge(g_nt, 2 * l + s + 1)
                    copy(ogt[:, :, s * T:(s + 1) * T],
                         ps[:, 4 + s, :].rearrange("p (a n) -> p a n", a=4)).then_inc(g_nt_copied, 1)
                for m in range(4):
                    act.wait_ge(x_mid, 4 * l + m + 1)
                    squares(2 * m, 2 * m + 2)
                inv_root(BIG_RMS, RSQ * l + 5)
                for w in window(l)[:2]:
                    ada_copy(*w)
                modulate(l, 1)
                act.wait_ge(r_rows, l + 1)
                copy(rrow, ps[:, 1, 0:NT]).then_inc(r_copied, 1)
                act.wait_ge(r_sum, l + 1)
                act.activation(rt[:, 1, :, :], rt[:, 1, :, :], ACT.Exp, scale=-1.0).then_inc(r_exp_in, 1)
                for b in range(4):
                    act.wait_ge(h2_t, 4 * l + b + 1)
                    copy(sgb[:, 2 * b:2 * b + 2, :], ps[:, 2 + b, :].rearrange("p (a n) -> p a n", a=2)).then_inc(h2_copied, 1)
                for w in window(l)[2:]:
                    ada_copy(*w)
                act.wait_ge(kv_out, 32 * (l + 1))
                act.wait_ge(routed, l + 1)
                passes = act.snap(act.value_load(npass[0:1, l:l + 1], min_val=1, max_val=4))
                for s_ in (m_hg, m_gwt_copied, m_sig, m_at_copied, m_y):
                    act.sem_inc(s_[l], 1)
                act.preload_act_table(ACT.Sigmoid)
                def gathered(q, b):
                    act.wait_ge(m_gather[l], q * 2 + 2 + b)
                    if b == 0:
                        act.wait_ge(m_gu[l][1], q + 1)
                    copy(hg[:, 4 * b:4 * b + 4, :], ps[:, 4 + b, :].rearrange("p (a n) -> p a n", a=4)).then_inc(m_hg[l], 1)

                def turned_gates(q):
                    act.wait_ge(m_gwt[l], q + 2)
                    act.wait_ge(m_scat[l], q * 4 + 1)
                    copy(gwt, ps[:, 7, 0:NT]).then_inc(m_gwt_copied[l], 1)

                def expert_pair(q, last):
                    for half in range(2):
                        act.wait_ge(m_gu[l][half], q + 2)
                        act.wait_ge(m_act[l], q * 2 + 1)
                        act.activation(eg[:, half, :], ps[:, half, 0:256], ACT.Sigmoid).then_inc(m_sig[l], 1)
                    for half in range(2):
                        act.wait_ge(m_at[l], q * 2 + 2 + half)
                        act.wait_ge(m_dn[l][half], q + 1)
                        copy(at_[:, 2 * half:2 * half + 2, :],
                             ps[:, 6, half * 256:(half + 1) * 256].rearrange("p (a n) -> p a n", a=2)
                             ).then_inc(m_at_copied[l], 1)
                        if not last:
                            gathered(q + 1, half)
                    for n in range(2):
                        act.wait_ge(*((m_dy[l], q + 1), (m_dn[l][1], q + 2))[n])
                        copy(yy[:, n * 512:(n + 1) * 512], ps[:, 2 + n, :]).then_inc(m_y[l], 1)
                    if not last:
                        turned_gates(q + 1)

                with act.Fori(0, passes) as pss:
                    for b in range(2):
                        gathered(pss * PAIRS, b)
                    turned_gates(pss * PAIRS)
                    with act.Fori(0, PAIRS - 1) as pr:
                        expert_pair(pss * PAIRS + pr, False)
                    expert_pair(pss * PAIRS + (PAIRS - 1), True)

        @block.vector
        def _(dve):
            steps = [0]

            def link(ins):
                steps[0] += 1
                ins.then_inc(dve_step, 1)
                dve.wait_ge(dve_step, steps[0])

            def rows(ap, shape):
                return ap.unsqueeze(1).to_broadcast(shape)

            def each(ap, shape):
                return ap.unsqueeze(len(shape) - 1).to_broadcast(shape)

            def inv_rms(work, n, src, step):
                v, y, t = work
                dve.tensor_scalar(v, src, 1.0 / n, EPS, ALU.mult, ALU.add).then_inc(var_ready, 1)
                dve.wait_ge(rsq_ready, step)
                link(dve.tensor_tensor(t, y, y, ALU.mult))
                link(dve.scalar_tensor_tensor(t, t, -0.5, v, ALU.mult, ALU.mult))
                link(dve.scalar_tensor_tensor(v, t, 1.5, y, ALU.add, ALU.mult))

            def one_over_one_plus(ap):
                link(dve.tensor_scalar(ap, ap, 1.0, None, ALU.add))
                link(dve.reciprocal(ap, ap))

            def squares():
                dve.tensor_tensor(h[:, 6:KT, :], x[:, 6:KT, :], x[:, 6:KT, :], ALU.mult).then_inc(sq_dve, 1)

            def gains(l, n):
                dve.wait_ge(ada_mod, l * ADA + (4 if n == 0 else 10))
                norm = PR("norm1" if n == 0 else "norm2")[:, l * KT:(l + 1) * KT]
                c = mod[:, l, 24 * n + 8:24 * n + 16, :]
                link(dve.tensor_scalar(modA[:, n, :, :], c, 1.0, None, ALU.add))
                dve.tensor_tensor(modA[:, n, :, :], modA[:, n, :, :], each(norm, [P, KT, S]),
                                  ALU.mult).then_inc(gain_ready, 1)
                dve.wait_ge(gain_ready, 2 * l + n + 1)

            def norm_sum(l, n):
                if l or n:
                    gains(l, n)
                dve.wait_ge(ssum, 2 * l + n + 1)
                inv_rms(BIG_RMS, D, ps[:, 0, 0:NT], RSQ * l + (1 if n == 0 else 5))
                for k in (4, 0, 6, 2):
                    dve.tensor_tensor(h[:, k:k + 2, :], x[:, k:k + 2, :], rows(rs[:, :], [P, 2, NT]),
                                      ALU.mult).then_inc(xr_ready, 1)

            def norm_mod(l, n):
                if not (l or n):
                    gains(l, n)
                dve.wait_ge(xr_ready, 4 * (2 * l + n + 1))
                for k in range(4):
                    for s in range(S):
                        c = slice(s * T, (s + 1) * T)
                        ins = dve.tensor_scalar(h[:, k, c], h[:, k, c], modA[:, n, k, s:s + 1],
                                                mod[:, l, 24 * n + k, s:s + 1], ALU.mult, ALU.add)
                    ins.then_inc(h_dve, 1)

            def ada_bias(l, a):
                dve.wait_ge(ada_cols, l * ADA + a + 1)
                b = PR("b_ada")[:, l * 48 + 4 * a:l * 48 + 4 * a + 4]
                m = mod[:, l, 4 * a:4 * a + 4, :]
                parts = ps[:, 6, :].rearrange("p (a q n) -> p a n q", a=4, q=4)[:, :, 0:S, :]
                link(dve.tensor_reduce(m, parts, AX, ALU.add))
                dve.tensor_tensor(m, m, each(b, [P, 4, S]), ALU.add).then_inc(ada_mod, 1)

            def merge_a(l, m):
                dve.wait_ge(gate_sig, l + 1)
                dve.wait_ge(pa_mm, 4 * l + m + 1)
                a = sga[:, 2 * m:2 * m + 2, :]
                dve.tensor_tensor(a, a, ps[:, 5, :].rearrange("p (a n) -> p a n", a=2), ALU.mult).then_inc(pa_used, 1)

            fills, late = [], []

            def fill(l):
                while late:
                    ada_bias(*late.pop())
                if fills:
                    kind, n = fills.pop(0)
                    if kind == "ada":
                        late.append((l, n))
                    elif kind == "pa":
                        merge_a(l, n)

            link(dve.memset(cs[:, :, :], 0.0))
            dve.wait_ge(in_p, 16)
            dve.wait_ge(cond_exp, 1)
            one_over_one_plus(sm[:, 0:16])
            dve.tensor_tensor(cs[:, :, 0:S], PR("cond").rearrange("p (k s) -> p k s", s=S),
                              sm[:, 0:16].rearrange("p (k s) -> p k s", s=S), ALU.mult).then_inc(cs_ready, 1)
            dve.wait_ge(in_x, 16)
            dve.wait_ge(in_c, 16)
            for l in range(LAYERS):
                squares()
                norm_sum(l, 0)
                if l == 0:
                    for a in range(4):
                        ada_bias(l, a)
                for a in early_units(l)[:1]:
                    ada_bias(l, a)
                norm_mod(l, 0)
                for a in early_units(l)[1:]:
                    ada_bias(l, a)
                dve.wait_ge(proj_copied, 10 * l + 4)
                dve.wait_ge(in_lp, 16 * (l + 1))
                qk = tm[:, :, 0:V0]
                tmp = ereg[:, :, :].rearrange("p a n -> p (a n)")[:, 0:S * V0].rearrange("p (s n) -> p s n", s=S)
                link(dve.tensor_tensor(tmp, qk, qk, ALU.mult))
                rq = sm[:, 32:52].rearrange("p (s n) -> p s n", s=S)
                link(dve.tensor_reduce(rq, tmp.rearrange("p s (h d) -> p s h d", d=HD), AX, ALU.add))
                inv_rms(QK_RMS, HD, sm[:, 32:52], RSQ * l + 2)
                for s in range(S):
                    v = tm[:, s, 0:V0].rearrange("p (h d) -> p h d", d=HD)
                    link(dve.tensor_tensor(v, v, each(rq[:, s, :], [P, 10, HD]), ALU.mult))
                    dve.tensor_tensor(v[:, 0:HEADS, :], v[:, 0:HEADS, :], rows(LP("qn"), [P, HEADS, HD]), ALU.mult)
                    dve.tensor_tensor(v[:, HEADS:10, :], v[:, HEADS:10, :], rows(LP("kn"), [P, KVH, HD]),
                                      ALU.mult).then_inc(k_normed, 1)
                    dve.wait_ge(k_normed, 2 * l + s + 1)
                v = tm[:, 1, 0:V0].rearrange("p (h d) -> p h d", d=HD)
                v5 = tm[:, 1, 0:V0].rearrange("p (h r c d) -> p h r c d", r=2, c=2, d=16)
                sn = C("sin").rearrange("p (r c d) -> p r c d", r=2, c=2)
                t1 = ereg[:, 0, 0:V0].rearrange("p (h d) -> p h d", d=HD)
                t2 = ereg[:, 1, 0:V0].rearrange("p (h r c d) -> p h r c d", r=2, c=2, d=16)
                dve.tensor_tensor(t1, v, rows(C("cos"), [P, 10, HD]), ALU.mult)
                for c in range(2):
                    ins = dve.tensor_tensor(t2[:, :, :, c, :], v5[:, :, :, 1 - c, :],
                                            sn[:, :, c, :].unsqueeze(1).to_broadcast([P, 10, 2, 16]), ALU.mult)
                link(ins)
                dve.tensor_tensor(tm[:, 1, 0:V0], ereg[:, 0, 0:V0], ereg[:, 1, 0:V0], ALU.add).then_inc(qk_ready, 1)
                dve.wait_ge(proj_lr, l + 1)
                link(dve.memset(lrt[32:33, :], 1.0))
                dve.tensor_copy(lrt[0:32, :], ps[0:32, 4, 0:NT]).then_inc(lr_copied, 1)
                for s in range(S):
                    dve.wait_ge(la_mm, 2 * l + s + 1)
                    link(dve.tensor_scalar(la[:, s, :], ps[:, 4 + 2 * s, :], 0.0, None, ALU.min))
                    dve.scalar_tensor_tensor(sga[:, 2 * s:2 * s + 2, :].rearrange("p a n -> p (a n)"), la[:, s, :], 2.0,
                                             ps[:, 4 + 2 * s, :], ALU.mult, ALU.subtract).then_inc(la_min, 1)
                for s in range(S):
                    dve.wait_ge(la_ln, 2 * l + s + 1)
                    dve.tensor_tensor(la[:, s, :].rearrange("p (a n) -> p a n", a=2),
                                      la[:, s, :].rearrange("p (a n) -> p a n", a=2), sga[:, 2 * s:2 * s + 2, :],
                                      ALU.subtract).then_inc(la_ready, 1)
                dve.wait_ge(gg_exp, l + 1)
                ge = sgb[:, 0:4, :].rearrange("p (s a) n -> p s (a n)", s=S)
                dve.tensor_tensor(tm[:, :, GG0:LR0], tm[:, :, GG0:LR0], ge, ALU.mult).then_inc(gg_ready, 1)
                fills[:] = fill_list(l)
                for _ in range(EARLY):
                    fill(l)
                for s in range(S):
                    fill(l)
                    nb = 1 + s
                    nk = nb * T
                    for v in range(KVH):
                        b = 4 * l + 2 * s + v
                        dve.wait_ge(scored, b + 1)
                        if nb == 1:
                            sc = ps[:, 0, :].rearrange("p (g n) -> p g n", g=G)
                        else:
                            sc = ps[:, 0:2, :].rearrange("p a (g n) -> p (a g) n", g=2)
                        link(dve.tensor_reduce(sm[:, 20:24], sc, AX, ALU.max))
                        dve.tensor_scalar(sm[:, 24:28], sm[:, 20:24], -HD ** -0.5, None, ALU.mult).then_inc(maxed, 1)
                        fill(l)
                        dve.wait_ge(exped, b + 1)
                        link(dve.reciprocal(sm[:, 28:32], sm[:, 28:32]))
                        pv = prob[:, 0:G * nk].rearrange("p (g n) -> p g n", g=G)
                        dve.tensor_tensor(pv, pv, each(sm[:, 28:32], [P, G, nk]), ALU.mult).then_inc(normed, 1)

                def gla_q(i):
                    n = 8 * l + i
                    dve.wait_ge(g_exp, n + 1)
                    dve.wait_ge(g_copied, n + 1)
                    if n:
                        dve.wait_ge(g_lev, 2 * n)
                    if i == 0:
                        dve.wait_ge(zeroed, 2 * (l + 1))
                    e, qs = ereg[:, i % 2, :], qk2[:, i % 2, 0, :]
                    for v in range(KE_DVE):
                        side(dve, ke, e, qk2[:, i % 2, 1, :], v, 1)
                    for v in range(LEVELS):
                        ins = side(dve, qe, e, qs, v, 0)
                    if i >= GH:
                        if i > GH:
                            dve.wait_ge(g_o, n)
                        ins = dve.tensor_tensor(qin[:, :], qs, e[:, LV_COLS:LV_COLS + T], ALU.mult)
                    ins.then_inc(g_qe, 1)

                def gla_mask(i):
                    n = 8 * l + i
                    if i:
                        dve.wait_ge(g_o, n)
                    if n == 0:
                        dve.wait_ge(in_d, 16)
                    m = C("mask").rearrange("p (a n) -> p a n", a=2)
                    for a in range(2):
                        dve.wait_ge(g_lev, 2 * n + a + 1)
                        ins = dve.tensor_tensor(ps[:, 2 + a, :], ps[:, 2 + a, :], m[:, a, :], ALU.mult)
                    link(ins)
                    dve.tensor_reduce(st[:, :], ps[:, 2:4, :].rearrange("p a (v t) -> p t (a v)", v=4), AX,
                                      ALU.add).then_inc(g_st, 1)

                def gla_norm(s):
                    dve.wait_ge(g_o_copied, 8 * l + 4 * s + 4)
                    o, t = tm[:, s, 0:512], tm[:, s, GQ0:GV0]
                    o3 = o.rearrange("p (h d) -> p h d", d=DV)
                    link(dve.tensor_tensor(t, o, o, ALU.mult))
                    link(dve.tensor_reduce(sm[:, 52:56], t.rearrange("p (h d) -> p h d", d=DV), AX, ALU.add))
                    inv_rms(GLA_RMS, DV, sm[:, 52:56], RSQ * l + 3 + s)
                    link(dve.tensor_tensor(o3, o3, each(sm[:, 52:56], [P, GH, DV]), ALU.mult))
                    link(dve.tensor_tensor(o3, o3, rows(LP("gln"), [P, GH, DV]), ALU.mult))
                    dve.tensor_tensor(o, o, tm[:, s, GG0:LR0], ALU.mult).then_inc(g_normed, 1)

                gla_q(0)
                for i in range(8):
                    fill(l)
                    gla_mask(i)
                    if i < 7:
                        gla_q(i + 1)
                    fill(l)
                    if i == GH:
                        gla_norm(0)
                fill(l)
                gla_norm(1)
                while fills or late:
                    fill(l)
                for m in range(4):
                    dve.wait_ge(pb_mm, 4 * l + m + 1)
                    a, b = sga[:, 2 * m:2 * m + 2, :], sgb[:, 2 * m:2 * m + 2, :]
                    if m == 0:
                        dve.wait_ge(pa_used, 4 * (l + 1))
                    link(dve.tensor_tensor(b, b, ps[:, m, :].rearrange("p (a n) -> p a n", a=2), ALU.mult))
                    dve.tensor_tensor(a, a, b, ALU.add).then_inc(merged, 1)
                dve.wait_ge(ada_mod, ada_before_experts(l))
                for m in range(4):
                    dve.wait_ge(out_mm, 4 * l + m + 1)
                    for i in range(2):
                        for s in range(S):
                            k, c = 2 * m + i, slice(s * T, (s + 1) * T)
                            ins = dve.scalar_tensor_tensor(x[:, k, c], ps[:, 4 + m, i * NT + s * T:i * NT + (s + 1) * T],
                                                           mod[:, l, 16 + k, s:s + 1], x[:, k, c], ALU.mult, ALU.add)
                    ins.then_inc(x_mid, 1)
                norm_sum(l, 1)
                ada_bias(*window(l)[0])
                norm_mod(l, 1)
                dve.wait_ge(r_log, l + 1)
                dve.tensor_reduce(rt[:, 1, :, :], ps[:, 1, NT:2 * NT].rearrange("p (s q n) -> p s n q", s=S, q=4)[:, :, 0:NE, :],
                                  AX, ALU.add).then_inc(r_sum, 1)
                dve.wait_ge(r_exp_in, l + 1)
                sel, score, biased, t3, t4 = (rt[:, i, :, :] for i in (0, 1, 2, 3, 4))
                one_over_one_plus(score)
                link(dve.tensor_tensor(biased, score, rows(PR("bias_r"), [P, S, NE]), ALU.add))
                bg = rt[:, 2, :, :].rearrange("p s (g e) -> p (s g) e", g=NG)
                pairs = rs[:, 96:144].rearrange("p (g n) -> p g n", n=6)
                dve.tensor_tensor(pairs[:, :, 0:3], bg[:, :, 0:3], bg[:, :, 1:4], ALU.add)
                dve.tensor_tensor(pairs[:, :, 3:5], bg[:, :, 0:2], bg[:, :, 2:4], ALU.add)
                link(dve.tensor_tensor(pairs[:, :, 5:6], bg[:, :, 0:1], bg[:, :, 3:4], ALU.add))
                gs = sm[:, 0:8].rearrange("p (s g) -> p s g", s=S)
                link(dve.tensor_reduce(sm[:, 0:8], pairs, AX, ALU.max))

                def first_max(vals, flags, n, order):
                    link(dve.tensor_reduce(sm[:, 8:10], vals, AX, ALU.max))
                    link(dve.tensor_tensor(flags, vals, each(sm[:, 8:10], [P, S, n]), ALU.is_equal))
                    link(dve.tensor_tensor(flags, flags, rows(order, [P, S, n]), ALU.mult))
                    link(dve.tensor_reduce(sm[:, 8:10], flags, AX, ALU.max))
                    link(dve.tensor_tensor(flags, flags, each(sm[:, 8:10], [P, S, n]), ALU.is_equal))

                gf = sm[:, 10:18].rearrange("p (s g) -> p s g", s=S)
                first_max(gs, gf, NG, C("order_g"))
                link(dve.tensor_tensor(bg, bg, each(sm[:, 10:18], [P, S * NG, EPG]), ALU.mult))
                link(dve.tensor_scalar(sm[:, 10:18], sm[:, 10:18], -1.0, -NEG, ALU.add, ALU.mult))
                link(dve.tensor_tensor(bg, bg, each(sm[:, 10:18], [P, S * NG, EPG]), ALU.add))
                first_max(biased, t3, NE, C("order_e"))
                link(dve.tensor_scalar(t4, t3, NEG, None, ALU.mult))
                link(dve.tensor_tensor(biased, biased, t4, ALU.add))
                first_max(biased, t4, NE, C("order_e"))
                dve.tensor_tensor(sel, t3, t4, ALU.add).then_inc(sel_ready, 1)
                ada_bias(*window(l)[1])
                dve.wait_ge(sel_ready, l + 1)
                dve.wait_ge(pos_mm, l + 1)
                pm = posm[:, :, 0:NE]
                link(dve.memset(posm[:, :, NE:NE + 2], -1.0))
                link(dve.tensor_scalar(pm, ps[:, 1, 64:64 + 2 * NE].rearrange("p (s e) -> p s e", s=S), 1.0, None, ALU.add))
                link(dve.tensor_tensor(pm, pm, sel, ALU.mult))
                link(dve.tensor_scalar(pm, pm, -1.0, None, ALU.add))
                link(dve.tensor_reduce(sm[:, 8:9], ps[:, 1, 128:128 + NE], AX, ALU.max))
                for j in range(3):
                    ins = dve.tensor_scalar(sm[:, 9 + j:10 + j], sm[:, 8:9], float(SLOTS * (j + 1)), None, ALU.is_gt)
                link(ins)
                link(dve.tensor_reduce(sm[:, 12:13], sm[:, 9:12], AX, ALU.add))
                link(dve.tensor_scalar(sm[:, 12:13], sm[:, 12:13], 1.0, None, ALU.add))
                dve.tensor_copy(npass[0:1, l:l + 1], sm[0:1, 12:13]).then_inc(routed, 1)
                gt = gates[:, :, 0:NE]
                link(dve.tensor_tensor(gt, score, sel, ALU.mult))
                link(dve.tensor_reduce(sm[:, 8:10], gt, AX, ALU.add))
                link(dve.reciprocal(sm[:, 8:10], sm[:, 8:10]))
                link(dve.memset(gates[:, :, NE:NE + 2], 0.0))
                link(dve.tensor_tensor(gt, gt, each(sm[:, 8:10], [P, S, NE]), ALU.mult))
                for w in window(l)[2:]:
                    ada_bias(*w)
                dve.wait_ge(ada_mod, ada_before_experts(l) + len(window(l)))
                dve.wait_ge(routed, l + 1)
                passes = dve.snap(dve.value_load(npass[0:1, l:l + 1], min_val=1, max_val=4))
                for s_ in (m_onehot, m_act, m_x):
                    dve.sem_inc(s_[l], 1)

                def onehots(pr, gathered):
                    dve.wait_ge(m_gather[l], gathered * 2 + 1)
                    dve.wait_ge(m_gwt[l], gathered + 1)
                    for s in range(S):
                        for e in range(2):
                            at = posm[:, s, bass.ds(pr * 2 + e, 1)]
                            c = slice(e * SLOTS, (e + 1) * SLOTS)
                            dve.tensor_scalar(gg[:, s, c], C("slot"), at, None, ALU.is_equal)
                            ins = dve.tensor_scalar(gw[:, s, c], C("slot"), at, gates[:, s, bass.ds(pr * 2 + e, 1)],
                                                    ALU.is_equal, ALU.mult)
                    ins.then_inc(m_onehot[l], 1)

                with dve.Fori(0, passes) as pss:
                    onehots(0, pss * PAIRS)
                    with dve.Fori(0, PAIRS) as pr:
                        q = pss * PAIRS + pr
                        onehots(pr + 1, q + 1)
                        for half in range(2):
                            dve.wait_ge(m_sig[l], q * 2 + 2 + half)
                            dve.wait_ge(m_at[l], q * 2 + 1)
                            g_, u_ = ps[:, half, 0:256], ps[:, half, 256:512]
                            e_ = eg[:, half, :]
                            dve.tensor_tensor(e_, e_, g_, ALU.mult).then_inc(m_silu[l], 1)
                            dve.wait_ge(m_silu[l], q * 2 + 1 + half)
                            dve.tensor_tensor(aa[:, half, :], e_, u_, ALU.mult).then_inc(m_act[l], 1)
                        for f in range(4):
                            dve.wait_ge(m_scat[l], q * 4 + f + 2)
                            for j in range(2):
                                for s in range(S):
                                    k, c = 2 * f + j, slice(s * T, (s + 1) * T)
                                    ins = dve.scalar_tensor_tensor(
                                        x[:, k, c], ps[:, 4 + f % 2, j * NT + s * T:j * NT + (s + 1) * T],
                                        mod[:, l, 40 + k, s:s + 1], x[:, k, c], ALU.mult, ALU.add)
                            ins.then_inc(m_x[l], 1)
                    dve.tensor_scalar(posm[:, :, :], posm[:, :, :], -float(SLOTS), None, ALU.add).then_inc(m_shift[l], 1)
                    dve.wait_ge(m_shift[l], pss + 1)
                dve.wait_ge(m_x[l], passes * (4 * PAIRS) + 1)
                dve.memset(sm[:, 0:1], 0.0).then_inc(x_done, 1)

        @block.gpsimd
        def _(pool):
            for l in range(LAYERS):
                if l:
                    pool.wait_ge(x_done, l)
                pool.memset(qe, 0.0).then_inc(zeroed, 1)
                pool.memset(ke, 0.0).then_inc(zeroed, 1)
                pool.wait_ge(zeroed, 2 * (l + 1))
                pool.dma_start(lpar, lparams[l]).then_inc(in_lp, 16)
                pool.wait_ge(k_normed, 2 * l + 1)
                pool.dma_start(new_k[l], tm[:, 0, K0:V0]).then_inc(kv_out, 16)
                pool.dma_start(new_v[l], tm[:, 0, V0:GQ0]).then_inc(kv_out, 16)
                for i in range(8):
                    n = 8 * l + i
                    pool.wait_ge(g_exp, n + 1)
                    pool.wait_ge(g_copied, n + 1)
                    if n:
                        pool.wait_ge(g_ke, n)
                        pool.wait_ge(g_lev, 2 * n)
                    e, ks = ereg[:, i % 2, :], qk2[:, i % 2, 1, :]
                    for v in range(KE_DVE, LEVELS):
                        ins = side(pool, ke, e, ks, v, 1)
                    if i < GH:
                        ins.then_inc(pool_step, 1)
                        pool.wait_ge(pool_step, 4 * l + i + 1)
                        if i or l:
                            pool.wait_ge(g_kt, 4 * l + i)
                        ins = pool.tensor_tensor(kst[:, :], ks, e[:, LV_COLS:LV_COLS + T], ALU.mult)
                    ins.then_inc(g_ke, 1)
                pool.wait_ge(g_sf_copied, 4 * (l + 1))
                pool.dma_start(new_state[l], sfin[:, :, :]).then_inc(st_out, 16)
            pool.wait_ge(kv_out, 32 * LAYERS)
            pool.wait_ge(st_out, 16 * LAYERS)


def side(eng, out, decay, vals, level, keys):
    half = P >> (level + 1)
    for d in range(2):
        r = slice(d * DK, (d + 1) * DK)
        right = (d + keys + 1) % 2
        def part(ap):
            v = ap.rearrange("p (b c n) -> p b c n", c=2, n=half)
            return v[:, :, right, :]
        ins = eng.tensor_tensor(part(out[r, level, :]), part(vals[r, :]), part(decay[r, level * T:(level + 1) * T]),
                                ALU.mult)
    return ins


def shape_constants():
    c = np.zeros((P, CW), np.float32)

    def put(name, v):
        at, n = CO[name]
        c[:, at:at + n] = v

    u = np.arange(P)[:, None]
    t = np.arange(P)[None, :]
    put("ident", u == t)
    put("ones", 1.0)
    f, b, m = [], [], []
    for v in range(LEVELS):
        half = P >> (v + 1)
        mid = t // (2 * half) * (2 * half) + half
        right = t >= mid
        f.append(np.where(right, (u >= mid) & (u <= t), (u > t) & (u < mid)))
        b.append(np.where(right, (u >= mid) & (u < t), (u >= t) & (u < mid)))
        m.append((u // (2 * half) == t // (2 * half)) & (u // half != t // half))
    put("dec_f", np.concatenate(f + [u > t, u <= t], 1))
    put("dec_b", np.concatenate(b + [u < t, u >= t], 1))
    put("mask", np.concatenate(m + [u == t], 1))
    put("before", u < t)
    put("slot", np.arange(SLOTS)[None])
    inv = (np.float32(ROPE_THETA) ** (-np.arange(0, HD // 2, 2, dtype=np.float32) / np.float32(HD // 2))).astype(np.float32)
    row = (np.arange(T) // int(GRID_W)).astype(np.float32)[:, None] * inv
    col = (np.arange(T) % int(GRID_W)).astype(np.float32)[:, None] * inv
    put("cos", np.concatenate([np.cos(row), np.cos(row), np.cos(col), np.cos(col)], 1))
    put("sin", np.concatenate([-np.sin(row), np.sin(row), -np.sin(col), np.sin(col)], 1))
    put("order_g", np.arange(NG, 0, -1)[None])
    put("order_e", np.arange(NE, 0, -1)[None])
    return c


def kernel(**inputs):
    import concourse.bacc as bacc
    from concourse.bass_utils import run_bass_kernel_spmd

    a = {k: np.asarray(v) for k, v in inputs.items()}
    L = LAYERS

    def chan(v):
        v = v.reshape(v.shape[:-1] + (v.shape[-1] // P, P))
        return np.moveaxis(v, -1, 0)

    xs = np.concatenate([a["x_prompt"][0], a["x_sample"][0]], 0)
    xT = np.ascontiguousarray(xs.T.reshape(KT, P, NT).transpose(1, 0, 2))
    cond = np.stack([a["c_ctx"], a["c"][0]], 0)
    params = np.concatenate([
        chan(cond).transpose(0, 2, 1).reshape(P, -1),
        chan(a["b_ada"]).reshape(P, -1),
        chan(a["norm1"]).reshape(P, -1),
        chan(a["norm2"]).reshape(P, -1),
        np.broadcast_to(a["router_bias"], (P, NE)),
        np.pad(a["router_w"].reshape(KT, P, NE).transpose(1, 0, 2), ((0, 0), (0, 0), (0, 32 - NE))).reshape(P, -1)], 1)
    lparams = np.zeros((L, P, LW), np.float32)
    for l in range(L):
        def put(name, v, rows=P):
            at, n = LO[name]
            lparams[l, 0:rows, at:at + n] = v
        put("state", a["state_gla"][0, l].transpose(0, 2, 1, 3).reshape(P, GH * DV))
        put("ck", a["cache_k"][0, l].reshape(P, P))
        put("cv", a["cache_v"][0, l].reshape(P, P))
        at, n = LO["w2"]
        lparams[l, 0:RANK, at:at + n // 2] = a["gla_w2"][l, 0]
        lparams[l, RANK:2 * RANK, at + n // 2:at + n] = a["gla_w2"][l, 1]
        lparams[l, 2 * RANK, at:at + n] = a["gla_b"][l].reshape(-1)
        put("qn", a["q_norm"][l][None])
        put("kn", a["k_norm"][l][None])
        put("gln", a["gla_norm"][l][None])
    arrays = {"xT": xT, "consts": shape_constants(), "params": np.ascontiguousarray(params), "lparams": lparams}
    for name in ("w_ada", "w_in", "w_pa", "w_pb", "w_out", "w_gate", "w_up", "w_down"):
        arrays[name] = np.ascontiguousarray(a[name])
    q = a["w_in"][:, :, Q0:K0].reshape(L, D, KVH, G, HD).transpose(0, 1, 3, 2, 4).reshape(L, D, K0)
    arrays["w_in"] = np.concatenate([q, a["w_in"][:, :, K0:]], 2)
    outs = [("yT", (P, KT, NT)), ("new_k", (L, T, P)), ("new_v", (L, T, P)), ("new_state", (L, P, GH, DV))]

    nc = bacc.Bacc("TRN2", target_bir_lowering=False, num_devices=1)
    args = [nc.dram_tensor(n, v.shape, F32, kind="ExternalInput").ap() for n, v in arrays.items()]
    args += [nc.dram_tensor(n, s, F32, kind="ExternalOutput").ap() for n, s in outs]
    build(nc, *args)
    r = run_bass_kernel_spmd(nc, [arrays], core_ids=[0]).results[0]
    y = np.asarray(r["yT"]).transpose(2, 1, 0).reshape(NT, D)
    state = np.asarray(r["new_state"]).reshape(L, 2, DK, GH, DV).transpose(0, 1, 3, 2, 4)
    return (y[None, 0:T], y[None, T:NT], np.asarray(r["new_k"]).reshape(1, L, T, KVH, HD),
            np.asarray(r["new_v"]).reshape(1, L, T, KVH, HD), np.ascontiguousarray(state)[None])
```
